# Optimizing a Trainium2 kernel written in Bass

```python
import jax, jax.numpy as jnp
from jax import lax
import numpy as np
import math

D_MODEL = 1024
BATCH = 1
SEQ = 256
DEPTH = 4

N_MIXERS = 3
N_RET_LAYERS = (DEPTH + 2) // 3
N_CONV_LAYERS = (DEPTH + 1) // 3
N_ATTN_LAYERS = DEPTH // 3

RET_QK_DIM = 256
RET_HEADS = D_MODEL // RET_QK_DIM
RET_V_DIM = 2 * RET_QK_DIM
RET_CHUNK = 128
RET_ROPE_BASE = 10000.0
RET_QK_WIDTH = RET_HEADS * RET_QK_DIM
RET_V_WIDTH = RET_HEADS * RET_V_DIM
RET_IN_WIDTH = 2 * RET_QK_WIDTH + 2 * RET_V_WIDTH

CONV_WIDTH = 31
CONV_PAD = (CONV_WIDTH - 1) // 2

ATTN_HEAD_DIM = 64
ATTN_HEADS = D_MODEL // ATTN_HEAD_DIM
DILATION_GROUPS = ((128, 1), (512, 4), (2048, 16))
N_ATTN_GROUPS = len(DILATION_GROUPS)
ATTN_IN_WIDTH = N_ATTN_GROUPS * 3 * ATTN_HEADS * ATTN_HEAD_DIM
ROPE_THETA = 500000.0
ROT_DIM = ATTN_HEAD_DIM // 4

FFN_HIDDEN = -(-8 * D_MODEL // (3 * 256)) * 256

RMS_EPS = 1e-6
LN_EPS = 1e-5
MASK_VALUE = -1e30


def _rmsnorm(x, g):
    xf = x.astype(jnp.float32)
    y = xf * lax.rsqrt(jnp.mean(xf * xf, axis=-1, keepdims=True) + RMS_EPS)
    return (y * g.astype(jnp.float32)).astype(x.dtype)

def _layernorm(x, g, b):
    xf = x.astype(jnp.float32)
    mu = jnp.mean(xf, axis=-1, keepdims=True)
    var = jnp.mean(jnp.square(xf - mu), axis=-1, keepdims=True)
    y = (xf - mu) * lax.rsqrt(var + LN_EPS)
    return (y * g.astype(jnp.float32) + b.astype(jnp.float32)).astype(x.dtype)

def _rotate(x, cos, sin):
    half = x.shape[-1] // 2
    x1, x2 = x[..., :half], x[..., half:]
    return jnp.concatenate([x1 * cos - x2 * sin, x2 * cos + x1 * sin], axis=-1).astype(x.dtype)

def _retention_dir(q, k, v, log1m_gamma, strict):
    B, H, S, dk = q.shape
    dv = v.shape[-1]
    C = RET_CHUNK
    n = S // C
    dt = v.dtype
    gamma = 1.0 - jnp.exp(log1m_gamma.astype(jnp.float32))
    lg = jnp.log(gamma)
    idx = jnp.arange(C)
    diff = idx[:, None] - idx[None, :]
    live = (diff > 0) if strict else (diff >= 0)
    dmat = jnp.where(live, jnp.exp(lg[:, None, None] * jnp.where(live, diff, 0)), 0.0)
    xi = jnp.exp(lg[:, None] * (idx + 1)[None, :]).astype(dt)
    zeta = jnp.exp(lg[:, None] * (C - 1 - idx)[None, :]).astype(dt)
    chunk_decay = jnp.exp(lg * C).astype(dt)

    qc = q.reshape(B, H, n, C, dk)
    kc = k.reshape(B, H, n, C, dk)
    vc = v.reshape(B, H, n, C, dv)
    scores = jnp.einsum('bhnid,bhnjd->bhnij', qc, kc) * dmat[None, :, None].astype(dt)
    intra = jnp.einsum('bhnij,bhnje->bhnie', scores, vc)

    def step(state, inp):
        qb, kb, vb = inp
        cross = jnp.einsum('bhcd,bhde->bhce', qb * xi[None, :, :, None], state)
        state = state * chunk_decay[None, :, None, None] + jnp.einsum(
            'bhcd,bhce->bhde', kb * zeta[None, :, :, None], vb)
        return state, cross

    state0 = jnp.zeros((B, H, dk, dv), dt)
    _, cross = lax.scan(step, state0, (jnp.moveaxis(qc, 2, 0), jnp.moveaxis(kc, 2, 0), jnp.moveaxis(vc, 2, 0)))
    out = intra + jnp.moveaxis(cross, 0, 2)
    return out.reshape(B, H, S, dv)

def _retention_mixer(h, w_in, log1m_decay, w_out):
    B, S, _ = h.shape
    proj = h @ w_in
    q = proj[..., :RET_QK_WIDTH]
    k = proj[..., RET_QK_WIDTH:2 * RET_QK_WIDTH]
    v = proj[..., 2 * RET_QK_WIDTH:2 * RET_QK_WIDTH + RET_V_WIDTH]
    g = proj[..., 2 * RET_QK_WIDTH + RET_V_WIDTH:]
    q = q.reshape(B, S, RET_HEADS, RET_QK_DIM).transpose(0, 2, 1, 3)
    k = k.reshape(B, S, RET_HEADS, RET_QK_DIM).transpose(0, 2, 1, 3)
    v = v.reshape(B, S, RET_HEADS, RET_V_DIM).transpose(0, 2, 1, 3)
    inv = 1.0 / (RET_ROPE_BASE ** jnp.linspace(0.0, 1.0, RET_QK_DIM // 2, dtype=jnp.float32))
    ang = jnp.arange(S, dtype=jnp.float32)[:, None] * inv[None, :]
    cos, sin = jnp.cos(ang), jnp.sin(ang)
    q = _rotate(q, cos, sin)
    k = (_rotate(k, cos, sin) * (RET_QK_DIM ** -0.5)).astype(h.dtype)
    fwd = _retention_dir(q, k, v, log1m_decay[0], strict=False)
    bwd = _retention_dir(q[:, :, ::-1], k[:, :, ::-1], v[:, :, ::-1], log1m_decay[1], strict=True)[:, :, ::-1]
    o = (fwd + bwd).astype(jnp.float32)
    o = o * lax.rsqrt(jnp.mean(o * o, axis=-1, keepdims=True) + RMS_EPS)
    o = o.transpose(0, 2, 1, 3).reshape(B, S, RET_V_WIDTH).astype(h.dtype)
    return (jax.nn.silu(g) * o) @ w_out

def _conv_mixer(h, w_in, b_in, w_dw, b_dw, ln_g, ln_b, w_out, b_out):
    a = h @ w_in + b_in
    u = a[..., :D_MODEL] * jax.nn.sigmoid(a[..., D_MODEL:])
    u = lax.conv_general_dilated(
        u, w_dw[:, None, :].astype(u.dtype), window_strides=(1,), padding=[(CONV_PAD, CONV_PAD)],
        dimension_numbers=('NWC', 'WIO', 'NWC'), feature_group_count=D_MODEL) + b_dw
    u = jax.nn.silu(_layernorm(u, ln_g, ln_b))
    return u @ w_out + b_out

def _dilated_band_attention(q, k, v, dil, radius):
    B, S, H, Dh = q.shape
    L = S // dil
    W = radius
    nb = -(-L // W)
    Lp = nb * W

    def strided(t):
        return t.reshape(B, L, dil, H, Dh).transpose(0, 2, 3, 1, 4)

    qs, ks, vs = strided(q), strided(k), strided(v)
    qs = jnp.pad(qs, ((0, 0), (0, 0), (0, 0), (0, Lp - L), (0, 0)))
    kvpad = ((0, 0), (0, 0), (0, 0), (W, Lp - L + W), (0, 0))
    kb = jnp.pad(ks, kvpad).reshape(B, dil, H, nb + 2, W, Dh)
    vb = jnp.pad(vs, kvpad).reshape(B, dil, H, nb + 2, W, Dh)
    qb = qs.reshape(B, dil, H, nb, W, Dh)
    kwin = jnp.concatenate([kb[:, :, :, 0:nb], kb[:, :, :, 1:nb + 1], kb[:, :, :, 2:nb + 2]], axis=4)
    vwin = jnp.concatenate([vb[:, :, :, 0:nb], vb[:, :, :, 1:nb + 1], vb[:, :, :, 2:nb + 2]], axis=4)
    blk = jnp.arange(nb)[:, None]
    qpos = blk * W + jnp.arange(W)[None, :]
    kpos = (blk - 1) * W + jnp.arange(3 * W)[None, :]
    mask = ((jnp.abs(qpos[:, :, None] - kpos[:, None, :]) <= radius)
            & (kpos[:, None, :] >= 0) & (kpos[:, None, :] < L))
    s = jnp.einsum('bghnqd,bghnkd->bghnqk', qb, kwin).astype(jnp.float32) * (Dh ** -0.5)
    s = jnp.where(mask, s, MASK_VALUE)
    mx = jnp.max(s, axis=-1, keepdims=True)
    p = jnp.exp(s - mx)
    den = jnp.sum(p, axis=-1)
    o = jnp.einsum('bghnqk,bghnkd->bghnqd', p.astype(v.dtype), vwin).astype(jnp.float32) / den[..., None]
    lse = mx[..., 0] + jnp.log(den)
    o = o.reshape(B, dil, H, Lp, Dh)[:, :, :, :L].transpose(0, 3, 1, 2, 4).reshape(B, S, H, Dh)
    lse = lse.reshape(B, dil, H, Lp)[:, :, :, :L].transpose(0, 3, 1, 2).reshape(B, S, H)
    return o, lse

def _dilated_attention_mixer(h, w_in, w_out):
    B, S, _ = h.shape
    proj = (h @ w_in).reshape(B, S, N_ATTN_GROUPS, 3, ATTN_HEADS, ATTN_HEAD_DIM)
    inv = ROPE_THETA ** (-jnp.arange(0, ROT_DIM, 2, dtype=jnp.float32) / ROT_DIM)
    ang = jnp.arange(S, dtype=jnp.float32)[:, None] * inv[None, :]
    cos, sin = jnp.cos(ang)[:, None, :], jnp.sin(ang)[:, None, :]

    def prope(t):
        return jnp.concatenate([_rotate(t[..., :ROT_DIM], cos, sin), t[..., ROT_DIM:]], axis=-1)

    outs, lses = [], []
    for g, (window, dil) in enumerate(DILATION_GROUPS):
        q = prope(proj[:, :, g, 0])
        k = prope(proj[:, :, g, 1])
        v = proj[:, :, g, 2]
        o, l = _dilated_band_attention(q, k, v, dil, window // (2 * dil))
        outs.append(o)
        lses.append(l)
    wts = jax.nn.softmax(jnp.stack(lses, 0), axis=0)
    o = jnp.sum(wts[..., None] * jnp.stack(outs, 0), axis=0).astype(h.dtype)
    return o.reshape(B, S, ATTN_HEADS * ATTN_HEAD_DIM) @ w_out

def _swiglu(h, w_in, w_out):
    a = h @ w_in
    return (jax.nn.silu(a[..., :FFN_HIDDEN]) * a[..., FFN_HIDDEN:]) @ w_out

def first_inputs(seed: int = 0) -> dict:
    key = jax.random.key(seed)
    ks = jax.random.split(key, 20)
    f32 = jnp.float32
    nrm = lambda k, shape, scale: jax.random.normal(k, shape, f32) * scale
    base_decay = -(5.0 + jnp.arange(RET_HEADS, dtype=f32)) * np.float32(np.log(2.0))
    return {
        "x": nrm(ks[0], (BATCH, SEQ, D_MODEL), 1.0),
        "norm_w": 1.0 + nrm(ks[1], (DEPTH, 4, D_MODEL), 0.05),
        "ffn_w_in": nrm(ks[2], (DEPTH, D_MODEL, 2 * FFN_HIDDEN), D_MODEL ** -0.5),
        "ffn_w_out": nrm(ks[3], (DEPTH, FFN_HIDDEN, D_MODEL), FFN_HIDDEN ** -0.5),
        "ret_w_in": nrm(ks[4], (N_RET_LAYERS, D_MODEL, RET_IN_WIDTH), D_MODEL ** -0.5),
        "ret_log1m_decay": base_decay[None, None, :] + nrm(ks[5], (N_RET_LAYERS, 2, RET_HEADS), 0.1),
        "ret_w_out": nrm(ks[6], (N_RET_LAYERS, RET_V_WIDTH, D_MODEL), RET_V_WIDTH ** -0.5),
        "conv_w_in": nrm(ks[7], (N_CONV_LAYERS, D_MODEL, 2 * D_MODEL), D_MODEL ** -0.5),
        "conv_b_in": nrm(ks[8], (N_CONV_LAYERS, 2 * D_MODEL), 0.02),
        "conv_w_dw": nrm(ks[9], (N_CONV_LAYERS, CONV_WIDTH, D_MODEL), CONV_WIDTH ** -0.5),
        "conv_b_dw": nrm(ks[10], (N_CONV_LAYERS, D_MODEL), 0.02),
        "conv_ln_g": 1.0 + nrm(ks[11], (N_CONV_LAYERS, D_MODEL), 0.05),
        "conv_ln_b": nrm(ks[12], (N_CONV_LAYERS, D_MODEL), 0.02),
        "conv_w_out": nrm(ks[13], (N_CONV_LAYERS, D_MODEL, D_MODEL), D_MODEL ** -0.5),
        "conv_b_out": nrm(ks[14], (N_CONV_LAYERS, D_MODEL), 0.02),
        "attn_w_in": nrm(ks[15], (N_ATTN_LAYERS, D_MODEL, ATTN_IN_WIDTH), D_MODEL ** -0.5),
        "attn_w_out": nrm(ks[16], (N_ATTN_LAYERS, ATTN_HEADS * ATTN_HEAD_DIM, D_MODEL),
                          (ATTN_HEADS * ATTN_HEAD_DIM) ** -0.5),
    }

def first_block(x, norm_w, ffn_w_in, ffn_w_out, ret_w_in, ret_log1m_decay, ret_w_out,
              conv_w_in, conv_b_in, conv_w_dw, conv_b_dw, conv_ln_g, conv_ln_b,
              conv_w_out, conv_b_out, attn_w_in, attn_w_out):
    for i in range(DEPTH):
        kind, j = i % N_MIXERS, i // N_MIXERS
        hn = _rmsnorm(x, norm_w[i, 0])
        if kind == 0:
            m = _retention_mixer(hn, ret_w_in[j], ret_log1m_decay[j], ret_w_out[j])
        elif kind == 1:
            m = _conv_mixer(hn, conv_w_in[j], conv_b_in[j], conv_w_dw[j], conv_b_dw[j],
                            conv_ln_g[j], conv_ln_b[j], conv_w_out[j], conv_b_out[j])
        else:
            m = _dilated_attention_mixer(hn, attn_w_in[j], attn_w_out[j])
        x = x + _rmsnorm(m, norm_w[i, 1])
        f = _swiglu(_rmsnorm(x, norm_w[i, 2]), ffn_w_in[i], ffn_w_out[i])
        x = x + _rmsnorm(f, norm_w[i, 3])
    return x


DEPTH_2 = 2

N_META = 16
EPS = 1e-6
A_HEADS = 4
A_WIDTH = D_MODEL
A_HEAD_DIM = A_WIDTH // A_HEADS
A_CHUNK = 64
B_WIDTH = D_MODEL
B_BLOCKS = 8
B_BLOCK_DIM = B_WIDTH // B_BLOCKS
B_CONV = 4
LRU_C = 8.0
C_HEADS = D_MODEL // 128
C_QK_DIM = D_MODEL // (2 * C_HEADS)
C_V_DIM = 2 * C_QK_DIM
ROT_DIM_2 = C_QK_DIM // 4
Q_BLOCK = 128
D_FF = 4 * D_MODEL
N_AB = (DEPTH_2 + 1) // 2
N_C = DEPTH_2 // 2
AB_SPLITS = [A_WIDTH, A_WIDTH, A_WIDTH, A_WIDTH, A_HEADS, A_HEADS, B_WIDTH, B_WIDTH]
AB_IN = sum(AB_SPLITS)
C_SPLITS = [C_HEADS * 2 * C_QK_DIM, C_HEADS * 2 * C_QK_DIM, C_HEADS * C_V_DIM]
C_IN = sum(C_SPLITS)


def _rmsnorm_2(x, g):
    xf = x.astype(jnp.float32)
    y = xf * lax.rsqrt(jnp.mean(xf * xf, axis=-1, keepdims=True) + EPS)
    return (y * g.astype(jnp.float32)).astype(x.dtype)

def _split(a, sizes):
    return jnp.split(a, np.cumsum(sizes)[:-1].tolist(), axis=-1)

def _mlstm_chunk(state, inp):
    c_mem, n_mem, m_prev = state
    q, k, v, log_i, log_f = inp
    L = q.shape[2]
    b = jnp.cumsum(log_f, axis=-1)
    causal = jnp.tril(jnp.ones((L, L), dtype=bool))
    log_d = b[..., :, None] - b[..., None, :] + log_i[..., None, :]
    log_d = jnp.where(causal, log_d, -jnp.inf)
    log_prev = b + m_prev[..., None]
    m_t = jnp.maximum(log_prev, jnp.max(log_d, axis=-1))
    d = jnp.exp(log_d - m_t[..., None])
    w_prev = jnp.exp(log_prev - m_t)
    s = jnp.einsum('bhtd,bhsd->bhts', q, k) * d
    num = (w_prev[..., None] * jnp.einsum('bhvk,bhtk->bhtv', c_mem, q)
           + jnp.einsum('bhts,bhsv->bhtv', s, v))
    den = w_prev * jnp.einsum('bhk,bhtk->bht', n_mem, q) + jnp.sum(s, axis=-1)
    h = num / jnp.maximum(jnp.abs(den), jnp.exp(-m_t))[..., None]
    log_end = b[..., -1:] - b + log_i
    m_new = jnp.maximum(b[..., -1] + m_prev, jnp.max(log_end, axis=-1))
    w_s = jnp.exp(log_end - m_new[..., None])
    decay = jnp.exp(b[..., -1] + m_prev - m_new)
    c_new = decay[..., None, None] * c_mem + jnp.einsum('bhs,bhsv,bhsk->bhvk', w_s, v, k)
    n_new = decay[..., None] * n_mem + jnp.einsum('bhs,bhsk->bhk', w_s, k)
    return (c_new, n_new, m_new), h

def _mlstm(q, k, v, i_pre, f_pre):
    bsz, t_all, nh, dh = q.shape
    seq = t_all - N_META
    nc = seq // A_CHUNK
    q = q.transpose(0, 2, 1, 3)
    k = k.transpose(0, 2, 1, 3) * (dh ** -0.5)
    v = v.transpose(0, 2, 1, 3)
    log_i = i_pre.transpose(0, 2, 1)
    log_f = jax.nn.log_sigmoid(f_pre).transpose(0, 2, 1)
    state = (jnp.zeros((bsz, nh, dh, dh), jnp.float32),
             jnp.zeros((bsz, nh, dh), jnp.float32),
             jnp.zeros((bsz, nh), jnp.float32))
    state, h_meta = _mlstm_chunk(
        state, (q[:, :, :N_META], k[:, :, :N_META], v[:, :, :N_META],
                log_i[:, :, :N_META], log_f[:, :, :N_META]))

    def chunks(a):
        a = a[:, :, N_META:]
        return jnp.moveaxis(a.reshape(bsz, nh, nc, A_CHUNK, *a.shape[3:]), 2, 0)

    _, h_rest = lax.scan(_mlstm_chunk, state,
                         (chunks(q), chunks(k), chunks(v), chunks(log_i), chunks(log_f)))
    h_rest = jnp.moveaxis(h_rest, 0, 2).reshape(bsz, nh, seq, dh)
    h = jnp.concatenate([h_meta, h_rest], axis=2)
    return h.transpose(0, 2, 1, 3)

def _rg_lru_branch(xb, gate, conv_w, conv_b, w_r, b_r, w_i, b_i, lam):
    bsz, t_all, w = xb.shape
    xc = lax.conv_general_dilated(
        xb.astype(jnp.float32), conv_w.astype(jnp.float32)[:, None, :],
        window_strides=(1,), padding=[(B_CONV - 1, 0)],
        dimension_numbers=('NWC', 'WIO', 'NWC'), feature_group_count=w)
    xc = xc + conv_b.astype(jnp.float32)
    xg = xc.reshape(bsz, t_all, B_BLOCKS, B_BLOCK_DIM)
    r = jax.nn.sigmoid(jnp.einsum('btnd,nde->btne', xg, w_r.astype(jnp.float32)).reshape(bsz, t_all, w)
                       + b_r.astype(jnp.float32))
    i = jax.nn.sigmoid(jnp.einsum('btnd,nde->btne', xg, w_i.astype(jnp.float32)).reshape(bsz, t_all, w)
                       + b_i.astype(jnp.float32))
    log_a = -LRU_C * r * jax.nn.softplus(-lam.astype(jnp.float32))
    a = jnp.exp(log_a)
    u = jnp.sqrt(-jnp.expm1(2.0 * log_a)) * (i * xc)

    def combine(left, right):
        a1, b1 = left
        a2, b2 = right
        return a1 * a2, a2 * b1 + b2

    _, h = lax.associative_scan(combine, (a, u), axis=1)
    return h * jax.nn.gelu(gate.astype(jnp.float32))

def _ab_mixer(hn, w_in, if_bias, mlstm_norm, conv_w, conv_b, w_r, b_r, w_i, b_i, lam, w_out):
    bsz, t_all, _ = hn.shape
    proj = hn @ w_in
    q, k, v, o, gi, gf, xb, gate = _split(proj, AB_SPLITS)
    f32 = jnp.float32
    hs = (bsz, t_all, A_HEADS, A_HEAD_DIM)
    ifb = if_bias.astype(f32)
    h_a = _mlstm(q.astype(f32).reshape(hs), k.astype(f32).reshape(hs), v.astype(f32).reshape(hs),
                 gi.astype(f32) + ifb[:A_HEADS], gf.astype(f32) + ifb[A_HEADS:])
    h_a = jax.nn.sigmoid(o.astype(f32)).reshape(hs) * h_a
    h_a = h_a * lax.rsqrt(jnp.mean(h_a * h_a, axis=-1, keepdims=True) + EPS)
    h_a = (h_a * mlstm_norm.astype(f32).reshape(A_HEADS, A_HEAD_DIM)).reshape(bsz, t_all, A_WIDTH)
    h_b = _rg_lru_branch(xb, gate, conv_w, conv_b, w_r, b_r, w_i, b_i, lam)
    y = jnp.concatenate([h_a, h_b], axis=-1).astype(hn.dtype)
    return y @ w_out

def _partial_rope(x, cos, sin):
    half = ROT_DIM_2 // 2
    x1, x2, rest = x[..., :half], x[..., half:ROT_DIM_2], x[..., ROT_DIM_2:]
    c = cos[:, None, None, :]
    s = sin[:, None, None, :]
    return jnp.concatenate([x1 * c - x2 * s, x2 * c + x1 * s, rest], axis=-1)

def _diff_attend(qb, q_pos, kh, vh, k_pos, lam):
    s = jnp.einsum('bhcqd,bhckd->bhcqk', qb, kh)
    mask = k_pos[None, :] <= q_pos[:, None]
    p = jax.nn.softmax(jnp.where(mask, s, -jnp.inf), axis=-1)
    pd = p[:, :, 0] - lam * p[:, :, 1]
    return jnp.einsum('bhqk,bhkv->bhqv', pd, vh)

def _diff_attn(hn, w_in, lam_vecs, subln, w_out, lambda_init):
    bsz, t_all, _ = hn.shape
    seq = t_all - N_META
    f32 = jnp.float32
    q, k, v = _split(hn @ w_in, C_SPLITS)
    q = q.astype(f32).reshape(bsz, t_all, C_HEADS, 2, C_QK_DIM)
    k = k.astype(f32).reshape(bsz, t_all, C_HEADS, 2, C_QK_DIM)
    v = v.astype(f32).reshape(bsz, t_all, C_HEADS, C_V_DIM)
    pos = jnp.arange(t_all, dtype=jnp.int32)
    inv_freq = jnp.power(jnp.float32(ROPE_THETA), -jnp.arange(0, ROT_DIM_2, 2, dtype=f32) / ROT_DIM_2)
    ang = pos.astype(f32)[:, None] * inv_freq[None, :]
    cos, sin = jnp.cos(ang), jnp.sin(ang)
    q = _partial_rope(q, cos, sin) * (C_QK_DIM ** -0.5)
    k = _partial_rope(k, cos, sin)
    lv = lam_vecs.astype(f32)
    lam = jnp.exp(jnp.sum(lv[0] * lv[1])) - jnp.exp(jnp.sum(lv[2] * lv[3])) + lambda_init
    qh = q.transpose(0, 2, 3, 1, 4)
    kh = k.transpose(0, 2, 3, 1, 4)
    vh = v.transpose(0, 2, 1, 3)
    o_meta = _diff_attend(qh[:, :, :, :N_META], pos[:N_META], kh[:, :, :, :N_META],
                          vh[:, :, :N_META], pos[:N_META], lam)
    nb = seq // Q_BLOCK
    q_blocks = jnp.moveaxis(qh[:, :, :, N_META:].reshape(bsz, C_HEADS, 2, nb, Q_BLOCK, C_QK_DIM), 3, 0)
    pos_blocks = pos[N_META:].reshape(nb, Q_BLOCK)
    o_rest = lax.map(lambda a: _diff_attend(a[0], a[1], kh, vh, pos, lam), (q_blocks, pos_blocks))
    o_rest = jnp.moveaxis(o_rest, 0, 2).reshape(bsz, C_HEADS, seq, C_V_DIM)
    o = jnp.concatenate([o_meta, o_rest], axis=2)
    o = o * lax.rsqrt(jnp.mean(o * o, axis=-1, keepdims=True) + EPS) * subln.astype(f32)
    o = o * (1.0 - lambda_init)
    o = o.transpose(0, 2, 1, 3).reshape(bsz, t_all, C_HEADS * C_V_DIM).astype(hn.dtype)
    return o @ w_out

def _sq_relu_mlp(hn, w1, w2):
    a = jax.nn.relu(hn @ w1)
    return (a * a) @ w2

def second_inputs(seed: int = 0) -> dict:
    key = jax.random.key(seed)
    ks = jax.random.split(key, 24)
    f32 = jnp.float32

    def nrm(k, shape, scale):
        return jax.random.normal(k, shape, f32) * scale

    x = nrm(ks[0], (BATCH, SEQ, D_MODEL), 1.0)
    meta_tokens = nrm(ks[1], (N_META, D_MODEL), 1.0)
    norm_mix = 1.0 + nrm(ks[2], (DEPTH_2, D_MODEL), 0.05)
    norm_mlp = 1.0 + nrm(ks[3], (DEPTH_2, D_MODEL), 0.05)
    norm_final = 1.0 + nrm(ks[4], (D_MODEL,), 0.05)
    ab_w_in = nrm(ks[5], (N_AB, D_MODEL, AB_IN), D_MODEL ** -0.5)
    i_b = -1.0 + nrm(ks[6], (N_AB, A_HEADS), 0.1)
    f_b = jnp.linspace(3.0, 6.0, A_HEADS, dtype=f32)[None, :] + nrm(ks[7], (N_AB, A_HEADS), 0.1)
    ab_if_bias = jnp.concatenate([i_b, f_b], axis=-1)
    mlstm_norm = 1.0 + nrm(ks[8], (N_AB, A_WIDTH), 0.05)
    lru_conv_w = nrm(ks[9], (N_AB, B_CONV, B_WIDTH), B_CONV ** -0.5)
    lru_conv_b = nrm(ks[10], (N_AB, B_WIDTH), 0.01)
    lru_w_r = nrm(ks[11], (N_AB, B_BLOCKS, B_BLOCK_DIM, B_BLOCK_DIM), B_BLOCK_DIM ** -0.5)
    lru_b_r = nrm(ks[12], (N_AB, B_WIDTH), 0.01)
    lru_w_i = nrm(ks[13], (N_AB, B_BLOCKS, B_BLOCK_DIM, B_BLOCK_DIM), B_BLOCK_DIM ** -0.5)
    lru_b_i = nrm(ks[14], (N_AB, B_WIDTH), 0.01)
    u = jax.random.uniform(ks[15], (N_AB, B_WIDTH), f32, 0.9, 0.999)
    p = u ** (1.0 / LRU_C)
    lru_lambda = jnp.log(p) - jnp.log1p(-p)
    ab_w_out = nrm(ks[16], (N_AB, A_WIDTH + B_WIDTH, D_MODEL), (A_WIDTH + B_WIDTH) ** -0.5)
    c_w_in = nrm(ks[17], (N_C, D_MODEL, C_IN), D_MODEL ** -0.5)
    c_lambda = nrm(ks[18], (N_C, 4, C_QK_DIM), 0.1)
    c_subln = 1.0 + nrm(ks[19], (N_C, C_V_DIM), 0.05)
    c_w_out = nrm(ks[20], (N_C, C_HEADS * C_V_DIM, D_MODEL), (C_HEADS * C_V_DIM) ** -0.5)
    mlp_w1 = nrm(ks[21], (DEPTH_2, D_MODEL, D_FF), D_MODEL ** -0.5)
    mlp_w2 = nrm(ks[22], (DEPTH_2, D_FF, D_MODEL), D_FF ** -0.5)
    return {"x": x, "meta_tokens": meta_tokens, "norm_mix": norm_mix, "norm_mlp": norm_mlp,
            "norm_final": norm_final, "ab_w_in": ab_w_in, "ab_if_bias": ab_if_bias,
            "mlstm_norm": mlstm_norm, "lru_conv_w": lru_conv_w, "lru_conv_b": lru_conv_b,
            "lru_w_r": lru_w_r, "lru_b_r": lru_b_r, "lru_w_i": lru_w_i, "lru_b_i": lru_b_i,
            "lru_lambda": lru_lambda, "ab_w_out": ab_w_out, "c_w_in": c_w_in,
            "c_lambda": c_lambda, "c_subln": c_subln, "c_w_out": c_w_out,
            "mlp_w1": mlp_w1, "mlp_w2": mlp_w2}

def second_block(x, meta_tokens, norm_mix, norm_mlp, norm_final, ab_w_in, ab_if_bias,
              mlstm_norm, lru_conv_w, lru_conv_b, lru_w_r, lru_b_r, lru_w_i, lru_b_i,
              lru_lambda, ab_w_out, c_w_in, c_lambda, c_subln, c_w_out, mlp_w1, mlp_w2):
    bsz = x.shape[0]
    meta = jnp.broadcast_to(meta_tokens[None].astype(x.dtype), (bsz, N_META, x.shape[-1]))
    h = jnp.concatenate([meta, x], axis=1)
    for layer in range(DEPTH_2):
        j = layer // 2
        hn = _rmsnorm_2(h, norm_mix[layer])
        if layer % 2 == 0:
            h = h + _ab_mixer(hn, ab_w_in[j], ab_if_bias[j], mlstm_norm[j], lru_conv_w[j],
                              lru_conv_b[j], lru_w_r[j], lru_b_r[j], lru_w_i[j], lru_b_i[j],
                              lru_lambda[j], ab_w_out[j])
        else:
            lambda_init = 0.8 - 0.6 * math.exp(-0.3 * layer)
            h = h + _diff_attn(hn, c_w_in[j], c_lambda[j], c_subln[j], c_w_out[j], lambda_init)
        h = h + _sq_relu_mlp(_rmsnorm_2(h, norm_mlp[layer]), mlp_w1[layer], mlp_w2[layer])
    h = _rmsnorm_2(h, norm_final)
    return h[:, N_META:, :]


def setup_inputs(seed=0):
    out = dict(first_inputs(seed))
    for name, value in second_inputs(seed + 1).items():
        if name != "x":
            out[name + "_2"] = value
    return out


def reference(
    x, norm_w, ffn_w_in, ffn_w_out, ret_w_in, ret_log1m_decay, ret_w_out, conv_w_in, conv_b_in,
    conv_w_dw, conv_b_dw, conv_ln_g, conv_ln_b, conv_w_out, conv_b_out, attn_w_in, attn_w_out,
    meta_tokens_2, norm_mix_2, norm_mlp_2, norm_final_2, ab_w_in_2, ab_if_bias_2, mlstm_norm_2,
    lru_conv_w_2, lru_conv_b_2, lru_w_r_2, lru_b_r_2, lru_w_i_2, lru_b_i_2, lru_lambda_2,
    ab_w_out_2, c_w_in_2, c_lambda_2, c_subln_2, c_w_out_2, mlp_w1_2, mlp_w2_2,
):
    x = first_block(
        x, norm_w, ffn_w_in, ffn_w_out, ret_w_in, ret_log1m_decay, ret_w_out, conv_w_in,
        conv_b_in, conv_w_dw, conv_b_dw, conv_ln_g, conv_ln_b, conv_w_out, conv_b_out,
        attn_w_in, attn_w_out,
    )
    return second_block(
        x, meta_tokens_2, norm_mix_2, norm_mlp_2, norm_final_2, ab_w_in_2, ab_if_bias_2,
        mlstm_norm_2, lru_conv_w_2, lru_conv_b_2, lru_w_r_2, lru_b_r_2, lru_w_i_2, lru_b_i_2,
        lru_lambda_2, ab_w_out_2, c_w_in_2, c_lambda_2, c_subln_2, c_w_out_2, mlp_w1_2,
        mlp_w2_2,
    )


_drawn_inputs = setup_inputs


def setup_inputs(seed=0):
    import zlib

    import numpy as np

    out = dict(_drawn_inputs(seed))
    spreads = {}
    factors = {'mlstm_norm_2': 4.501,
     'lru_conv_b_2': 8.0,
     'lru_b_r_2': 200.0,
     'lru_b_i_2': 64.0,
     'c_lambda_2': 8.0,
     'c_subln_2': 20.739,
     'norm_mlp_2': 2.836,
     'lru_w_r_2': 3.277}
    for name, (base, spread) in spreads.items():
        noise = np.random.default_rng([zlib.crc32(name.encode()), seed]).standard_normal(out[name].shape)
        drawn = base * np.exp(spread * noise) if base else spread * noise
        out[name] = __import__('jax').numpy.asarray(drawn.astype(out[name].dtype))
    for name, factor in factors.items():
        out[name] = (out[name] * factor).astype(out[name].dtype)
    return out
```

```python
from contextlib import ExitStack
import math

import concourse.bass as bass
from concourse import mybir
import numpy as np

F32 = mybir.dt.float32
ALU = mybir.AluOpType
ACT = mybir.ActivationFunctionType
AX = mybir.AxisListType.X

P = 128
D = 1024
DC = D // P
S1 = 256
META = 16
S2 = S1 + META
DEPTH = 4
RMS_EPS, LN_EPS = 1e-6, 1e-5

RET_HEADS, RET_QK, RET_V = 4, 256, 512
RET_IN = 2 * RET_HEADS * (RET_QK + RET_V) // P
FFN = 2816 // P
CONV_TAPS, CONV_PAD = 31, 15
GROUPS = ((128, 1), (512, 4), (2048, 16))
ATT_IN = 3 * 3 * DC
A_HEADS, A_DIM = 4, 256
AB_IN = 6 * DC
LRU_TAPS, LRU_C = 4, 8.0
C_HEADS, C_QK = 8, 64
C_IN = 3 * DC
MLP = 32
LAMBDA_INIT = 0.8 - 0.6 * math.exp(-0.3)
ROPE_THETA, RET_BASE = 500000.0, 10000.0
BIG = 1e30
TILES2 = ((0, 128), (128, 128), (256, 16))
SLOTS = 4
SLOT_TILES = 11


class Phase:

    def __init__(self, name, units, tiles=8, upo=1, pairs=False):
        self.name, self.units, self.tiles, self.upo, self.pairs = name, units, tiles, upo, pairs
        self.outs = units // upo


def plan():
    seq = []
    for layer in range(DEPTH):
        if layer % 3 == 0:
            seq += [Phase(f"ret_qkv{layer}", 32), Phase(f"ret_g{layer}", 16), Phase(f"ret_out{layer}", 16, 8, 2)]
        elif layer % 3 == 1:
            seq += [Phase("conv_in", 16, pairs=True), Phase("conv_out", 8)]
        else:
            seq += [Phase("att_in", ATT_IN), Phase("att_out", 8)]
        seq += [Phase(f"ffn_in{layer}", 2 * FFN, pairs=True), Phase(f"ffn_out{layer}", 16, FFN // 2, 2)]
    seq += [Phase("ab_in", AB_IN), Phase("ab_out", 16, 8, 2)]
    seq += [Phase("mlp_in0", MLP), Phase("mlp_out0", MLP, 8, 4)]
    seq += [Phase("c_in", C_IN), Phase("c_out", 8)]
    seq += [Phase("mlp_in1", MLP), Phase("mlp_out1", MLP, 8, 4)]
    unit = out = pair = 0
    for ph in seq:
        ph.unit0, ph.out0, ph.pair0 = unit, out, pair
        unit += ph.units
        if ph.pairs:
            pair += ph.units // 2
        else:
            out += ph.outs
    return seq



def constants():
    p = np.arange(P)
    first, second = {}, {}
    first["ident"] = np.eye(P)
    first["mean"] = np.full((P, P), 1.0 / D)
    first["ones"] = np.ones((P, P))
    swap = np.zeros((P, P))
    half = 8
    for base in (0, 64):
        for i in range(half):
            swap[base + half + i, base + i] = -1.0
            swap[base + i, base + half + i] = 1.0
    first["swap"] = swap
    inv = (np.float32(1.0) / np.float32(RET_BASE) ** np.linspace(0.0, 1.0, RET_QK // 2, dtype=np.float32)).astype(np.float32)
    ang = (np.arange(S1, dtype=np.float32)[None, :] * inv[:, None]).astype(np.float32).astype(np.float64)
    first["ret_cos"], first["ret_sin"] = np.cos(ang), np.sin(ang)
    inv = (np.float32(ROPE_THETA) ** (-np.arange(0, 16, 2, dtype=np.float32) / np.float32(16))).astype(np.float32)
    ang = (np.arange(S2, dtype=np.float32)[None, :] * inv[:, None]).astype(np.float32).astype(np.float64)
    cos, sin = np.ones((P, S2)), np.zeros((P, S2))
    for base in (0, 64):
        for i in range(16):
            cos[base + i], sin[base + i] = np.cos(ang[i % 8]), np.sin(ang[i % 8])
    first["rope_cos"], first["rope_sin"] = cos, sin
    first["rms_eps"], first["ln_eps"] = np.full((P, 1), RMS_EPS), np.full((P, 1), LN_EPS)
    first["one"] = np.ones((P, 1))
    n = np.arange(S1)
    m = np.arange(2)[:, None] * P + p[None, :]
    gap = n[None, None, :] - m[:, :, None]
    first_b = {}
    first_b["after"] = np.concatenate([np.maximum(gap[t], 0) for t in range(2)], 1)
    first_b["before"] = np.concatenate([np.maximum(-gap[t], 0) for t in range(2)], 1)
    masks = []
    for it in range(2):
        q = it * P + p[:, None]
        k = np.arange(S1)[None, :]
        for window, dil in GROUPS:
            radius = window // (2 * dil)
            live = ((q - k) % dil == 0) & (np.abs(q // dil - k // dil) <= radius)
            masks.append(np.where(live, 0.0, -BIG))
    first_b["att_mask"] = np.concatenate(masks, 1)
    pos = np.arange(S2)[None, :]
    row = [t0 + p[:, None] for t0, _ in TILES2]
    second["causal_T"] = np.concatenate([np.where(r > pos, BIG, 0.0) for r in row], 1)
    second["causal"] = np.concatenate([np.where(pos > r, -BIG, 0.0) for r in row], 1)
    sel = np.zeros((P, A_HEADS * P))
    for h in range(A_HEADS):
        sel[h, h * P:(h + 1) * P] = 1.0
    second["sel"] = sel

    def packed(parts):
        where, at = {}, 0
        for name, a in parts.items():
            where[name] = (at, a.shape[1])
            at += a.shape[1]
        return np.ascontiguousarray(np.concatenate(list(parts.values()), 1), dtype=np.float32), where

    return packed(first), packed(first_b), packed(second)


PARAMS = (
    ("norm_w", DEPTH * 4 * DC), ("conv_b_in", 2 * DC), ("conv_w_dw", DC * CONV_TAPS), ("conv_b_dw", DC),
    ("conv_ln_g", DC), ("conv_ln_b", DC), ("conv_b_out", DC), ("norm_mix", 2 * DC), ("norm_mlp", 2 * DC),
    ("norm_final", DC), ("mlstm_norm", DC), ("lru_conv_w", DC * LRU_TAPS), ("lru_conv_b", DC), ("lru_b_r", DC),
    ("lru_b_i", DC), ("lru_lambda", DC), ("subln", 1), ("decay", 2 * 2 * RET_HEADS), ("if_bias", 2),
    ("c_lambda", 4 * C_QK),
)
PARAM_AT = {}
_at = 0
for _name, _n in PARAMS:
    PARAM_AT[_name] = _at
    _at += _n
N_PARAMS = _at


def build(nc, dram, out, const_at):
    at_a, at_b, at_c = const_at
    phases = plan()
    ph = {x.name: x for x in phases}
    with ExitStack() as ctx:
        def sb(name, shape):
            return ctx.enter_context(nc.sbuf_tensor(name, shape, F32))

        def sem(name):
            return ctx.enter_context(nc.semaphore(name))

        ring = [sb(f"weights{s}", [P, SLOT_TILES, P]) for s in range(SLOTS)]
        x = sb("x", [P, DC, S1])
        h = sb("h", [P, DC, S2])
        xn = sb("xn", [P, DC, S2])
        y = sb("y", [P, DC, S2])
        sq = sb("sq", [P, DC, S2])
        proj_raw = sb("proj", [P, ATT_IN * S1])
        scr = sb("scratch", [P, 10240])
        ca = sb("const_a", [P, sum(n for _, n in at_a.values())])
        n_b = max(sum(n for _, n in at_b.values()), sum(n for _, n in at_c.values()))
        cb = sb("const_b", [P, n_b])
        par = sb("params", [P, N_PARAMS])
        w_r = x[:, 0:DC // 2, :].rearrange("p c t -> p (c t)").rearrange("p (n e) -> p n e", n=DC)
        w_i = x[:, DC // 2:DC, :].rearrange("p c t -> p (c t)").rearrange("p (n e) -> p n e", n=DC)
        w_gates = sb("w_gates", [P, DC, 2 * A_HEADS])
        rstd = sb("rstd", [P, S2])
        lnv = sb("lnv", [P, S2])
        silu = sb("silu", [P, 4, S2])
        small = sb("small", [P, 64])
        PS = ctx.enter_context(nc.psum_tensor("acc", [P, 8, 512], F32))

        proj1 = proj_raw[:, :].rearrange("p (c t) -> p c t", t=S1)
        proj2 = proj_raw[:, 0:AB_IN * S2].rearrange("p (c t) -> p c t", t=S2)
        spare = proj_raw[:, AB_IN * S2:]

        def const(name):
            for buf, at in ((ca, at_a), (cb, at_b), (cb, at_c)):
                if name in at:
                    return buf[:, at[name][0]:at[name][0] + at[name][1]]
            raise KeyError(name)

        def param(name, c=0, n=1):
            return par[:, PARAM_AT[name] + c:PARAM_AT[name] + c + n]

        ident, mean, ones, swap = const("ident"), const("mean"), const("ones"), const("swap")
        rope_cos, rope_sin = const("rope_cos"), const("rope_sin")
        rms_eps, ln_eps, one = const("rms_eps"), const("ln_eps"), const("one")

        x_loaded = sem("x_loaded")
        consts_loaded = sem("consts_loaded")
        consts2_loaded = sem("consts2_loaded")
        meta_loaded = sem("meta_loaded")
        weights_loaded = [sem(f"weights{s}_loaded") for s in range(SLOTS)]
        unit_multiplied = sem("unit_multiplied")
        out_evacuated = sem("out_evacuated")
        gate_ready = sem("gate_ready")
        pair_done = sem("pair_done")
        relu_ready = sem("relu_ready")
        hidden_ready = sem("hidden_ready")
        squares_ready = sem("squares_ready")
        sum_ready = sem("sum_ready")
        rstd_ready = sem("rstd_ready")
        xn_ready = sem("xn_ready")
        x_ready = sem("x_ready")
        act_chain = sem("act_chain")
        dve_chain = sem("dve_chain")
        out_stored = sem("out_stored")
        wait_taken = sem("wait_taken")
        relu_used = sem("relu_used")
        c_logged, c_rot, c_m1, c_d1, c_d2 = (sem("c_" + n) for n in ("logged", "rotation_parts", "maxima", "den_inverse", "scaled"))
        att_rot, att_m1, att_m2 = (sem("att_" + n) for n in ("rotation_parts", "maxima", "maximum"))

        FREE_BANKS, FREE_PAIRS = 4, 2

        def evacuated(phase, n=None):
            return FREE_BANKS + phase.out0 + (phase.outs if n is None else n)

        def pairs_done(phase):
            return FREE_PAIRS + phase.pair0 + phase.units // 2

        def region(buf, at, *shape):
            n = int(np.prod(shape))
            v = buf[:, at:at + n]
            if len(shape) == 2:
                v = v.rearrange("p (a b) -> p a b", a=shape[0])
            return v

        def spread(row, n):
            return row.unsqueeze(1).to_broadcast((row.shape[0], n, row.shape[1]))

        ret_decay = region(scr, 0, RET_HEADS, 512)
        ret_p = region(scr, 2048, 2, 512)
        ret_exp = region(scr, 3072, 2, 512)
        ret_half = region(scr, 4096, 4, 1024)
        ret_sq = region(scr, 8192, 4, S1)
        ret_v = region(proj_raw, 48 * S1, 2, 2048)
        lg = small[:, 0:16]
        conv_u = proj1[:, 0:DC, :]
        conv_acc = proj1[:, DC:2 * DC, :]
        conv_sq = proj1[:, 2 * DC:3 * DC, :]
        conv_mix = proj1[:, 3 * DC:4 * DC, :]
        att_q = region(scr, 0, 3, S1)
        att_k = region(scr, 768, 3, S1)
        att_vs = region(scr, 1536, 3, S1)
        att_vn = region(scr, 2304, 6, P)
        att_s = region(scr, 3072, 2, 768)
        att_p = region(scr, 4608, 2, 768)
        att_pt = region(scr, 6144, 2, 768)
        att_o = region(scr, 7680, 2, P)
        att_t = region(scr, 7936, 6, S1)
        att_max = small[:, 16:26].rearrange("p (u k) -> p u k", u=2)
        att_den = small[:, 26:28]
        att_rden = small[:, 28:30]
        ab_row = region(scr, 0, 10, S2)
        r_in, r_f, r_e, r_l, r_lf, r_F, r_a, r_m, r_en, r_sum = (ab_row[0:A_HEADS, i, :] for i in range(10))
        ab_t = region(scr, 10 * S2, 3, S2)
        ab_w = region(scr, 13 * S2, 3, S2)
        ab_p = region(scr, 16 * S2, 6, S2)
        ab_den = region(scr, 22 * S2, 4, S2)
        ab_hh = region(scr, 26 * S2, 4, S2)
        ab_sq = region(scr, 30 * S2, 2, S2)
        ab_r = region(scr, 32 * S2, 2, S2)
        ab_v = region(spare, 0, 3, D)
        ab_col = small[:, 32:44].rearrange("p (t n) -> p t n", t=3)
        lru_xb, lru_gate, lru_out = proj2[:, 32:40, :], proj2[:, 40:48, :], proj2[:, 8:16, :]
        lru_xc, lru_r, lru_i, lru_a = y, xn, proj2[:, 32:40, :], sq
        lam8 = small[:, 44:52]
        lam_t = region(scr, 34 * S2, 4, DC)
        c_q, c_k, c_vs = scr[:, 0:S2], scr[:, S2:2 * S2], scr[:, 2 * S2:3 * S2]
        c_t = region(scr, 3 * S2, 2, S2)
        c_vn = region(scr, 5 * S2, 3, P)
        c_s = region(scr, 7 * S2, 4, S2)
        c_p = region(scr, 11 * S2, 4, S2)
        c_pd = region(scr, 15 * S2, 2, S2)
        c_pt = region(scr, 17 * S2, 3, S2)
        c_sq, c_ln, c_r = scr[:, 20 * S2:21 * S2], scr[:, 21 * S2:22 * S2], scr[:, 22 * S2:23 * S2]
        c_max = small[:, 52:60].rearrange("p (u k) -> p u k", u=2)
        c_den = small[:, 60:64].rearrange("p (u k) -> p u k", u=2)
        lam_s = scr[:, 23 * S2:23 * S2 + 2 * C_QK + 8]
        neg_lam = small[:, 30:31]
        subln = small[:, 31:32]

        def sems(prefix, names):
            return {n: sem(prefix + n) for n in names.split()}

        ret_sem = sems("ret_", "v_turned v_ready lg_in lg_ready exponent_ready decay_ready roped scores_ready p_ready "
                               "o_ready squares_ready sum_ready rstd_ready gated")
        conv_sem = sems("conv_", "acc_ready mean_ready centered squares_ready var_ready rstd_ready scaled mixed")
        att_sem = sems("att_", "rotated roped v_staged v_turned v_ready scores_ready max_ready p_ready den_ready "
                               "p_turned pt_ready o_ready o_scaled o_turned mixed")
        ab_sem = sems("ab_", "gate_sums log_in log_ready rows_ready floor_in floor_ready turned cols_ready v_turned "
                             "v_ready run_ready shifted w_ready scores_ready p_ready num_ready floor_spread den_abs h_ready "
                             "squares_ready sum_ready rstd_ready mixed")
        lru_sem = sems("lru_", "lam_ready softplus_ready conv_ready gates_summed gates_ready loga_ready a_ready root_in "
                               "root_ready gelu_in gelu_ready done")
        c_sem = sems("c_", "lam_in lam_exp rotated roped v_staged v_turned v_ready scores_ready max_ready p_ready "
                           "pd_ready p_turned pt_ready o_ready squares_ready sum_ready rstd_ready mixed")

        block = ctx.enter_context(nc.Block())

        @block.sync
        def _(sp):
            sp.dma_start(x[:, :, :], dram["x"]).then_inc(x_loaded, 16)
            sp.dma_start(ca[:, :], dram["const_a"]).then_inc(consts_loaded, 16)
            sp.dma_start(par[:, :], dram["params"]).then_inc(consts_loaded, 16)

            def load(phase, slot, unit):
                n = phase.tiles * P
                sp.dma_start(ring[slot][:, 0:phase.tiles, :].rearrange("p k f -> p (k f)"),
                             dram[phase.name][unit, :, 0:n]).then_inc(weights_loaded[slot], 16)

            for number, phase in enumerate(phases):
                first = 0
                if number == 0:
                    for s in range(SLOTS):
                        load(phase, s, s)
                    sp.dma_start(cb[:, 0:sum(n for _, n in at_b.values())], dram["const_b"]).then_inc(consts_loaded, 16)
                    first = 1
                with sp.Fori(first, phase.units // SLOTS) as i:
                    for s in range(SLOTS):
                        sp.wait_ge(unit_multiplied, phase.unit0 + i * SLOTS + (s - SLOTS + 1))
                        load(phase, s, i * SLOTS + s)
            sp.wait_ge(xn_ready, 13)
            sp.dma_start(out, xn[:, :, META:S2]).then_inc(out_stored, 16)
            sp.wait_ge(out_stored, 16)

        @block.gpsimd
        def _(pool):
            pool.dma_start(h[:, :, 0:META], dram["meta"]).then_inc(meta_loaded, 16)
            pool.dma_start(w_gates[:, :, :], dram["ab_gates"]).then_inc(meta_loaded, 16)
            pool.wait_ge(x_ready, 2 * DEPTH)
            pool.dma_start(cb[:, 0:sum(n for _, n in at_c.values())], dram["const_c"]).then_inc(consts2_loaded, 16)
            pool.dma_start(w_r, dram["lru_w_r"]).then_inc(consts2_loaded, 16)
            pool.dma_start(w_i, dram["lru_w_i"]).then_inc(consts2_loaded, 16)

        @block.tensor
        def _(pe):
            def dense(phase, src, n, free, first_free):
                body = max(SLOTS, 2 * phase.upo)
                banks = SLOTS if phase.upo == 1 else 2
                with pe.Fori(0, phase.units // body) as i:
                    for u in range(body):
                        s, o = u % SLOTS, u // phase.upo
                        pe.wait_ge(weights_loaded[s], i * (16 * body // SLOTS) + 16 * (phase.unit0 // SLOTS + u // SLOTS + 1))
                        if phase.pairs:
                            if u % 2 == 0:
                                pe.wait_ge(free, i * (body // 2) + (first_free + u // 2))
                        elif u % phase.upo == 0:
                            pe.wait_ge(free, i * (body // phase.upo) + (first_free + o))
                        acc = PS[:, o % banks, 0:n]
                        for k in range(phase.tiles):
                            kk = (u % phase.upo) * phase.tiles + k
                            last = nc.tensor.matmul(acc, ring[s][:, k, :], src(kk),
                                                    start=(kk == 0), stop=(kk == phase.upo * phase.tiles - 1))
                        last.then_inc(unit_multiplied, 1)

            def dense_outputs(phase, src, n):
                banks = SLOTS if phase.upo == 1 else 2
                dense(phase, src, n, out_evacuated, FREE_BANKS + phase.out0 - banks + 1)

            def dense_pairs(phase, src, n):
                dense(phase, src, n, pair_done, FREE_PAIRS + phase.pair0 - 1)

            def norm_sum(k, n):
                for c in range(DC):
                    pe.wait_ge(squares_ready, DC * k + c + 1)
                    last = nc.tensor.matmul(PS[:, 4, 0:n], mean, sq[:, c, 0:n], start=(c == 0), stop=(c == DC - 1))
                last.then_inc(sum_ready, 1)

            def retention(j, layer):
                g_end = evacuated(ph[f"ret_g{layer}"])
                R = ret_sem
                pe.wait_ge(R["roped"], 2 * j + 2)
                pe.wait_ge(R["v_ready"], 8 * j + 8)
                pe.wait_ge(out_evacuated, g_end)

                def scores(hd):
                    acc = PS[:, 4 + hd % 2, :]
                    for kt in range(2):
                        for c in range(2):
                            last = nc.tensor.matmul(acc[:, kt * S1:(kt + 1) * S1],
                                                    proj1[:, 8 + 2 * hd + c, kt * P:(kt + 1) * P], proj1[:, 2 * hd + c, :],
                                                    start=(c == 0), stop=(c == 1))
                    last.then_inc(R["scores_ready"], 1)

                scores(0)
                for hd in range(RET_HEADS):
                    n = 4 * j + hd
                    if hd + 1 < RET_HEADS:
                        if hd >= 1:
                            pe.wait_ge(R["p_ready"], n)
                        scores(hd + 1)
                    pe.wait_ge(R["p_ready"], n + 1)
                    if hd >= 2:
                        pe.wait_ge(R["gated"], n - 1)
                    first = 6 if hd % 2 == 0 else 0
                    for e in range(4):
                        acc = PS[:, first + e // 2, (e % 2) * S1:(e % 2 + 1) * S1]
                        for kt in range(2):
                            last = nc.tensor.matmul(acc, ret_v[:, kt, hd * RET_V + e * P:hd * RET_V + (e + 1) * P],
                                                    ret_p[:, hd % 2, kt * S1:(kt + 1) * S1], start=(kt == 0), stop=(kt == 1))
                    last.then_inc(R["o_ready"], 1)
                    pe.wait_ge(R["squares_ready"], n + 1)
                    for e in range(4):
                        last = nc.tensor.matmul(PS[:, 2 + hd % 2, 0:S1], mean, ret_sq[:, e, :], start=(e == 0), stop=(e == 3))
                    last.then_inc(R["sum_ready"], 1)

            def turn_values(j, layer):
                pe.wait_ge(out_evacuated, evacuated(ph[f"ret_qkv{layer}"]))
                for b in range(8):
                    hd, kt = b // 2, b % 2
                    if b >= 2:
                        pe.wait_ge(ret_sem["v_ready"], 8 * j + b - 1)
                    for e in range(4):
                        last = nc.tensor.transpose(PS[:, 4 + b % 2, e * P:(e + 1) * P],
                                                   proj1[:, 16 + 4 * hd + e, kt * P:(kt + 1) * P], ident)
                    last.then_inc(ret_sem["v_turned"], 1)

            def conv():
                C = conv_sem
                pe.wait_ge(C["acc_ready"], 1)
                for c in range(DC):
                    last = nc.tensor.matmul(PS[:, 4, 0:S1], mean, conv_acc[:, c, :], start=(c == 0), stop=(c == DC - 1))
                last.then_inc(C["mean_ready"], 1)
                pe.wait_ge(C["squares_ready"], 1)
                for c in range(DC):
                    last = nc.tensor.matmul(PS[:, 5, 0:S1], mean, conv_sq[:, c, :], start=(c == 0), stop=(c == DC - 1))
                last.then_inc(C["var_ready"], 1)

            def attention():
                A = att_sem
                pe.wait_ge(out_evacuated, evacuated(ph["att_in"]))
                with pe.Fori(0, DC) as i:
                    pe.wait_ge(A["roped"], i * 3 + 3)
                    for g in range(3):
                        for w in range(2):
                            last = nc.tensor.matmul(PS[:, g, w * S1:(w + 1) * S1], swap, proj1[:, i + (g * 24 + w * 8), :],
                                                    start=True, stop=True)
                        last.then_inc(A["rotated"], 1)
                    pe.wait_ge(A["v_staged"], i * 3 + 3)
                    for g in range(3):
                        for kt in range(2):
                            last = nc.tensor.transpose(PS[:, 3 + g // 2, (g % 2) * S1 + kt * P:(g % 2) * S1 + (kt + 1) * P],
                                                       att_vs[:, g, kt * P:(kt + 1) * P], ident)
                    last.then_inc(A["v_turned"], 1)
                    pe.wait_ge(A["roped"], i * 3 + 6)

                    def scores(u):
                        e, it = u // 2, u % 2
                        rows = slice(64 * e, 64 * e + 64)
                        for g in range(3):
                            b = (5 if u % 2 == 0 else 0) + g // 2
                            last = nc.tensor.matmul(PS[:, b, (g % 2) * S1:(g % 2 + 1) * S1],
                                                    att_q[rows, g, it * P:(it + 1) * P], att_k[rows, g, :], start=True, stop=True)
                        last.then_inc(A["scores_ready"], 1)

                    scores(0)
                    for u in range(4):
                        e = u // 2
                        if u < 3:
                            scores(u + 1)
                        pe.wait_ge(A["p_ready"], i * 4 + (u + 1))
                        if u == 0:
                            pe.wait_ge(A["v_ready"], i + 1)
                        for t in range(6):
                            acc = PS[:, 7, t * P:(t + 1) * P] if t < 4 else PS[:, 4, S1 + (t - 4) * P:S1 + (t - 3) * P]
                            last = nc.tensor.transpose(acc, att_p[:, u % 2, t * P:(t + 1) * P], ident)
                        last.then_inc(A["p_turned"], 1)
                        pe.wait_ge(A["pt_ready"], i * 8 + 2 * (u + 1))
                        for t in range(6):
                            last = nc.tensor.matmul(PS[:, 3, u * 64:(u + 1) * 64], att_pt[:, u % 2, t * P:(t + 1) * P],
                                                    att_vn[:, t, e * 64:(e + 1) * 64], start=(t == 0), stop=(t == 5))
                        last.then_inc(A["o_ready"], 1)
                    pe.wait_ge(A["o_scaled"], i * 4 + 4)
                    for it in range(2):
                        last = nc.tensor.transpose(PS[:, 6, S1 + it * P:S1 + (it + 1) * P], att_o[:, it, :], ident)
                    last.then_inc(A["o_turned"], 1)
                pe.wait_ge(A["mixed"], DC)

            def gates():
                pe.wait_ge(meta_loaded, 32)
                for gate in range(2):
                    for k in range(DC):
                        last = nc.tensor.matmul(PS[0:A_HEADS, 5 + gate, 0:S2], w_gates[:, k, gate * A_HEADS:(gate + 1) * A_HEADS],
                                                xn[:, k, :], start=(k == 0), stop=(k == DC - 1))
                last.then_inc(ab_sem["gate_sums"], 1)

            def mlstm():
                A = ab_sem
                pe.wait_ge(out_evacuated, evacuated(ph["ab_in"]))
                for st, (t0, tl) in enumerate(TILES2):
                    if st >= 2:
                        pe.wait_ge(A["v_ready"], st - 1)
                    for c in range(DC):
                        b = 2 * (st % 2) + c // 4
                        last = nc.tensor.transpose(PS[0:tl, b, (c % 4) * P:(c % 4 + 1) * P], proj2[:, 16 + c, t0:t0 + tl], ident)
                    last.then_inc(A["v_turned"], 1)
                pe.wait_ge(A["rows_ready"], 1)
                for st, (t0, tl) in enumerate(TILES2):
                    last = nc.tensor.transpose(PS[0:tl, 7, st * 4:st * 4 + 4], r_a[:, t0:t0 + tl], ident[0:A_HEADS, 0:A_HEADS])
                last.then_inc(A["turned"], 1)
                pe.wait_ge(A["v_ready"], 3)
                pe.wait_ge(A["floor_ready"], 1)
                pe.wait_ge(A["cols_ready"], 1)
                pe.wait_ge(consts2_loaded, 48)
                sel = const("sel")
                for hd in range(A_HEADS):
                    if hd >= 1:
                        pe.wait_ge(A["h_ready"], hd)
                        pe.wait_ge(A["p_ready"], 3 * hd)
                    head_sel = sel[0:A_HEADS, hd * P:(hd + 1) * P]
                    nc.tensor.matmul(PS[:, 0, 0:S2], head_sel, r_m, start=True, stop=True).then_inc(A["run_ready"], 1)
                    for st, (t0, tl) in enumerate(TILES2):
                        for c in range(2):
                            last = nc.tensor.matmul(PS[0:tl, 1 + st, 0:S2], proj2[:, 8 + 2 * hd + c, t0:t0 + tl],
                                                    proj2[:, 2 * hd + c, :], start=(c == 0), stop=(c == 1))
                        last.then_inc(A["scores_ready"], 1)
                    nc.tensor.matmul(PS[:, 7, 0:S2], head_sel, r_en, start=True, stop=True)
                    pe.wait_ge(A["p_ready"], 3 * hd + 3)
                    pt = [ab_p[0:tl, 3 * (hd % 2) + st, :] for st, (_, tl) in enumerate(TILES2)]
                    for st, (_, tl) in enumerate(TILES2):
                        nc.tensor.matmul(PS[:, 4, 0:S2], ones[0:tl, :], pt[st], start=(st == 0), stop=(st == 2))
                    for c in range(2):
                        for st, (_, tl) in enumerate(TILES2):
                            last = nc.tensor.matmul(PS[:, 5 + c, 0:S2], ab_v[0:tl, st, hd * A_DIM + c * P:hd * A_DIM + (c + 1) * P],
                                                    pt[st], start=(st == 0), stop=(st == 2))
                    last.then_inc(A["num_ready"], 1)
                    pe.wait_ge(A["squares_ready"], hd + 1)
                    for c in range(2):
                        last = nc.tensor.matmul(PS[:, 0, 0:S2], mean, ab_sq[:, c, :], start=(c == 0), stop=(c == 1))
                    last.then_inc(A["sum_ready"], 1)
                    pe.wait_ge(A["rstd_ready"], hd + 1)

            def lru_gates():
                L = lru_sem
                pe.wait_ge(L["conv_ready"], 1)
                pe.wait_ge(ab_sem["h_ready"], A_HEADS)
                for c in range(DC):
                    if c >= 2:
                        pe.wait_ge(L["gates_ready"], 2 * (c - 1))
                    for gate, w in ((0, w_r), (1, w_i)):
                        last = nc.tensor.matmul(PS[:, 2 * (c % 2) + gate, 0:S2], w[:, c, :], lru_xc[:, c, :], start=True, stop=True)
                    last.then_inc(L["gates_summed"], 1)

            def diff_attention():
                A = c_sem
                pe.wait_ge(out_evacuated, evacuated(ph["c_in"]))
                with pe.Fori(0, C_HEADS) as i:
                    pe.wait_ge(A["roped"], i + 1)
                    for w in range(2):
                        last = nc.tensor.matmul(PS[:, w, 0:S2], swap, proj2[:, i + w * 8, :], start=True, stop=True)
                    last.then_inc(A["rotated"], 1)
                    pe.wait_ge(A["mixed"], i + 1)
                    pe.wait_ge(A["v_staged"], i + 1)
                    for st, (t0, tl) in enumerate(TILES2):
                        last = nc.tensor.transpose(PS[0:tl, 2, st * P:(st + 1) * P], c_vs[:, t0:t0 + tl], ident)
                    last.then_inc(A["v_turned"], 1)
                    pe.wait_ge(A["roped"], i + 2)

                    def scores(u):
                        t0, tl = TILES2[u]
                        for e in range(2):
                            rows = slice(64 * e, 64 * e + 64)
                            last = nc.tensor.matmul(PS[0:tl, 3 + 2 * (u % 2) + e, 0:t0 + tl], c_q[rows, t0:t0 + tl],
                                                    c_k[rows, 0:t0 + tl], start=True, stop=True)
                        last.then_inc(A["scores_ready"], 1)

                    scores(0)
                    for u, (t0, tl) in enumerate(TILES2):
                        if u < 2:
                            scores(u + 1)
                        pe.wait_ge(A["pd_ready"], i * 3 + (u + 1))
                        if u == 2:
                            pe.sem_inc(wait_taken, 1)
                        for st in range(u + 1):
                            s0, sl = TILES2[st]
                            last = nc.tensor.transpose(PS[0:sl, (7, 0, 1)[st], t0:t0 + tl], c_pd[0:tl, u % 2, s0:s0 + sl],
                                                       ident[0:tl, 0:tl])
                        last.then_inc(A["p_turned"], 1)
                    pe.wait_ge(A["v_ready"], i + 1)
                    pe.wait_ge(A["pt_ready"], i + 1)
                    for st, (s0, sl) in enumerate(TILES2):
                        last = nc.tensor.matmul(PS[:, 2, s0:S2], c_vn[0:sl, st, :], c_pt[0:sl, st, s0:S2],
                                                start=(st == 0), stop=(st == 2))
                    last.then_inc(A["o_ready"], 1)
                    pe.wait_ge(A["squares_ready"], i + 1)
                    nc.tensor.matmul(PS[:, 5, 0:S2], mean, c_sq, start=True, stop=True).then_inc(A["sum_ready"], 1)
                pe.wait_ge(A["mixed"], C_HEADS + 1)

            pe.wait_ge(consts_loaded, 48)
            for layer in range(DEPTH):
                norm_sum(4 * layer, S1)
                pe.wait_ge(xn_ready, 2 * layer + 1)
                normed = lambda k: xn[:, k, 0:S1]
                if layer % 3 == 0:
                    j = layer // 3
                    dense_outputs(ph[f"ret_qkv{layer}"], normed, S1)
                    turn_values(j, layer)
                    dense_outputs(ph[f"ret_g{layer}"], normed, S1)
                    retention(j, layer)
                    pe.wait_ge(ret_sem["gated"], 4 * j + 4)
                    dense_outputs(ph[f"ret_out{layer}"], lambda k: proj1[:, 32 + k, :], S1)
                elif layer % 3 == 1:
                    dense_pairs(ph["conv_in"], normed, S1)
                    conv()
                    pe.wait_ge(conv_sem["mixed"], 1)
                    dense_outputs(ph["conv_out"], lambda k: conv_mix[:, k, :], S1)
                else:
                    dense_outputs(ph["att_in"], normed, S1)
                    attention()
                    dense_outputs(ph["att_out"], lambda k: proj1[:, k, :], S1)
                norm_sum(4 * layer + 1, S1)
                norm_sum(4 * layer + 2, S1)
                pe.wait_ge(xn_ready, 2 * layer + 2)
                dense_pairs(ph[f"ffn_in{layer}"], normed, S1)
                pe.wait_ge(pair_done, pairs_done(ph[f"ffn_in{layer}"]))
                dense_outputs(ph[f"ffn_out{layer}"], lambda k: proj1[:, k, :], S1)
                norm_sum(4 * layer + 3, S1)
            normed2 = lambda k: xn[:, k, :]
            hidden2 = lambda k: proj2[:, k, :]
            for layer in range(2):
                norm_sum(16 + 2 * layer, S2)
                pe.wait_ge(xn_ready, 8 + 2 * layer + 1)
                if layer == 0:
                    gates()
                    dense_outputs(ph["ab_in"], normed2, S2)
                    mlstm()
                    lru_gates()
                    pe.wait_ge(ab_sem["mixed"], A_HEADS)
                    pe.wait_ge(lru_sem["done"], 1)
                    dense_outputs(ph["ab_out"], hidden2, S2)
                else:
                    dense_outputs(ph["c_in"], normed2, S2)
                    diff_attention()
                    dense_outputs(ph["c_out"], hidden2, S2)
                norm_sum(17 + 2 * layer, S2)
                pe.wait_ge(xn_ready, 8 + 2 * layer + 2)
                dense_outputs(ph[f"mlp_in{layer}"], normed2, S2)
                pe.wait_ge(hidden_ready, MLP * (layer + 1))
                dense_outputs(ph[f"mlp_out{layer}"], hidden2, S2)
            norm_sum(20, S2)

        @block.scalar
        def _(act):
            chain = [0]

            def step(ins):
                chain[0] += 1
                ins.then_inc(act_chain, 1)
                act.wait_ge(act_chain, chain[0])

            def evacuate(phase, dst, n, func=ACT.Copy, start=0, count=None, bias=None):
                count = phase.outs if count is None else count
                body = SLOTS if phase.upo == 1 else 2
                banks = body
                with act.Fori(0, count // body) as i:
                    for o in range(body):
                        act.wait_ge(unit_multiplied, i * (body * phase.upo) + (phase.unit0 + (start + o + 1) * phase.upo))
                        extra = {} if bias is None else {"bias": param(bias, 0, DC)[:, bass.ds(i * body + o, 1)]}
                        nc.scalar.activation(dst[:, i * body + o, 0:n], PS[:, o % banks, 0:n], func, **extra)\
                            .then_inc(out_evacuated, 1)

            def norm(k, src, n):
                for c in range(DC):
                    nc.scalar.activation(sq[:, c, 0:n], src[:, c, 0:n], ACT.Square).then_inc(squares_ready, 1)
                act.wait_ge(sum_ready, k + 1)
                step(nc.scalar.activation(lnv[:, 0:n], PS[:, 4, 0:n], ACT.Ln, bias=rms_eps))
                nc.scalar.activation(rstd[:, 0:n], lnv[:, 0:n], ACT.Exp, scale=-0.5).then_inc(rstd_ready, 1)

            def post_norm(k, phase, n):
                act.wait_ge(out_evacuated, evacuated(phase))
                norm(k, y, n)

            def silu_pairs(phase):
                with act.Fori(0, phase.units // SLOTS) as i:
                    for q in range(2):
                        act.wait_ge(unit_multiplied, i * SLOTS + (phase.unit0 + 2 * q + 1))
                        nc.scalar.activation(silu[:, q, 0:S1], PS[:, 2 * q, 0:S1], ACT.Silu).then_inc(gate_ready, 1)

            def decay(j):
                for hd in range(RET_HEADS):
                    act.wait_ge(ret_sem["exponent_ready"], 4 * j + hd + 1)
                    nc.scalar.activation(ret_decay[:, hd, :], ret_exp[:, hd % 2, :], ACT.Exp).then_inc(ret_sem["decay_ready"], 1)

            def retention(j):
                R = ret_sem
                for hd in range(RET_HEADS):
                    n = 4 * j + hd
                    first = 6 if hd % 2 == 0 else 0
                    act.wait_ge(R["o_ready"], n + 1)
                    nc.scalar.activation(ret_sq[:, :, :], PS[:, first:first + 2, :].rearrange("p b (e t) -> p (b e) t", t=S1),
                                         ACT.Square).then_inc(R["squares_ready"], 1)
                    act.wait_ge(R["sum_ready"], n + 1)
                    step(nc.scalar.activation(lnv[:, 0:S1], PS[:, 2 + hd % 2, 0:S1], ACT.Ln, bias=rms_eps, scale=float(D) / RET_V))
                    if hd >= 1:
                        act.wait_ge(R["gated"], n)
                    nc.scalar.activation(rstd[:, 0:S1], lnv[:, 0:S1], ACT.Exp, scale=-0.5).then_inc(R["rstd_ready"], 1)

            def conv():
                C = conv_sem
                act.wait_ge(C["centered"], 1)
                nc.scalar.activation(conv_sq[:, :, :], conv_acc[:, :, :], ACT.Square).then_inc(C["squares_ready"], 1)
                act.wait_ge(C["var_ready"], 1)
                step(nc.scalar.activation(lnv[:, 0:S1], PS[:, 5, 0:S1], ACT.Ln, bias=ln_eps))
                nc.scalar.activation(rstd[:, 0:S1], lnv[:, 0:S1], ACT.Exp, scale=-0.5).then_inc(C["rstd_ready"], 1)
                act.wait_ge(C["scaled"], 1)
                for c in range(DC):
                    last = nc.scalar.activation(conv_mix[:, c, :], conv_sq[:, c, :], ACT.Silu, bias=param("conv_ln_b", c),
                                                scale=param("conv_ln_g", c))
                last.then_inc(C["mixed"], 1)

            def attention():
                A = att_sem
                act.wait_ge(out_evacuated, evacuated(ph["att_in"]))
                with act.Fori(0, DC) as i:
                    for g in range(3):
                        nc.scalar.activation(att_vs[:, g, :], proj1[:, i + (g * 24 + 16), :], ACT.Copy).then_inc(A["v_staged"], 1)

                    def exp(u):
                        act.wait_ge(A["max_ready"], i * 4 + (u + 1))
                        nc.scalar.activation(att_p[:, u % 2, :], att_s[:, u % 2, :], ACT.Exp, bias=att_max[:, u % 2, 4:5],
                                             scale=0.125, accum_out=att_den[:, u % 2:u % 2 + 1]).then_inc(A["p_ready"], 1)

                    exp(0)
                    for u in range(4):
                        e, it = u // 2, u % 2
                        if u < 3:
                            exp(u + 1)
                        act.wait_ge(A["p_turned"], i * 4 + (u + 1))
                        nc.scalar.activation(att_pt[:, u % 2, 512:768], PS[:, 4, S1:512], ACT.Copy).then_inc(A["pt_ready"], 1)
                        act.wait_ge(A["o_ready"], i * 4 + (u + 1))
                        act.wait_ge(A["den_ready"], i * 4 + (u + 1))
                        nc.scalar.activation(att_o[:, it, e * 64:(e + 1) * 64], PS[:, 3, u * 64:(u + 1) * 64], ACT.Copy,
                                             scale=att_rden[:, u % 2:u % 2 + 1]).then_inc(A["o_scaled"], 1)

            def mlstm():
                A = ab_sem
                act.wait_ge(A["log_in"], 1)
                step(nc.scalar.activation(r_l, r_e, ACT.Exp))
                nc.scalar.activation(r_l, r_l, ACT.Ln, bias=one[0:A_HEADS, :]).then_inc(A["log_ready"], 1)
                act.wait_ge(A["floor_in"], 1)
                nc.scalar.activation(r_en, r_sum, ACT.Exp, scale=-1.0).then_inc(A["floor_ready"], 1)
                for hd in range(A_HEADS):
                    for st, (_, tl) in enumerate(TILES2):
                        act.wait_ge(A["shifted"], 3 * hd + st + 1)
                        nc.scalar.activation(ab_w[0:tl, st, :], ab_t[0:tl, st, :], ACT.Exp, bias=ab_col[0:tl, st, hd:hd + 1],
                                             scale=-1.0).then_inc(A["w_ready"], 1)
                    act.wait_ge(A["num_ready"], hd + 1)
                    nc.scalar.activation(ab_den[:, 2 * (hd % 2), :], PS[:, 4, 0:S2], ACT.Abs).then_inc(A["den_abs"], 1)
                    act.wait_ge(A["h_ready"], hd + 1)
                    for c in range(2):
                        last = nc.scalar.activation(ab_sq[:, c, :], ab_hh[:, 2 * (hd % 2) + c, :], ACT.Square)
                    last.then_inc(A["squares_ready"], 1)
                    act.wait_ge(A["sum_ready"], hd + 1)
                    step(nc.scalar.activation(lnv[:, :], PS[:, 0, 0:S2], ACT.Ln, bias=rms_eps, scale=float(D) / A_DIM))
                    nc.scalar.activation(ab_r[:, hd % 2, :], lnv[:, :], ACT.Exp, scale=-0.5).then_inc(A["rstd_ready"], 1)

            def lru():
                L = lru_sem
                for c in range(DC):
                    act.wait_ge(L["gates_summed"], c + 1)
                    for gate, dst, bias in ((0, lru_r, "lru_b_r"), (1, lru_i, "lru_b_i")):
                        nc.scalar.activation(dst[:, c, :], PS[:, 2 * (c % 2) + gate, 0:S2], ACT.Sigmoid, bias=param(bias, c))\
                            .then_inc(L["gates_ready"], 1)
                act.wait_ge(L["loga_ready"], 1)
                nc.scalar.activation(lru_a[:, :, :], lru_r[:, :, :], ACT.Exp)
                nc.scalar.activation(lru_r[:, :, :], lru_r[:, :, :], ACT.Tanh, scale=-1.0).then_inc(L["a_ready"], 1)
                act.wait_ge(L["root_in"], 1)
                nc.scalar.activation(lru_r[:, :, :], lru_r[:, :, :], ACT.Sqrt, scale=2.0).then_inc(L["root_ready"], 1)
                act.wait_ge(L["gelu_in"], 1)
                nc.scalar.activation(lru_r[:, :, :], lru_r[:, :, :], ACT.Tanh, scale=math.sqrt(2.0 / math.pi))\
                    .then_inc(L["gelu_ready"], 1)

            def relu(phase):
                with act.Fori(0, phase.units // SLOTS) as i:
                    for s in range(SLOTS):
                        act.wait_ge(unit_multiplied, i * SLOTS + (phase.unit0 + s + 1))
                        act.wait_ge(relu_used, i * SLOTS + (MLP * (phase.name == "mlp_in1") + s + 1))
                        nc.scalar.activation(silu[:, s, :], PS[:, s, 0:S2], ACT.Relu).then_inc(out_evacuated, 1)

            def diff_attention():
                A = c_sem
                act.wait_ge(out_evacuated, evacuated(ph["c_in"]))
                with act.Fori(0, C_HEADS) as i:
                    nc.scalar.activation(c_vs, proj2[:, i + 16, :], ACT.Copy).then_inc(A["v_staged"], 1)
                    for u, (t0, tl) in enumerate(TILES2):
                        act.wait_ge(A["max_ready"], i * 3 + (u + 1))
                        for e in range(2):
                            last = nc.scalar.activation(c_p[0:tl, 2 * (u % 2) + e, 0:t0 + tl], c_s[0:tl, 2 * (u % 2) + e, 0:t0 + tl],
                                                        ACT.Exp, bias=c_max[0:tl, u % 2, 2 + e:3 + e], scale=0.125,
                                                        accum_out=c_den[0:tl, u % 2, e:e + 1])
                        last.then_inc(A["p_ready"], 1)
                    act.wait_ge(A["o_ready"], i + 1)
                    nc.scalar.activation(c_sq, PS[:, 2, 0:S2], ACT.Square).then_inc(A["squares_ready"], 1)
                    act.wait_ge(A["sum_ready"], i + 1)
                    nc.scalar.activation(c_ln, PS[:, 5, 0:S2], ACT.Ln, bias=rms_eps, scale=float(D) / P).then_inc(c_logged, 1)
                    act.wait_ge(c_logged, i + 1)
                    nc.scalar.activation(c_r, c_ln, ACT.Exp, scale=-0.5).then_inc(A["rstd_ready"], 1)

            act.sem_inc(out_evacuated, FREE_BANKS)
            act.wait_ge(consts_loaded, 48)
            act.wait_ge(x_loaded, 16)
            for layer in range(DEPTH):
                if layer:
                    act.wait_ge(x_ready, 2 * layer)
                norm(4 * layer, x, S1)
                if layer % 3 == 0:
                    j = layer // 3
                    if j == 0:
                        step(nc.scalar.activation(lg, param("decay", 0, 16), ACT.Exp))
                        nc.scalar.activation(lg, lg, ACT.Ln, bias=one, scale=-1.0).then_inc(ret_sem["lg_ready"], 1)
                    decay(j)
                    evacuate(ph[f"ret_qkv{layer}"], proj1, S1)
                    evacuate(ph[f"ret_g{layer}"], proj1[:, 32:48, :], S1, ACT.Silu)
                    retention(j)
                    last_phase = ph[f"ret_out{layer}"]
                    evacuate(last_phase, y, S1)
                elif layer % 3 == 1:
                    phase = ph["conv_in"]
                    with act.Fori(0, phase.units // SLOTS) as i:
                        for q in range(2):
                            act.wait_ge(unit_multiplied, i * SLOTS + (phase.unit0 + 2 * q + 1))
                            nc.scalar.activation(silu[:, q, 0:S1], PS[:, 2 * q, 0:S1], ACT.Sigmoid,
                                                 bias=param("conv_b_in", DC, DC)[:, bass.ds(i * 2 + q, 1)]).then_inc(gate_ready, 1)
                    conv()
                    last_phase = ph["conv_out"]
                    evacuate(last_phase, y, S1, ACT.Identity, bias="conv_b_out")
                else:
                    evacuate(ph["att_in"], proj1, S1)
                    attention()
                    last_phase = ph["att_out"]
                    evacuate(last_phase, y, S1)
                post_norm(4 * layer + 1, last_phase, S1)
                act.wait_ge(x_ready, 2 * layer + 1)
                norm(4 * layer + 2, x, S1)
                silu_pairs(ph[f"ffn_in{layer}"])
                evacuate(ph[f"ffn_out{layer}"], y, S1)
                post_norm(4 * layer + 3, ph[f"ffn_out{layer}"], S1)
            act.wait_ge(meta_loaded, 32)
            for layer in range(2):
                act.wait_ge(x_ready, 8 + 2 * layer)
                norm(16 + 2 * layer, h, S2)
                if layer == 0:
                    act.wait_ge(lru_sem["lam_ready"], 1)
                    nc.scalar.activation(lam_t[:, 1, :], lam_t[:, 0, :], ACT.Exp).then_inc(lru_sem["softplus_ready"], 1)
                    ab = ph["ab_in"]
                    evacuate(ab, proj2, S2, count=24)
                    evacuate(ab, proj2[:, 24:32, :], S2, ACT.Sigmoid, start=24, count=8)
                    evacuate(ab, proj2[:, 32:48, :], S2, start=32, count=16)
                    mlstm()
                    lru()
                    evacuate(ph["ab_out"], y, S2)
                else:
                    act.wait_ge(c_sem["lam_in"], 1)
                    nc.scalar.activation(lam_s[:, 2:4], lam_s[:, 0:2], ACT.Exp).then_inc(c_sem["lam_exp"], 1)
                    evacuate(ph["c_in"], proj2, S2)
                    diff_attention()
                    evacuate(ph["c_out"], y, S2)
                act.wait_ge(x_ready, 9 + 2 * layer)
                norm(17 + 2 * layer, h, S2)
                relu(ph[f"mlp_in{layer}"])
                evacuate(ph[f"mlp_out{layer}"], y, S2)
            act.wait_ge(x_ready, 12)
            norm(20, h, S2)

        @block.vector
        def _(dve):
            chain = [0]

            def step(ins):
                chain[0] += 1
                ins.then_inc(dve_chain, 1)
                dve.wait_ge(dve_chain, chain[0])

            stt = nc.vector.scalar_tensor_tensor

            def pre_norm(k, src, n, weight, col):
                dve.wait_ge(rstd_ready, k + 1)
                for c in range(DC):
                    last = stt(xn[:, c, 0:n], src[:, c, 0:n], param(weight, col + c), rstd[:, 0:n], ALU.mult, ALU.mult)
                last.then_inc(xn_ready, 1)

            def post_norm(k, dst, col):
                dve.wait_ge(rstd_ready, k + 1)
                for c in range(DC):
                    last = stt(y[:, c, 0:S1], y[:, c, 0:S1], param("norm_w", col + c), rstd[:, 0:S1], ALU.mult, ALU.mult)
                step(last)
                nc.vector.tensor_tensor(dst, x[:, :, :], y[:, :, 0:S1], ALU.add).then_inc(x_ready, 1)

            def add_to_h(phase):
                dve.wait_ge(out_evacuated, evacuated(phase))
                nc.vector.tensor_tensor(h[:, :, :], h[:, :, :], y[:, :, :], ALU.add).then_inc(x_ready, 1)

            def ffn_pairs(phase):
                with dve.Fori(0, phase.units // SLOTS) as i:
                    for q in range(2):
                        dve.wait_ge(unit_multiplied, i * SLOTS + (phase.unit0 + 2 * q + 2))
                        dve.wait_ge(gate_ready, i * 2 + (phase.pair0 + q + 1))
                        nc.vector.tensor_tensor(proj1[:, i * 2 + q, :], PS[:, 2 * q + 1, 0:S1], silu[:, q, 0:S1], ALU.mult)\
                            .then_inc(pair_done, 1)

            def exponents(j):
                after, before = const("after"), const("before")
                if j == 0:
                    dve.wait_ge(ret_sem["lg_ready"], 1)
                for hd in range(RET_HEADS):
                    fwd = lg[:, 8 * j + hd:8 * j + hd + 1]
                    bwd = lg[:, 8 * j + 4 + hd:8 * j + 5 + hd]
                    if hd >= 2:
                        dve.wait_ge(ret_sem["decay_ready"], 4 * j + hd - 1)
                    step(nc.vector.tensor_scalar(ret_exp[:, hd % 2, :], after, fwd, None, ALU.mult))
                    stt(ret_exp[:, hd % 2, :], before, bwd, ret_exp[:, hd % 2, :], ALU.mult, ALU.add)\
                        .then_inc(ret_sem["exponent_ready"], 1)

            def retention(j, layer):
                R = ret_sem
                qkv = ph[f"ret_qkv{layer}"]
                cos, sin = spread(const("ret_cos"), 4), spread(const("ret_sin"), 4)
                for w in range(2):
                    dve.wait_ge(out_evacuated, evacuated(qkv, 8 * w + 8))
                    halves = proj1[:, 8 * w:8 * w + 8, :].rearrange("p (hd two) t -> p hd two t", two=2)
                    x1, x2 = halves[:, :, 0, :], halves[:, :, 1, :]
                    prod = [ret_half[:, n, :].rearrange("p (hd t) -> p hd t", t=S1) for n in range(4)]
                    nc.vector.tensor_tensor(prod[0], x1, cos, ALU.mult)
                    nc.vector.tensor_tensor(prod[1], x2, sin, ALU.mult)
                    nc.vector.tensor_tensor(prod[2], x2, cos, ALU.mult)
                    step(nc.vector.tensor_tensor(prod[3], x1, sin, ALU.mult))
                    nc.vector.tensor_tensor(x1, prod[0], prod[1], ALU.subtract)
                    last = nc.vector.tensor_tensor(x2, prod[2], prod[3], ALU.add)
                    last.then_inc(R["roped"], 1)
                    dve.wait_ge(R["roped"], 2 * j + w + 1)
                for b in range(8):
                    dve.wait_ge(R["v_turned"], 8 * j + b + 1)
                    hd, kt = b // 2, b % 2
                    nc.vector.tensor_copy(ret_v[:, kt, hd * RET_V:(hd + 1) * RET_V], PS[:, 4 + b % 2, :]).then_inc(R["v_ready"], 1)
                dve.wait_ge(R["decay_ready"], 4 * j + 4)

                def decayed(hd):
                    dve.wait_ge(R["scores_ready"], 4 * j + hd + 1)
                    if hd >= 2:
                        dve.wait_ge(R["o_ready"], 4 * j + hd - 1)
                    stt(ret_p[:, hd % 2, :], PS[:, 4 + hd % 2, :], RET_QK ** -0.5, ret_decay[:, hd, :], ALU.mult, ALU.mult)\
                        .then_inc(R["p_ready"], 1)

                dve.wait_ge(out_evacuated, evacuated(ph[f"ret_g{layer}"]))
                decayed(0)
                for hd in range(RET_HEADS):
                    if hd + 1 < RET_HEADS:
                        decayed(hd + 1)
                    first = 6 if hd % 2 == 0 else 0
                    dve.wait_ge(R["rstd_ready"], 4 * j + hd + 1)
                    g = proj1[:, 32 + 4 * hd:36 + 4 * hd, :]
                    step(nc.vector.tensor_tensor(g, g, spread(rstd[:, 0:S1], 4), ALU.mult))
                    nc.vector.tensor_tensor(g, g, PS[:, first:first + 2, :].rearrange("p b (e t) -> p (b e) t", t=S1), ALU.mult)\
                        .then_inc(R["gated"], 1)

            def conv():
                C = conv_sem
                phase = ph["conv_in"]
                with dve.Fori(0, phase.units // SLOTS) as i:
                    for q in range(2):
                        dve.wait_ge(unit_multiplied, i * SLOTS + (phase.unit0 + 2 * q + 2))
                        dve.wait_ge(gate_ready, i * 2 + (phase.pair0 + q + 1))
                        stt(conv_u[:, i * 2 + q, :], PS[:, 2 * q + 1, 0:S1], param("conv_b_in", 0, DC)[:, bass.ds(i * 2 + q, 1)],
                            silu[:, q, 0:S1], ALU.add, ALU.mult).then_inc(pair_done, 1)
                dve.wait_ge(pair_done, pairs_done(phase))
                taps = [CONV_PAD] + [t for t in range(CONV_TAPS) if t != CONV_PAD]
                for t in taps:
                    for c in range(DC):
                        w = param("conv_w_dw", c * CONV_TAPS + t)
                        lo, hi = max(0, CONV_PAD - t), min(S1, S1 + CONV_PAD - t)
                        src = conv_u[:, c, lo + t - CONV_PAD:hi + t - CONV_PAD]
                        if t == CONV_PAD:
                            last = nc.vector.tensor_scalar(conv_acc[:, c, :], src, w, param("conv_b_dw", c), ALU.mult, ALU.add)
                        else:
                            last = stt(conv_acc[:, c, lo:hi], src, w, conv_acc[:, c, lo:hi], ALU.mult, ALU.add)
                    if t != taps[-1]:
                        step(last)
                last.then_inc(C["acc_ready"], 1)
                dve.wait_ge(C["mean_ready"], 1)
                nc.vector.tensor_tensor(conv_acc, conv_acc, spread(PS[:, 4, 0:S1], DC), ALU.subtract).then_inc(C["centered"], 1)
                dve.wait_ge(C["rstd_ready"], 1)
                nc.vector.tensor_tensor(conv_sq, conv_acc, spread(rstd[:, 0:S1], DC), ALU.mult).then_inc(C["scaled"], 1)

            def attention():
                A = att_sem
                mask = const("att_mask").rearrange("p (it g k) -> p it g k", it=2, g=3)
                dve.wait_ge(out_evacuated, evacuated(ph["att_in"]))
                cos, sin = rope_cos[:, 0:S1], rope_sin[:, 0:S1]
                dve.sem_inc(A["roped"], 3)
                with dve.Fori(0, DC) as i:
                    for g in range(3):
                        dve.wait_ge(A["rotated"], i * 3 + (g + 1))
                        nc.vector.tensor_tensor(att_t[:, 2 * g, :], PS[:, g, 0:S1], sin, ALU.mult)
                        nc.vector.tensor_tensor(att_t[:, 2 * g + 1, :], PS[:, g, S1:512], sin, ALU.mult)
                        nc.vector.tensor_tensor(att_q[:, g, :], proj1[:, i + g * 24, :], cos, ALU.mult)
                        nc.vector.tensor_tensor(att_k[:, g, :], proj1[:, i + (g * 24 + 8), :], cos, ALU.mult).then_inc(att_rot, 1)
                        dve.wait_ge(att_rot, i * 3 + (g + 1))
                        nc.vector.tensor_tensor(att_q[:, g, :], att_q[:, g, :], att_t[:, 2 * g, :], ALU.add)
                        nc.vector.tensor_tensor(att_k[:, g, :], att_k[:, g, :], att_t[:, 2 * g + 1, :], ALU.add).then_inc(A["roped"], 1)
                    dve.wait_ge(A["v_turned"], i + 1)
                    nc.vector.tensor_copy(att_vn[:, 0:4, :].rearrange("p a b -> p (a b)"), PS[:, 3, :])
                    nc.vector.tensor_copy(att_vn[:, 4:6, :].rearrange("p a b -> p (a b)"), PS[:, 4, 0:S1]).then_inc(A["v_ready"], 1)

                    def maxima(u):
                        it, m = u % 2, att_max[:, u % 2, :]
                        dve.wait_ge(A["scores_ready"], i * 4 + (u + 1))
                        dve.sem_inc(wait_taken, 1)
                        for g in range(3):
                            b = (5 if u % 2 == 0 else 0) + g // 2
                            last = nc.vector.tensor_tensor_reduce(
                                att_s[:, u % 2, g * S1:(g + 1) * S1], PS[:, b, (g % 2) * S1:(g % 2 + 1) * S1], mask[:, it, g, :],
                                1.0, -3e38, ALU.add, ALU.max, m[:, g:g + 1])
                        last.then_inc(att_m1, 1)
                        dve.wait_ge(att_m1, i * 4 + (u + 1))
                        nc.vector.tensor_reduce(m[:, 3:4], m[:, 0:3], AX, ALU.max).then_inc(att_m2, 1)
                        dve.wait_ge(att_m2, i * 4 + (u + 1))
                        nc.vector.tensor_scalar(m[:, 4:5], m[:, 3:4], -0.125, None, ALU.mult).then_inc(A["max_ready"], 1)

                    maxima(0)
                    for u in range(4):
                        if u < 3:
                            maxima(u + 1)
                        dve.wait_ge(A["p_ready"], i * 4 + (u + 1))
                        nc.vector.reciprocal(att_rden[:, u % 2:u % 2 + 1], att_den[:, u % 2:u % 2 + 1]).then_inc(A["den_ready"], 1)
                        dve.wait_ge(A["p_turned"], i * 4 + (u + 1))
                        nc.vector.tensor_copy(att_pt[:, u % 2, 0:512], PS[:, 7, :]).then_inc(A["pt_ready"], 1)
                    dve.wait_ge(out_evacuated, evacuated(ph["att_in"]))
                    dve.wait_ge(A["o_turned"], i + 1)
                    nc.vector.tensor_copy(proj1[:, i, :], PS[:, 6, S1:512]).then_inc(A["mixed"], 1)

            def mlstm_rows():
                A = ab_sem
                dve.wait_ge(A["gate_sums"], 1)
                bias_i, bias_f = (param("if_bias", n)[0:A_HEADS, :] for n in range(2))
                ones_row = spread(one[0:A_HEADS, :], 1)
                nc.vector.tensor_scalar(r_in, PS[0:A_HEADS, 5, 0:S2], bias_i, None, ALU.add)
                step(nc.vector.tensor_scalar(r_f, PS[0:A_HEADS, 6, 0:S2], bias_f, None, ALU.add))
                stt(r_e, r_f, -1.0, r_f, ALU.mult, ALU.min).then_inc(A["log_in"], 1)
                dve.wait_ge(A["log_ready"], 1)
                step(stt(r_lf, r_f, 0.0, r_l, ALU.min, ALU.subtract))
                step(nc.vector.memset(r_sum, 1.0))
                step(nc.vector.tensor_tensor_scan(r_F, r_sum, r_lf, 0.0, ALU.mult, ALU.add))
                step(nc.vector.tensor_tensor(r_a, r_in, r_F, ALU.subtract))
                step(nc.vector.tensor_tensor_scan(r_m, r_sum, r_a, 0.0, ALU.mult, ALU.max))
                nc.vector.tensor_tensor(r_sum, r_F, r_m, ALU.add).then_inc(A["floor_in"], 1)
                dve.wait_ge(A["floor_in"], 1)
                dve.sem_inc(A["rows_ready"], 1)

            def mlstm():
                A = ab_sem
                dve.wait_ge(A["turned"], 1)
                for st, (_, tl) in enumerate(TILES2):
                    last = nc.vector.tensor_copy(ab_col[0:tl, st, :], PS[0:tl, 7, st * 4:st * 4 + 4])
                last.then_inc(A["cols_ready"], 1)

            def mlstm_values():
                A = ab_sem
                for st, (_, tl) in enumerate(TILES2):
                    dve.wait_ge(A["v_turned"], st + 1)
                    nc.vector.tensor_copy(ab_v[0:tl, st, :], PS[0:tl, 2 * (st % 2):2 * (st % 2) + 2, :].rearrange("p b f -> p (b f)"))\
                        .then_inc(A["v_ready"], 1)

            def mlstm_heads():
                A = ab_sem
                dve.wait_ge(consts2_loaded, 48)
                causal = const("causal_T").rearrange("p (s t) -> p s t", s=3)
                for hd in range(A_HEADS):
                    dve.wait_ge(A["run_ready"], hd + 1)
                    if hd >= 1:
                        dve.wait_ge(A["w_ready"], 3 * hd)
                    for st, (_, tl) in enumerate(TILES2):
                        nc.vector.tensor_tensor(ab_t[0:tl, st, :], causal[0:tl, st, :], PS[0:tl, 0, 0:S2], ALU.add)\
                            .then_inc(A["shifted"], 1)
                    for st, (_, tl) in enumerate(TILES2):
                        dve.wait_ge(A["scores_ready"], 3 * hd + st + 1)
                        dve.wait_ge(A["w_ready"], 3 * hd + st + 1)
                        stt(ab_p[0:tl, 3 * (hd % 2) + st, :], PS[0:tl, 1 + st, 0:S2], A_DIM ** -0.5, ab_w[0:tl, st, :],
                            ALU.mult, ALU.mult).then_inc(A["p_ready"], 1)
                    den, rec = ab_den[:, 2 * (hd % 2), :], ab_den[:, 2 * (hd % 2) + 1, :]
                    dve.wait_ge(A["den_abs"], hd + 1)
                    step(nc.vector.tensor_tensor(den, den, PS[:, 7, 0:S2], ALU.max))
                    step(nc.vector.reciprocal(rec, den))
                    for c in range(2):
                        last = nc.vector.tensor_tensor(ab_hh[:, 2 * (hd % 2) + c, :], rec, PS[:, 5 + c, 0:S2], ALU.mult)
                    step(last)
                    hh = ab_hh[:, 2 * (hd % 2):2 * (hd % 2) + 2, :]
                    nc.vector.tensor_tensor(hh, hh, proj2[:, 24 + 2 * hd:26 + 2 * hd, :], ALU.mult).then_inc(A["h_ready"], 1)
                    dve.wait_ge(A["rstd_ready"], hd + 1)
                    for c in range(2):
                        last = stt(proj2[:, 2 * hd + c, :], ab_hh[:, 2 * (hd % 2) + c, :], param("mlstm_norm", 2 * hd + c),
                                   ab_r[:, hd % 2, :], ALU.mult, ALU.mult)
                    last.then_inc(A["mixed"], 1)

            def softplus():
                L = lru_sem
                lam = param("lru_lambda", 0, DC)
                neg, e, z, z2 = (lam_t[:, n, :] for n in range(4))
                stt(neg, lam, -1.0, lam, ALU.mult, ALU.min).then_inc(L["lam_ready"], 1)
                dve.wait_ge(L["softplus_ready"], 1)
                step(nc.vector.tensor_scalar(z, e, 2.0, None, ALU.add))
                step(nc.vector.reciprocal(z, z))
                step(nc.vector.tensor_tensor(z, z, e, ALU.mult))
                step(nc.vector.tensor_tensor(z2, z, z, ALU.mult))
                step(nc.vector.memset(e, 1.0 / 21))
                for n in range(19, 0, -2):
                    step(nc.vector.tensor_tensor(e, e, z2, ALU.mult))
                    step(nc.vector.tensor_scalar(e, e, 1.0 / n, None, ALU.add))
                step(nc.vector.tensor_tensor(e, e, z, ALU.mult))
                step(nc.vector.tensor_scalar(neg, lam, -1.0, 0.0, ALU.mult, ALU.max))
                step(stt(e, e, 2.0, neg, ALU.mult, ALU.add))
                step(nc.vector.tensor_scalar(lam8, e, -LRU_C, None, ALU.mult))

            def lru_conv():
                L = lru_sem
                dve.wait_ge(out_evacuated, evacuated(ph["ab_in"], 40))
                for t in range(LRU_TAPS - 1, -1, -1):
                    back = LRU_TAPS - 1 - t
                    for c in range(DC):
                        w = param("lru_conv_w", c * LRU_TAPS + t)
                        if back == 0:
                            last = nc.vector.tensor_scalar(lru_xc[:, c, :], lru_xb[:, c, :], w, param("lru_conv_b", c), ALU.mult, ALU.add)
                        else:
                            last = stt(lru_xc[:, c, back:S2], lru_xb[:, c, 0:S2 - back], w, lru_xc[:, c, back:S2], ALU.mult, ALU.add)
                    if t:
                        step(last)
                last.then_inc(L["conv_ready"], 1)

            def lru():
                L = lru_sem
                dve.wait_ge(L["gates_ready"], 2 * DC)
                for c in range(DC):
                    last = nc.vector.tensor_scalar(lru_r[:, c, :], lru_r[:, c, :], lam8[:, c:c + 1], None, ALU.mult)
                last.then_inc(L["loga_ready"], 1)
                step(nc.vector.tensor_tensor(lru_i[:, :, :], lru_i[:, :, :], lru_xc[:, :, :], ALU.mult))
                dve.wait_ge(L["a_ready"], 1)
                step(nc.vector.tensor_scalar(y[:, :, :], lru_r[:, :, :], 1.0, None, ALU.add))
                step(nc.vector.reciprocal(y[:, :, :], y[:, :, :]))
                nc.vector.tensor_tensor(lru_r[:, :, :], lru_r[:, :, :], y[:, :, :], ALU.mult).then_inc(L["root_in"], 1)
                dve.wait_ge(L["root_ready"], 1)
                step(nc.vector.tensor_tensor(lru_i[:, :, :], lru_i[:, :, :], lru_r[:, :, :], ALU.mult))
                for c in range(DC):
                    last = nc.vector.tensor_tensor_scan(y[:, c, :], lru_a[:, c, :], lru_i[:, c, :], 0.0, ALU.mult, ALU.add)
                step(last)
                step(nc.vector.tensor_tensor(lru_r[:, :, :], lru_gate, lru_gate, ALU.mult))
                step(nc.vector.tensor_scalar(lru_r[:, :, :], lru_r[:, :, :], 0.044715, 1.0, ALU.mult, ALU.add))
                nc.vector.tensor_tensor(lru_r[:, :, :], lru_r[:, :, :], lru_gate, ALU.mult).then_inc(L["gelu_in"], 1)
                dve.wait_ge(L["gelu_ready"], 1)
                for c in range(DC):
                    last = stt(lru_r[:, c, :], lru_r[:, c, :], 1.0, lru_gate[:, c, :], ALU.add, ALU.mult)
                step(last)
                for c in range(DC):
                    last = stt(lru_out[:, c, :], y[:, c, :], 0.5, lru_r[:, c, :], ALU.mult, ALU.mult)
                last.then_inc(L["done"], 1)

            def square_relu(layer):
                phase = ph[f"mlp_in{layer}"]
                with dve.Fori(0, phase.units // SLOTS) as i:
                    for s in range(SLOTS):
                        dve.wait_ge(out_evacuated, i * SLOTS + evacuated(phase, s + 1))
                        nc.vector.tensor_tensor(proj2[:, i * SLOTS + s, :], silu[:, s, :], silu[:, s, :], ALU.mult).then_inc(relu_used, 1)
                dve.wait_ge(relu_used, SLOTS + MLP * (layer + 1))
                dve.sem_inc(hidden_ready, MLP)

            def lambdas():
                A = c_sem
                for n in range(2):
                    last = nc.vector.tensor_tensor_reduce(lam_s[:, 8 + C_QK * n:8 + C_QK * (n + 1)], param("c_lambda", 2 * n * C_QK, C_QK),
                                                          param("c_lambda", (2 * n + 1) * C_QK, C_QK), 1.0, 0.0, ALU.mult, ALU.add,
                                                          lam_s[:, n:n + 1])
                last.then_inc(A["lam_in"], 1)
                nc.vector.tensor_scalar(subln, param("subln"), 1.0 - LAMBDA_INIT, None, ALU.mult)
                dve.wait_ge(A["lam_exp"], 1)
                step(nc.vector.tensor_tensor(lam_s[:, 4:5], lam_s[:, 3:4], lam_s[:, 2:3], ALU.subtract))
                step(nc.vector.tensor_scalar(neg_lam, lam_s[:, 4:5], -LAMBDA_INIT, None, ALU.add))

            def diff_attention():
                A = c_sem
                causal = const("causal").rearrange("p (s t) -> p s t", s=3)
                dve.wait_ge(out_evacuated, evacuated(ph["c_in"]))
                dve.sem_inc(A["roped"], 1)
                dve.sem_inc(A["mixed"], 1)
                with dve.Fori(0, C_HEADS) as i:
                    dve.wait_ge(A["rotated"], i + 1)
                    nc.vector.tensor_tensor(c_t[:, 0, :], PS[:, 0, 0:S2], rope_sin, ALU.mult)
                    nc.vector.tensor_tensor(c_t[:, 1, :], PS[:, 1, 0:S2], rope_sin, ALU.mult)
                    nc.vector.tensor_tensor(c_q, proj2[:, i, :], rope_cos, ALU.mult)
                    nc.vector.tensor_tensor(c_k, proj2[:, i + 8, :], rope_cos, ALU.mult).then_inc(c_rot, 1)
                    dve.wait_ge(c_rot, i + 1)
                    nc.vector.tensor_tensor(c_q, c_q, c_t[:, 0, :], ALU.add)
                    nc.vector.tensor_tensor(c_k, c_k, c_t[:, 1, :], ALU.add).then_inc(A["roped"], 1)
                    dve.wait_ge(A["v_turned"], i + 1)
                    nc.vector.tensor_copy(c_vn[:, 0:2, :].rearrange("p a b -> p (a b)"), PS[:, 2, 0:2 * P])
                    nc.vector.tensor_copy(c_vn[0:META, 2, :], PS[0:META, 2, 2 * P:3 * P]).then_inc(A["v_ready"], 1)

                    def maxima(u):
                        t0, tl = TILES2[u]
                        m = c_max[0:tl, u % 2, :]
                        dve.wait_ge(A["scores_ready"], i * 3 + (u + 1))
                        dve.sem_inc(wait_taken, 1)
                        for e in range(2):
                            last = nc.vector.tensor_tensor_reduce(
                                c_s[0:tl, 2 * (u % 2) + e, 0:t0 + tl], PS[0:tl, 3 + 2 * (u % 2) + e, 0:t0 + tl],
                                causal[0:tl, u, 0:t0 + tl], 1.0, -3e38, ALU.add, ALU.max, m[:, e:e + 1])
                        last.then_inc(c_m1, 1)
                        dve.wait_ge(c_m1, i * 3 + (u + 1))
                        nc.vector.tensor_scalar(m[:, 2:4], m[:, 0:2], -0.125, None, ALU.mult).then_inc(A["max_ready"], 1)

                    maxima(0)
                    for u, (t0, tl) in enumerate(TILES2):
                        if u < 2:
                            maxima(u + 1)
                        n = t0 + tl
                        den = c_den[0:tl, u % 2, :]
                        p0, p1 = c_p[0:tl, 2 * (u % 2), 0:n], c_p[0:tl, 2 * (u % 2) + 1, 0:n]
                        dve.wait_ge(A["p_ready"], i * 3 + (u + 1))
                        nc.vector.reciprocal(den, den).then_inc(c_d1, 1)
                        dve.wait_ge(c_d1, i * 3 + (u + 1))
                        nc.vector.tensor_scalar(p1, p1, den[:, 1:2], neg_lam[0:tl, :], ALU.mult, ALU.mult).then_inc(c_d2, 1)
                        dve.wait_ge(c_d2, i * 3 + (u + 1))
                        stt(c_pd[0:tl, u % 2, 0:n], p0, den[:, 0:1], p1, ALU.mult, ALU.add).then_inc(A["pd_ready"], 1)
                    dve.wait_ge(A["p_turned"], i * 3 + 3)
                    for st, (s0, sl) in enumerate(TILES2):
                        last = nc.vector.tensor_copy(c_pt[0:sl, st, s0:S2], PS[0:sl, (7, 0, 1)[st], s0:S2])
                    last.then_inc(A["pt_ready"], 1)
                    dve.wait_ge(A["rstd_ready"], i + 1)
                    stt(proj2[:, i, :], PS[:, 2, 0:S2], subln, c_r, ALU.mult, ALU.mult).then_inc(A["mixed"], 1)

            dve.sem_inc(pair_done, FREE_PAIRS)
            dve.sem_inc(relu_used, SLOTS)
            dve.wait_ge(consts_loaded, 48)
            dve.wait_ge(x_loaded, 16)
            for layer in range(DEPTH):
                pre_norm(4 * layer, x, S1, "norm_w", (4 * layer) * DC)
                if layer % 3 == 0:
                    exponents(layer // 3)
                    retention(layer // 3, layer)
                elif layer % 3 == 1:
                    conv()
                else:
                    attention()
                post_norm(4 * layer + 1, x[:, :, :], (4 * layer + 1) * DC)
                pre_norm(4 * layer + 2, x, S1, "norm_w", (4 * layer + 2) * DC)
                ffn_pairs(ph[f"ffn_in{layer}"])
                post_norm(4 * layer + 3, x[:, :, :] if layer < DEPTH - 1 else h[:, :, META:S2], (4 * layer + 3) * DC)
            pre_norm(16, h, S2, "norm_mix", 0)
            softplus()
            mlstm_rows()
            lru_conv_after = ph["ab_in"]
            mlstm_values()
            mlstm()
            lru_conv()
            mlstm_heads()
            lru()
            add_to_h(ph["ab_out"])
            pre_norm(17, h, S2, "norm_mlp", 0)
            square_relu(0)
            add_to_h(ph["mlp_out0"])
            pre_norm(18, h, S2, "norm_mix", DC)
            lambdas()
            diff_attention()
            add_to_h(ph["c_out"])
            pre_norm(19, h, S2, "norm_mlp", DC)
            square_relu(1)
            add_to_h(ph["mlp_out1"])
            pre_norm(20, h, S2, "norm_final", 0)



def kernel(**inputs):
    import concourse.bacc as bacc
    from concourse.bass_utils import run_bass_kernel_spmd as run

    a = {k: np.asarray(v) for k, v in inputs.items()}

    def features(v):
        return v.reshape(-1, P).T

    def units(w, halves=1):
        k, m = w.shape
        t = k // P // halves
        return np.ascontiguousarray(w.reshape(halves, t, P, m // P, P).transpose(3, 0, 2, 1, 4).reshape(m // P * halves, P, t * P))

    def interleaved(w):
        u = units(w)
        n = u.shape[0] // 2
        return np.ascontiguousarray(np.stack([u[:n], u[n:]], 1).reshape(u.shape))

    (const_a, at_a), (const_b, at_b), (const_c, at_c) = constants()
    arrays = {"const_a": const_a, "const_b": const_b, "const_c": const_c}
    arrays["x"] = np.ascontiguousarray(a["x"][0].T.reshape(DC, P, S1).transpose(1, 0, 2))
    arrays["meta"] = np.ascontiguousarray(a["meta_tokens_2"].T.reshape(DC, P, META).transpose(1, 0, 2))
    for layer in range(DEPTH):
        j = layer // 3
        if layer % 3 == 0:
            u = units(a["ret_w_in"][j])
            arrays[f"ret_qkv{layer}"] = np.ascontiguousarray(u[:32])
            arrays[f"ret_g{layer}"] = np.ascontiguousarray(u[32:])
            arrays[f"ret_out{layer}"] = units(a["ret_w_out"][j], 2)
        elif layer % 3 == 1:
            w = a["conv_w_in"][0]
            arrays["conv_in"] = interleaved(np.concatenate([w[:, D:], w[:, :D]], 1))
            arrays["conv_out"] = units(a["conv_w_out"][0])
        else:
            arrays["att_in"] = units(a["attn_w_in"][0])
            arrays["att_out"] = units(a["attn_w_out"][0])
        arrays[f"ffn_in{layer}"] = interleaved(a["ffn_w_in"][layer])
        arrays[f"ffn_out{layer}"] = units(a["ffn_w_out"][layer], 2)
    w = a["ab_w_in_2"][0]
    g0 = 4 * D
    arrays["ab_in"] = units(np.concatenate([w[:, :g0], w[:, g0 + 2 * A_HEADS:]], 1))
    arrays["ab_gates"] = np.ascontiguousarray(w[:, g0:g0 + 2 * A_HEADS].reshape(DC, P, 2 * A_HEADS).transpose(1, 0, 2))
    arrays["ab_out"] = units(a["ab_w_out_2"][0], 2)
    arrays["c_in"] = units(a["c_w_in_2"][0])
    arrays["c_out"] = units(a["c_w_out_2"][0])
    for layer in range(2):
        arrays[f"mlp_in{layer}"] = units(a["mlp_w1_2"][layer])
        arrays[f"mlp_out{layer}"] = units(a["mlp_w2_2"][layer], 4)
    arrays["lru_w_r"] = np.ascontiguousarray(a["lru_w_r_2"][0].transpose(1, 0, 2))
    arrays["lru_w_i"] = np.ascontiguousarray(a["lru_w_i_2"][0].transpose(1, 0, 2))

    taps = lambda w, n: w.reshape(n, DC, P).transpose(2, 1, 0).reshape(P, DC * n)
    if_bias = np.zeros((P, 2), np.float32)
    if_bias[:A_HEADS] = a["ab_if_bias_2"][0].reshape(2, A_HEADS).T
    cols = {
        "norm_w": features(a["norm_w"].reshape(-1)), "conv_b_in": features(a["conv_b_in"][0]),
        "conv_w_dw": taps(a["conv_w_dw"][0], CONV_TAPS), "conv_b_dw": features(a["conv_b_dw"][0]),
        "conv_ln_g": features(a["conv_ln_g"][0]), "conv_ln_b": features(a["conv_ln_b"][0]),
        "conv_b_out": features(a["conv_b_out"][0]), "norm_mix": features(a["norm_mix_2"].reshape(-1)),
        "norm_mlp": features(a["norm_mlp_2"].reshape(-1)), "norm_final": features(a["norm_final_2"]),
        "mlstm_norm": features(a["mlstm_norm_2"][0]), "lru_conv_w": taps(a["lru_conv_w_2"][0], LRU_TAPS),
        "lru_conv_b": features(a["lru_conv_b_2"][0]), "lru_b_r": features(a["lru_b_r_2"][0]),
        "lru_b_i": features(a["lru_b_i_2"][0]), "lru_lambda": features(a["lru_lambda_2"][0]),
        "subln": features(a["c_subln_2"][0]),
        "decay": np.broadcast_to(a["ret_log1m_decay"].reshape(1, -1), (P, 16)), "if_bias": if_bias,
        "c_lambda": np.broadcast_to(a["c_lambda_2"][0].reshape(1, -1), (P, 4 * C_QK)),
    }
    assert all(cols[name].shape[1] == n for name, n in PARAMS)
    arrays["params"] = np.ascontiguousarray(np.concatenate([cols[name] for name, _ in PARAMS], 1))

    nc = bacc.Bacc("TRN2", target_bir_lowering=False, num_devices=1)
    dram = {k: nc.dram_tensor("in_" + k, v.shape, F32, kind="ExternalInput").ap() for k, v in arrays.items()}
    out = nc.dram_tensor("out", [P, DC, S1], F32, kind="ExternalOutput").ap()
    build(nc, dram, out, (at_a, at_b, at_c))
    got = run(nc, [{"in_" + k: v for k, v in arrays.items()}], core_ids=[0]).results[0]["out"]
    return np.ascontiguousarray(np.asarray(got).transpose(2, 1, 0).reshape(1, S1, D))
```

```python
from contextlib import ExitStack
import math

import concourse.bass as bass
from concourse import mybir
import numpy as np

F32 = mybir.dt.float32
F32R = mybir.dt.float32r
ALU = mybir.AluOpType
ACT = mybir.ActivationFunctionType
AX = mybir.AxisListType.X

P = 128
D = 1024
DC = D // P
S1 = 256
META = 16
S2 = S1 + META
DEPTH = 4
RMS_EPS, LN_EPS = 1e-6, 1e-5

RET_HEADS, RET_QK, RET_V = 4, 256, 512
RET_IN = 2 * RET_HEADS * (RET_QK + RET_V) // P
FFN = 2816 // P
CONV_TAPS, CONV_PAD = 31, 15
GROUPS = ((128, 1), (512, 4), (2048, 16))
ATT_IN = 3 * 3 * DC
A_HEADS, A_DIM = 4, 256
AB_IN = 6 * DC
LRU_TAPS, LRU_C = 4, 8.0
C_HEADS, C_QK = 8, 64
C_IN = 3 * DC
MLP = 32
LAMBDA_INIT = 0.8 - 0.6 * math.exp(-0.3)
ROPE_THETA, RET_BASE = 500000.0, 10000.0
BIG = 1e30
TILES2 = ((0, 128), (128, 128), (256, 16))
SLOTS = 4
SUB = 4
SUBS = 4
SLOT_TILES = 11


class Phase:

    def __init__(self, name, units, tiles=8, upo=1, pairs=False):
        self.name, self.units, self.tiles, self.upo, self.pairs = name, units, tiles, upo, pairs
        self.outs = units // upo
        self.body = max(SLOTS, 2 * upo)
        self.sps = -(-tiles // SUB)


def plan():
    seq = []
    for layer in range(DEPTH):
        if layer % 3 == 0:
            seq += [Phase(f"ret_qk{layer}", 16), Phase(f"ret_v{layer}", 16), Phase(f"ret_g{layer}", 16), Phase(f"ret_out{layer}", 16, 8, 2)]
        elif layer % 3 == 1:
            seq += [Phase("conv_in", 16, pairs=True), Phase("conv_out", 8)]
        else:
            seq += [Phase("att_in0", ATT_IN // 2), Phase("att_in1", ATT_IN // 2), Phase("att_out", 8)]
        seq += [Phase(f"ffn_in{layer}", 2 * FFN, pairs=True), Phase(f"ffn_out{layer}", 16, FFN // 2, 2)]
    seq += [Phase("ab_qkv", 3 * DC), Phase("ab_o", DC), Phase("ab_x", 2 * DC), Phase("ab_out", 16, 8, 2)]
    seq += [Phase("mlp_in0", MLP), Phase("mlp_out0", MLP, 8, 4)]
    seq += [Phase("c_in", C_IN), Phase("c_out", 8)]
    seq += [Phase("mlp_in1", MLP), Phase("mlp_out1", MLP, 8, 4)]
    unit = out = pair = sub = 0
    for ph, after in zip(seq, seq[1:] + [None]):
        ph.unit0, ph.out0, ph.pair0, ph.sub0, ph.after = unit, out, pair, sub, after
        unit += ph.units
        sub += ph.units * ph.sps
        if ph.pairs:
            pair += ph.units // 2
        else:
            out += ph.outs
    return seq



def constants():
    p = np.arange(P)
    first, second = {}, {}
    first["ident"] = np.eye(P)
    first["mean"] = np.full((P, P), 1.0 / D)
    first["ones"] = np.ones((P, P))
    swap = np.zeros((P, P))
    half = 8
    for base in (0, 64):
        for i in range(half):
            swap[base + half + i, base + i] = -1.0
            swap[base + i, base + half + i] = 1.0
    first["swap"] = swap
    inv = (np.float32(1.0) / np.float32(RET_BASE) ** np.linspace(0.0, 1.0, RET_QK // 2, dtype=np.float32)).astype(np.float32)
    ang = (np.arange(S1, dtype=np.float32)[None, :] * inv[:, None]).astype(np.float32).astype(np.float64)
    first["ret_cos"], first["ret_sin"] = np.cos(ang), np.sin(ang)
    inv = (np.float32(ROPE_THETA) ** (-np.arange(0, 16, 2, dtype=np.float32) / np.float32(16))).astype(np.float32)
    ang = (np.arange(S2, dtype=np.float32)[None, :] * inv[:, None]).astype(np.float32).astype(np.float64)
    cos, sin = np.ones((P, S2)), np.zeros((P, S2))
    for base in (0, 64):
        for i in range(16):
            cos[base + i], sin[base + i] = np.cos(ang[i % 8]), np.sin(ang[i % 8])
    first["rope_cos"], first["rope_sin"] = cos, sin
    first["rms_eps"], first["ln_eps"] = np.full((P, 1), RMS_EPS), np.full((P, 1), LN_EPS)
    first["one"] = np.ones((P, 1))
    n = np.arange(S1)
    m = np.arange(2)[:, None] * P + p[None, :]
    gap = n[None, None, :] - m[:, :, None]
    first_b = {}
    first_b["after"] = np.concatenate([np.maximum(gap[t], 0) for t in range(2)], 1)
    first_b["before"] = np.concatenate([np.maximum(-gap[t], 0) for t in range(2)], 1)
    masks = []
    for it in range(2):
        q = it * P + p[:, None]
        k = np.arange(S1)[None, :]
        for window, dil in GROUPS[:1] if it else GROUPS:
            radius = window // (2 * dil)
            live = ((q - k) % dil == 0) & (np.abs(q // dil - k // dil) <= radius)
            masks.append(np.where(live, 0.0, -BIG))
            assert dil == 1 or (live == ((q - k) % dil == 0)).all()
    first_b["att_mask"] = np.concatenate(masks, 1)
    pos = np.arange(S2)[None, :]
    row = [t0 + p[:, None] for t0, _ in TILES2]
    second["causal_T"] = np.concatenate([np.where(r > pos, BIG, 0.0) for r in row], 1)
    second["causal"] = np.concatenate([np.where(pos > r, -BIG, 0.0) for r in row], 1)
    sel = np.zeros((P, A_HEADS * P))
    for h in range(A_HEADS):
        sel[h, h * P:(h + 1) * P] = 1.0
    second["sel"] = sel

    def packed(parts):
        where, at = {}, 0
        for name, a in parts.items():
            where[name] = (at, a.shape[1])
            at += a.shape[1]
        return np.ascontiguousarray(np.concatenate(list(parts.values()), 1), dtype=np.float32), where

    return packed(first), packed(first_b), packed(second)


PARAMS = (
    ("norm_w", DEPTH * 4 * DC), ("conv_b_in", 2 * DC), ("conv_w_dw", DC * CONV_TAPS), ("conv_b_dw", DC),
    ("conv_ln_g", DC), ("conv_ln_b", DC), ("conv_b_out", DC), ("norm_mix", 2 * DC), ("norm_mlp", 2 * DC),
    ("norm_final", DC), ("mlstm_norm", DC), ("lru_conv_w", DC * LRU_TAPS), ("lru_conv_b", DC), ("lru_b_r", DC),
    ("lru_b_i", DC), ("lru_lambda", DC), ("subln", 1), ("decay", 2 * 2 * RET_HEADS), ("if_bias", 2),
    ("c_lambda", 4 * C_QK),
)
PARAM_AT = {}
_at = 0
for _name, _n in PARAMS:
    PARAM_AT[_name] = _at
    _at += _n
N_PARAMS = _at


def build(nc, dram, out, const_at):
    at_a, at_b, at_c = const_at
    phases = plan()
    ph = {x.name: x for x in phases}
    with ExitStack() as ctx:
        def sb(name, shape):
            return ctx.enter_context(nc.sbuf_tensor(name, shape, F32))

        def sbr(name, shape):
            return ctx.enter_context(nc.sbuf_tensor(name, shape, F32R))

        def sem(name):
            return ctx.enter_context(nc.semaphore(name))

        raw = [sb(f"weights{s}", [P, SLOT_TILES, P]) for s in range(SLOTS)]
        w_hi = [sbr(f"weights_hi{s}", [P, SUB, P]) for s in range(SUBS)]
        w_lo = [sbr(f"weights_lo{s}", [P, SUB, P]) for s in range(SUBS)]
        h = sb("h", [P, DC, S2])
        x = h[:, :, META:S2]
        xh = sbr("xn_hi", [P, DC, S2])
        xl = sbr("xn_lo", [P, DC, S2])
        xt = sb("xn", [P, 4, S2])
        y = sb("y", [P, DC, S2])
        sq = sb("sq", [P, 4, S2])
        ssum = sb("sum_of_squares", [P, S2])
        ca = sb("const_a", [P, sum(n for _, n in at_a.values())])
        n_b = max(sum(n for _, n in at_b.values()), sum(n for _, n in at_c.values()))
        cb = sb("const_b", [P, n_b])
        par = sb("params", [P, N_PARAMS])
        w_gates = sb("w_gates", [P, DC, 2 * A_HEADS])
        gates_hi = sbr("w_gates_hi", [P, DC, 2 * A_HEADS])
        gates_lo = sbr("w_gates_lo", [P, DC, 2 * A_HEADS])
        rstd = sb("rstd", [P, S2])
        lnv = sb("lnv", [P, S2])
        silu = sb("silu", [P, 2, S2])
        small = sb("small", [P, 64])
        lam_t = sb("lam_parts", [P, 4, DC])
        arena_at = -(-nc.sbuf_base // 64) * 64
        N_ARENA = 26400
        arena = nc.alloc_sbuf_tensor_at("arena", [P, N_ARENA], F32, offset=arena_at)
        arena_r = nc.alloc_sbuf_tensor_at("arena_r", [P, N_ARENA], F32R, offset=arena_at)
        PS = ctx.enter_context(nc.psum_tensor("acc", [P, 8, 512], F32))

        def chunks(buf, at, n, t):
            return buf[:, at:at + n * t].rearrange("p (c t) -> p c t", t=t)

        proj1 = chunks(arena, 0, 48, S1)
        proj1_r = chunks(arena_r, 0, 48, S1)
        proj2 = chunks(arena, 0, AB_IN, S2)
        proj2_r = chunks(arena_r, 0, AB_IN, S2)
        w_r = chunks(arena, 24288, DC, P)
        w_i = chunks(arena, 24288 + D, DC, P)
        hid_hi, hid_lo = chunks(arena_r, 0, FFN, S1), chunks(arena_r, FFN * S1, FFN, S1)
        mlp_hi, mlp_lo = chunks(arena_r, 0, MLP, S2), chunks(arena_r, MLP * S2, MLP, S2)
        part = chunks(arena, 25344, 2, S2)

        def const(name):
            for buf, at in ((ca, at_a), (cb, at_b), (cb, at_c)):
                if name in at:
                    return buf[:, at[name][0]:at[name][0] + at[name][1]]
            raise KeyError(name)

        def param(name, c=0, n=1):
            return par[:, PARAM_AT[name] + c:PARAM_AT[name] + c + n]

        ident, mean, ones, swap = const("ident"), const("mean"), const("ones"), const("swap")
        rope_cos, rope_sin = const("rope_cos"), const("rope_sin")
        rms_eps, ln_eps, one = const("rms_eps"), const("ln_eps"), const("one")

        x_loaded = sem("x_loaded")
        consts_loaded = sem("consts_loaded")
        consts2_loaded = sem("consts2_loaded")
        meta_loaded = sem("meta_loaded")
        weights_loaded = [sem(f"weights{s}_loaded") for s in range(SLOTS)]
        hi_ready = sem("hi_ready")
        split_ready = sem("split_ready")
        sub_multiplied = sem("sub_multiplied")
        square_summed = sem("square_summed")
        y_added = sem("y_added")
        y_squared = sem("y_squared")
        xt_ready, xh_ready, x_split = sem("xt_ready"), sem("xh_ready"), sem("x_split")
        part_ready, part_hi, part_lo = sem("part_ready"), sem("part_hi"), sem("part_lo")
        scaled = sem("post_scaled")
        sum_cleared = sem("sum_cleared")
        out_evacuated = sem("out_evacuated")
        gate_ready = sem("gate_ready")
        pair_done = sem("pair_done")
        squares_ready = sem("squares_ready")
        sum_ready = sem("sum_ready")
        rstd_ready = sem("rstd_ready")
        x_ready = sem("x_ready")
        act_chain = sem("act_chain")
        dve_chain = sem("dve_chain")
        final_ready = sem("final_ready")
        out_stored = sem("out_stored")
        wait_taken = sem("wait_taken")
        c_logged, c_rot, c_m1, c_d1, c_d2 = (sem("c_" + n) for n in ("logged", "rotation_parts", "maxima", "den_inverse", "scaled"))
        att_rot, att_m1, att_m2 = (sem("att_" + n) for n in ("rotation_parts", "maxima", "maximum"))

        FREE_BANKS, FREE_PAIRS, FREE_SUBS = 4, 2, 4

        def multiplied(phase, units):
            return units * phase.sps + (FREE_SUBS + phase.sub0)

        def evacuated(phase, n=None):
            return FREE_BANKS + phase.out0 + (phase.outs if n is None else n)

        def pairs_done(phase):
            return FREE_PAIRS + phase.pair0 + phase.units // 2

        def region(buf, at, *shape):
            n = int(np.prod(shape))
            v = buf[:, at:at + n]
            if len(shape) == 2:
                v = v.rearrange("p (a b) -> p a b", a=shape[0])
            return v

        def spread(row, n):
            return row.unsqueeze(1).to_broadcast((row.shape[0], n, row.shape[1]))

        ret_v = region(arena, 48 * S1, 2, 2048)
        ret_half = region(arena, 48 * S1, 4, 1024)
        ret_decay = region(arena, 64 * S1, RET_HEADS, 512)
        ret_p = region(arena, 72 * S1, 2, 512)
        ret_exp = region(arena, 72 * S1, 2, 512)
        ret_sq = region(arena, 76 * S1, 4, S1)
        ret_o = region(arena, 80 * S1, 4, S1)
        ret_hi = [proj1_r[:, 32 + n, :] for n in range(16)]
        ret_lo = [proj1_r[:, (2 * (n // 4) + n % 2) + (8 if n % 4 >= 2 else 0), :] for n in range(16)]
        lg = small[:, 0:16]
        conv_u, conv_acc, conv_sq, conv_mix = (proj1[:, n * DC:(n + 1) * DC, :] for n in range(4))
        conv_hi, conv_lo = proj1_r[:, 4 * DC:5 * DC, :], proj1_r[:, 5 * DC:6 * DC, :]
        att_raw = arena[:, 36 * S1:]
        att_q = region(att_raw, 0, 3, S1)
        att_k = region(att_raw, 768, 3, S1)
        att_vs = region(att_raw, 1536, 3, S1)
        att_vn = region(att_raw, 2304, 6, P)
        att_s = region(att_raw, 3072, 2, 768)
        att_p = region(att_raw, 4608, 2, 768)
        att_pt = region(att_raw, 6144, 2, 768)
        att_o = region(att_raw, 7680, 2, P)
        att_t = region(att_raw, 7936, 6, S1)
        att_x = att_raw[:, 9472:9472 + S1]
        att_hi, att_lo = chunks(arena_r, 36 * S1 + 9728, DC, S1), chunks(arena_r, 36 * S1 + 9728 + DC * S1, DC, S1)
        att_max = small[:, 16:26].rearrange("p (u k) -> p u k", u=2)
        att_den = small[:, 26:28]
        att_rden = small[:, 28:30]
        ab_v = region(arena, AB_IN * S2, 3, D)
        ab_raw = arena[:, AB_IN * S2 + 3 * D:24288]
        ab_row = region(ab_raw, 0, 10, S2)
        r_in, r_f, r_e, r_l, r_lf, r_F, r_a, r_m, r_en, r_sum = (ab_row[0:A_HEADS, i, :] for i in range(10))
        ab_t = region(ab_raw, 10 * S2, 3, S2)
        ab_w = region(ab_raw, 13 * S2, 3, S2)
        ab_p = region(ab_raw, 16 * S2, 6, S2)
        ab_den = region(ab_raw, 22 * S2, 2, S2)
        ab_hh = region(ab_raw, 24 * S2, 2, S2)
        ab_sq = region(ab_raw, 26 * S2, 2, S2)
        ab_r = region(ab_raw, 28 * S2, 2, S2)
        ab_col = small[:, 32:44].rearrange("p (t n) -> p t n", t=3)
        lru_xb, lru_gate = proj2[:, 32:40, :], proj2[:, 40:48, :]
        lru_xc, lru_i = y, proj2[:, 32:40, :]
        lru_a, lru_r = chunks(arena, AB_IN * S2 + 3 * D, DC, S2), chunks(arena, AB_IN * S2 + 3 * D + DC * S2, DC, S2)
        lru_o = chunks(arena, AB_IN * S2, DC, S2)
        ab_hi = [proj2_r[:, n, :] for n in range(8)] + [proj2_r[:, 32 + n, :] for n in range(8)]
        ab_lo = [proj2_r[:, 8 + n, :] for n in range(8)] + [proj2_r[:, 40 + n, :] for n in range(8)]
        lam8 = small[:, 44:52]
        c_raw = arena[:, C_IN * S2:]
        c_q, c_k, c_vs = c_raw[:, 0:S2], c_raw[:, S2:2 * S2], c_raw[:, 2 * S2:3 * S2]
        c_t = region(c_raw, 3 * S2, 2, S2)
        c_vn = region(c_raw, 5 * S2, 3, P)
        c_s = region(c_raw, 7 * S2, 4, S2)
        c_p = region(c_raw, 11 * S2, 4, S2)
        c_pd = region(c_raw, 15 * S2, 2, S2)
        c_pt = region(c_raw, 17 * S2, 3, S2)
        c_sq, c_ln, c_r, c_o = (c_raw[:, n * S2:(n + 1) * S2] for n in range(20, 24))
        c_hi, c_lo = chunks(arena_r, 48 * S2, DC, S2), chunks(arena_r, 56 * S2, DC, S2)
        c_max = small[:, 52:60].rearrange("p (u k) -> p u k", u=2)
        c_den = small[:, 60:64].rearrange("p (u k) -> p u k", u=2)
        lam_s = chunks(arena, 64 * S2, 1, 2 * C_QK + 8)[:, 0, :]
        neg_lam = small[:, 30:31]
        subln = small[:, 31:32]

        def sems(prefix, names):
            return {n: sem(prefix + n) for n in names.split()}

        ret_sem = sems("ret_", "v_turned v_ready lg_in lg_ready exponent_ready decay_ready half_rotated roped scores_ready p_ready "
                               "o_ready squares_ready sum_ready rstd_ready gated split")
        conv_sem = sems("conv_", "acc_ready mean_ready centered squares_ready var_ready rstd_ready scaled mixed split")
        att_sem = sems("att_", "rotated roped v_staged v_turned v_ready scores_ready max_ready p_ready den_ready "
                               "p_turned pt_ready o_ready o_scaled o_turned mixed")
        ab_sem = sems("ab_", "gate_sums log_in log_ready rows_ready floor_in floor_ready turned cols_ready v_turned "
                             "v_ready run_ready shifted w_ready scores_ready p_ready num_ready floor_spread den_abs h_ready "
                             "squares_ready sum_ready rstd_ready mixed")
        lru_sem = sems("lru_", "lam_ready softplus_ready conv_ready gates_summed gates_ready loga_ready a_ready root_in "
                               "root_ready gelu_in gelu_ready done")
        gates_split = sem("gate_weights_split")
        att_rounded, c_scaled, c_rounded = sem("att_rounded"), sem("c_output_scaled"), sem("c_output_rounded")
        c_sem = sems("c_", "lam_in lam_exp rotated roped v_staged v_turned v_ready scores_ready max_ready p_ready "
                           "pd_ready p_turned pt_ready o_ready squares_ready sum_ready rstd_ready mixed")

        FREE_SQUARES = 4
        hidden0 = {f"ffn_in{n}": FFN * n for n in range(DEPTH)}
        hidden0.update({f"mlp_in{n}": DEPTH * FFN + MLP * n for n in range(2)})

        def post_index(k):
            return k // 2 if k < 16 else k - 9

        block = ctx.enter_context(nc.Block())

        @block.sync
        def _(sp):
            sp.dma_start(x[:, :, :], dram["x"]).then_inc(x_loaded, 16)
            sp.dma_start(ca[:, :], dram["const_a"]).then_inc(consts_loaded, 16)
            sp.dma_start(par[:, :], dram["params"]).then_inc(consts_loaded, 16)

            def load(phase, slot, unit):
                n = phase.tiles * P
                sp.dma_start(raw[slot][:, 0:phase.tiles, :].rearrange("p k f -> p (k f)"),
                             dram[phase.name][unit, :, 0:n]).then_inc(weights_loaded[slot], 16)

            before = None
            for phase in phases:
                for s in range(SLOTS):
                    if before:
                        sp.wait_ge(split_ready, before.sub0 + (before.units - SLOTS + s + 1) * before.sps)
                    load(phase, s, s)
                if before is None:
                    sp.dma_start(cb[:, 0:sum(n for _, n in at_b.values())], dram["const_b"]).then_inc(consts_loaded, 16)
                with sp.Fori(1, phase.units // SLOTS) as i:
                    for s in range(SLOTS):
                        sp.wait_ge(split_ready, i * (SLOTS * phase.sps) + (phase.sub0 + (s - SLOTS + 1) * phase.sps))
                        load(phase, s, i * SLOTS + s)
                before = phase
            for c in range(0, DC, 2):
                sp.wait_ge(final_ready, c + 2)
                sp.dma_start(out[:, c:c + 2, :], y[:, c:c + 2, META:S2]).then_inc(out_stored, 16)
            sp.wait_ge(out_stored, 16 * DC // 2)

        @block.gpsimd
        def _(pool):
            pool.dma_start(h[:, :, 0:META], dram["meta"]).then_inc(meta_loaded, 16)
            pool.dma_start(w_gates[:, :, :], dram["ab_gates"]).then_inc(meta_loaded, 16)
            pool.wait_ge(x_ready, 2 * DEPTH * DC)
            pool.dma_start(cb[:, 0:sum(n for _, n in at_c.values())], dram["const_c"]).then_inc(consts2_loaded, 16)
            pool.dma_start(w_r, dram["lru_w_r"]).then_inc(consts2_loaded, 16)
            pool.dma_start(w_i, dram["lru_w_i"]).then_inc(consts2_loaded, 16)

        @block.tensor
        def _(pe):
            def product(acc, hi, lo, src, first, last):
                src_hi, src_lo = src
                nc.tensor.matmul(acc, hi, src_hi, start=first, stop=False)
                nc.tensor.matmul(acc, hi, src_lo, start=False, stop=False)
                return nc.tensor.matmul(acc, lo, src_hi, start=False, stop=last)

            def dense(phase, src, n, free, first_free, ready):
                body = phase.body
                banks = SLOTS if phase.upo == 1 else 2
                with pe.Fori(0, phase.units // body) as i:
                    for u in range(body):
                        o = u // phase.upo
                        if phase.pairs:
                            if u % 2 == 0:
                                pe.wait_ge(free, i * (body // 2) + (first_free + u // 2))
                        elif u % phase.upo == 0:
                            pe.wait_ge(free, i * (body // phase.upo) + (first_free + o))
                        acc = PS[:, o % banks, 0:n]
                        for k in range(phase.tiles):
                            kk = (u % phase.upo) * phase.tiles + k
                            sub = u * phase.sps + k // SUB
                            if k % SUB == 0:
                                pe.wait_ge(split_ready, i * (body * phase.sps) + (phase.sub0 + sub + 1))
                            if u < phase.upo:
                                pe.wait_ge(*ready(kk))
                            last = product(acc, w_hi[sub % SUBS][:, k % SUB, :], w_lo[sub % SUBS][:, k % SUB, :], src(kk),
                                           kk == 0, kk == phase.upo * phase.tiles - 1)
                            if k % SUB == SUB - 1 or k == phase.tiles - 1:
                                last.then_inc(sub_multiplied, 1)

            def dense_outputs(phase, src, n, ready):
                banks = SLOTS if phase.upo == 1 else 2
                dense(phase, src, n, out_evacuated, FREE_BANKS + phase.out0 - banks + 1, ready)

            def dense_pairs(phase, src, n, ready):
                dense(phase, src, n, pair_done, FREE_PAIRS + phase.pair0 - 1, ready)

            def norm_sum(k, n):
                first = DC * (k // 2)
                for c in range(DC):
                    pe.wait_ge(squares_ready, first + c + 1)
                    nc.tensor.matmul(PS[:, 4, 0:n], mean, sq[:, c % 4, 0:n], start=(c == 0), stop=(c == DC - 1))\
                        .then_inc(square_summed, 1)

            def post_sum(k, n):
                pe.wait_ge(y_added, FREE_SQUARES + DC * (post_index(k) + 1))
                nc.tensor.matmul(PS[:, 4, 0:n], mean, ssum[:, 0:n], start=True, stop=True).then_inc(sum_ready, 1)

            def retention(j, layer):
                g_end = evacuated(ph[f"ret_g{layer}"])
                R = ret_sem
                pe.wait_ge(R["roped"], 8 * j + 8)
                pe.wait_ge(R["v_ready"], 8 * j + 8)
                pe.wait_ge(out_evacuated, g_end)

                def scores(hd):
                    acc = PS[:, 4 + hd % 2, :]
                    for kt in range(2):
                        for c in range(2):
                            last = nc.tensor.matmul(acc[:, kt * S1:(kt + 1) * S1],
                                                    proj1[:, 8 + 2 * hd + c, kt * P:(kt + 1) * P], proj1[:, 2 * hd + c, :],
                                                    start=(c == 0), stop=(c == 1))
                    last.then_inc(R["scores_ready"], 1)

                scores(0)
                for hd in range(RET_HEADS):
                    n = 4 * j + hd
                    if hd + 1 < RET_HEADS:
                        if hd >= 1:
                            pe.wait_ge(R["p_ready"], n)
                        scores(hd + 1)
                    pe.wait_ge(R["p_ready"], n + 1)
                    if hd >= 2:
                        pe.wait_ge(R["gated"], n - 1)
                    first = 6 if hd % 2 == 0 else 2
                    for e in range(4):
                        acc = PS[:, first + e // 2, (e % 2) * S1:(e % 2 + 1) * S1]
                        for kt in range(2):
                            last = nc.tensor.matmul(acc, ret_v[:, kt, hd * RET_V + e * P:hd * RET_V + (e + 1) * P],
                                                    ret_p[:, hd % 2, kt * S1:(kt + 1) * S1], start=(kt == 0), stop=(kt == 1))
                    last.then_inc(R["o_ready"], 1)
                    pe.wait_ge(R["squares_ready"], n + 1)
                    for e in range(4):
                        last = nc.tensor.matmul(PS[:, hd % 2, 0:S1], mean, ret_sq[:, e, :], start=(e == 0), stop=(e == 3))
                    last.then_inc(R["sum_ready"], 1)
                pe.wait_ge(R["gated"], 4 * j + 3)

            def turn_values(j, layer):
                for b in range(8):
                    hd, kt = b // 2, b % 2
                    pe.wait_ge(out_evacuated, evacuated(ph[f"ret_v{layer}"], 4 * hd + 4))
                    if b >= 2:
                        pe.wait_ge(ret_sem["v_ready"], 8 * j + b - 1)
                    for e in range(4):
                        last = nc.tensor.transpose(PS[:, 4 + b % 2, e * P:(e + 1) * P],
                                                   proj1[:, 16 + 4 * hd + e, kt * P:(kt + 1) * P], ident)
                    last.then_inc(ret_sem["v_turned"], 1)

            def conv():
                C = conv_sem
                pe.wait_ge(C["acc_ready"], 1)
                for c in range(DC):
                    last = nc.tensor.matmul(PS[:, 4, 0:S1], mean, conv_acc[:, c, :], start=(c == 0), stop=(c == DC - 1))
                last.then_inc(C["mean_ready"], 1)
                pe.wait_ge(C["squares_ready"], 1)
                for c in range(DC):
                    last = nc.tensor.matmul(PS[:, 5, 0:S1], mean, conv_sq[:, c, :], start=(c == 0), stop=(c == DC - 1))
                last.then_inc(C["var_ready"], 1)

            def attention(half):
                A = att_sem
                base = half * (DC // 2)
                pe.wait_ge(out_evacuated, evacuated(ph[f"att_in{half}"]))
                with pe.Fori(0, DC // 2) as i:
                    pe.wait_ge(A["roped"], i * 3 + (3 * base + 3))
                    for g in range(3):
                        for w in range(2):
                            last = nc.tensor.matmul(PS[:, g, w * S1:(w + 1) * S1], swap, proj1[:, i + (g * 3 + w) * 4, :],
                                                    start=True, stop=True)
                        last.then_inc(A["rotated"], 1)
                    pe.wait_ge(A["v_staged"], i * 3 + (3 * base + 3))
                    for g in range(3):
                        for kt in range(2):
                            last = nc.tensor.transpose(PS[:, 3 + g // 2, (g % 2) * S1 + kt * P:(g % 2) * S1 + (kt + 1) * P],
                                                       att_vs[:, g, kt * P:(kt + 1) * P], ident)
                    last.then_inc(A["v_turned"], 1)
                    pe.wait_ge(A["roped"], i * 3 + (3 * base + 6))

                    def scores(u):
                        e, it = u // 2, u % 2
                        rows = slice(64 * e, 64 * e + 64)
                        for g in range(3):
                            b = (5 if u % 2 == 0 else 0) + g // 2
                            last = nc.tensor.matmul(PS[:, b, (g % 2) * S1:(g % 2 + 1) * S1],
                                                    att_q[rows, g, it * P:(it + 1) * P], att_k[rows, g, :], start=True, stop=True)
                        last.then_inc(A["scores_ready"], 1)

                    scores(0)
                    for u in range(4):
                        e = u // 2
                        if u < 3:
                            scores(u + 1)
                        pe.wait_ge(A["p_ready"], i * 4 + (4 * base + u + 1))
                        if u == 0:
                            pe.wait_ge(A["v_ready"], i + (base + 1))
                        for t in range(6):
                            acc = PS[:, 7, t * P:(t + 1) * P] if t < 4 else PS[:, 4, S1 + (t - 4) * P:S1 + (t - 3) * P]
                            last = nc.tensor.transpose(acc, att_p[:, u % 2, t * P:(t + 1) * P], ident)
                        last.then_inc(A["p_turned"], 1)
                        pe.wait_ge(A["pt_ready"], i * 8 + (8 * base + 2 * (u + 1)))
                        for t in range(6):
                            last = nc.tensor.matmul(PS[:, 3, u * 64:(u + 1) * 64], att_pt[:, u % 2, t * P:(t + 1) * P],
                                                    att_vn[:, t, e * 64:(e + 1) * 64], start=(t == 0), stop=(t == 5))
                        last.then_inc(A["o_ready"], 1)
                    pe.wait_ge(A["o_scaled"], i * 4 + (4 * base + 4))
                    for it in range(2):
                        last = nc.tensor.transpose(PS[:, 6, S1 + it * P:S1 + (it + 1) * P], att_o[:, it, :], ident)
                    last.then_inc(A["o_turned"], 1)
                pe.wait_ge(A["mixed"], base + DC // 2)

            def gates():
                pe.wait_ge(gates_split, 1)
                for k in range(DC):
                    pe.wait_ge(x_split, DC * (2 * DEPTH) + k + 1)
                    for gate in range(2):
                        cols = slice(gate * A_HEADS, (gate + 1) * A_HEADS)
                        last = product(PS[0:A_HEADS, 5 + gate, 0:S2], gates_hi[:, k, cols], gates_lo[:, k, cols],
                                       (xh[:, k, :], xl[:, k, :]), k == 0, k == DC - 1)
                last.then_inc(ab_sem["gate_sums"], 1)

            def mlstm():
                A = ab_sem
                pe.wait_ge(out_evacuated, evacuated(ph["ab_x"]))
                for st, (t0, tl) in enumerate(TILES2):
                    if st >= 2:
                        pe.wait_ge(A["v_ready"], st - 1)
                    for c in range(DC):
                        b = 2 * (st % 2) + c // 4
                        last = nc.tensor.transpose(PS[0:tl, b, (c % 4) * P:(c % 4 + 1) * P], proj2[:, 16 + c, t0:t0 + tl], ident)
                    last.then_inc(A["v_turned"], 1)
                pe.wait_ge(A["rows_ready"], 1)
                for st, (t0, tl) in enumerate(TILES2):
                    last = nc.tensor.transpose(PS[0:tl, 7, st * 4:st * 4 + 4], r_a[:, t0:t0 + tl], ident[0:A_HEADS, 0:A_HEADS])
                last.then_inc(A["turned"], 1)
                pe.wait_ge(A["v_ready"], 3)
                pe.wait_ge(A["floor_ready"], 1)
                pe.wait_ge(A["cols_ready"], 1)
                pe.wait_ge(consts2_loaded, 48)
                sel = const("sel")
                for hd in range(A_HEADS):
                    if hd >= 1:
                        pe.wait_ge(A["h_ready"], hd)
                        pe.wait_ge(A["p_ready"], 3 * hd)
                    head_sel = sel[0:A_HEADS, hd * P:(hd + 1) * P]
                    nc.tensor.matmul(PS[:, 0, 0:S2], head_sel, r_m, start=True, stop=True).then_inc(A["run_ready"], 1)
                    for st, (t0, tl) in enumerate(TILES2):
                        for c in range(2):
                            last = nc.tensor.matmul(PS[0:tl, 1 + st, 0:S2], proj2[:, 8 + 2 * hd + c, t0:t0 + tl],
                                                    proj2[:, 2 * hd + c, :], start=(c == 0), stop=(c == 1))
                        last.then_inc(A["scores_ready"], 1)
                    nc.tensor.matmul(PS[:, 7, 0:S2], head_sel, r_en, start=True, stop=True)
                    pe.wait_ge(A["p_ready"], 3 * hd + 3)
                    pt = [ab_p[0:tl, 3 * (hd % 2) + st, :] for st, (_, tl) in enumerate(TILES2)]
                    for st, (_, tl) in enumerate(TILES2):
                        nc.tensor.matmul(PS[:, 4, 0:S2], ones[0:tl, :], pt[st], start=(st == 0), stop=(st == 2))
                    for c in range(2):
                        for st, (_, tl) in enumerate(TILES2):
                            last = nc.tensor.matmul(PS[:, 5 + c, 0:S2], ab_v[0:tl, st, hd * A_DIM + c * P:hd * A_DIM + (c + 1) * P],
                                                    pt[st], start=(st == 0), stop=(st == 2))
                    last.then_inc(A["num_ready"], 1)
                    pe.wait_ge(A["squares_ready"], hd + 1)
                    for c in range(2):
                        last = nc.tensor.matmul(PS[:, 0, 0:S2], mean, ab_sq[:, c, :], start=(c == 0), stop=(c == 1))
                    last.then_inc(A["sum_ready"], 1)
                    pe.wait_ge(A["rstd_ready"], hd + 1)

            def lru_gates():
                L = lru_sem
                pe.wait_ge(L["conv_ready"], 1)
                pe.wait_ge(ab_sem["h_ready"], A_HEADS)
                for c in range(DC):
                    if c >= 2:
                        pe.wait_ge(L["gates_ready"], 2 * (c - 1))
                    for gate, w in ((0, w_r), (1, w_i)):
                        last = nc.tensor.matmul(PS[:, 2 * (c % 2) + gate, 0:S2], w[:, c, :], lru_xc[:, c, :], start=True, stop=True)
                    last.then_inc(L["gates_summed"], 1)
                pe.wait_ge(L["gates_ready"], 2 * DC)

            def diff_attention():
                A = c_sem
                pe.wait_ge(out_evacuated, evacuated(ph["c_in"]))
                with pe.Fori(0, C_HEADS) as i:
                    pe.wait_ge(A["roped"], i + 1)
                    for w in range(2):
                        last = nc.tensor.matmul(PS[:, w, 0:S2], swap, proj2[:, i + w * 8, :], start=True, stop=True)
                    last.then_inc(A["rotated"], 1)
                    pe.wait_ge(A["mixed"], i + 1)
                    pe.wait_ge(A["v_staged"], i + 1)
                    for st, (t0, tl) in enumerate(TILES2):
                        last = nc.tensor.transpose(PS[0:tl, 2, st * P:(st + 1) * P], c_vs[:, t0:t0 + tl], ident)
                    last.then_inc(A["v_turned"], 1)
                    pe.wait_ge(A["roped"], i + 2)

                    def scores(u):
                        t0, tl = TILES2[u]
                        for e in range(2):
                            rows = slice(64 * e, 64 * e + 64)
                            last = nc.tensor.matmul(PS[0:tl, 3 + 2 * (u % 2) + e, 0:t0 + tl], c_q[rows, t0:t0 + tl],
                                                    c_k[rows, 0:t0 + tl], start=True, stop=True)
                        last.then_inc(A["scores_ready"], 1)

                    scores(0)
                    for u, (t0, tl) in enumerate(TILES2):
                        if u < 2:
                            scores(u + 1)
                        pe.wait_ge(A["pd_ready"], i * 3 + (u + 1))
                        if u == 2:
                            pe.sem_inc(wait_taken, 1)
                        for st in range(u + 1):
                            s0, sl = TILES2[st]
                            last = nc.tensor.transpose(PS[0:sl, (7, 0, 1)[st], t0:t0 + tl], c_pd[0:tl, u % 2, s0:s0 + sl],
                                                       ident[0:tl, 0:tl])
                        last.then_inc(A["p_turned"], 1)
                    pe.wait_ge(A["v_ready"], i + 1)
                    pe.wait_ge(A["pt_ready"], i + 1)
                    for st, (s0, sl) in enumerate(TILES2):
                        last = nc.tensor.matmul(PS[:, 2, s0:S2], c_vn[0:sl, st, :], c_pt[0:sl, st, s0:S2],
                                                start=(st == 0), stop=(st == 2))
                    last.then_inc(A["o_ready"], 1)
                    pe.wait_ge(A["squares_ready"], i + 1)
                    nc.tensor.matmul(PS[:, 5, 0:S2], mean, c_sq, start=True, stop=True).then_inc(A["sum_ready"], 1)
                pe.wait_ge(A["mixed"], C_HEADS + 1)

            pe.sem_inc(sub_multiplied, FREE_SUBS)
            pe.sem_inc(square_summed, FREE_SQUARES)
            pe.wait_ge(consts_loaded, 48)

            def normed(number, n):
                return (lambda k: (xh[:, k, 0:n], xl[:, k, 0:n])), (lambda k: (x_split, DC * number + k + 1))

            def hidden(hi, lo, name):
                return (lambda k: (hi[:, k, :], lo[:, k, :])), (lambda k: (part_lo, hidden0[name] + k + 1))

            for layer in range(DEPTH):
                norm_sum(4 * layer, S1)
                src, ready = normed(2 * layer, S1)
                if layer % 3 == 0:
                    j = layer // 3
                    dense_outputs(ph[f"ret_qk{layer}"], src, S1, ready)
                    dense_outputs(ph[f"ret_v{layer}"], src, S1, ready)
                    turn_values(j, layer)
                    dense_outputs(ph[f"ret_g{layer}"], src, S1, ready)
                    retention(j, layer)
                    dense_outputs(ph[f"ret_out{layer}"], lambda k: (ret_hi[k], ret_lo[k]), S1,
                                  lambda k: (ret_sem["split"], 4 * j + k // 4 + 1))
                elif layer % 3 == 1:
                    dense_pairs(ph["conv_in"], src, S1, ready)
                    conv()
                    dense_outputs(ph["conv_out"], lambda k: (conv_hi[:, k, :], conv_lo[:, k, :]), S1,
                                  lambda k: (conv_sem["split"], k + 1))
                else:
                    for half in range(2):
                        dense_outputs(ph[f"att_in{half}"], src, S1, ready)
                        attention(half)
                    dense_outputs(ph["att_out"], lambda k: (att_hi[:, k, :], att_lo[:, k, :]), S1,
                                  lambda k: (att_sem["mixed"], k + 1))
                post_sum(4 * layer + 1, S1)
                norm_sum(4 * layer + 2, S1)
                src, ready = normed(2 * layer + 1, S1)
                dense_pairs(ph[f"ffn_in{layer}"], src, S1, ready)
                src, ready = hidden(hid_hi, hid_lo, f"ffn_in{layer}")
                dense_outputs(ph[f"ffn_out{layer}"], src, S1, ready)
                post_sum(4 * layer + 3, S1)
            norm_sum(16, S2)
            for layer in range(2):
                src, ready = normed(2 * DEPTH + 2 * layer, S2)
                if layer == 0:
                    gates()
                    for name in ("ab_qkv", "ab_o", "ab_x"):
                        dense_outputs(ph[name], src, S2, ready)
                    mlstm()
                    lru_gates()
                    dense_outputs(ph["ab_out"], lambda k: (ab_hi[k], ab_lo[k]), S2,
                                  lambda k: (ab_sem["mixed"], k // 2 + 1) if k < DC else (lru_sem["done"], 1))
                else:
                    dense_outputs(ph["c_in"], src, S2, ready)
                    diff_attention()
                    dense_outputs(ph["c_out"], lambda k: (c_hi[:, k, :], c_lo[:, k, :]), S2,
                                  lambda k: (c_sem["mixed"], k + 2))
                post_sum(17 + 2 * layer, S2)
                src, ready = normed(2 * DEPTH + 2 * layer + 1, S2)
                dense_outputs(ph[f"mlp_in{layer}"], src, S2, ready)
                src, ready = hidden(mlp_hi, mlp_lo, f"mlp_in{layer}")
                dense_outputs(ph[f"mlp_out{layer}"], src, S2, ready)
                post_sum(18 + 2 * layer, S2)

        @block.scalar
        def _(act):
            chain = [0]

            def step(ins):
                chain[0] += 1
                ins.then_inc(act_chain, 1)
                act.wait_ge(act_chain, chain[0])

            def split(phase, i, u):
                slot = u % SLOTS
                for j in range(phase.sps):
                    n = min(SUB, phase.tiles - j * SUB)
                    sub = u * phase.sps + j
                    if j == 0:
                        act.wait_ge(weights_loaded[slot], i * (16 * phase.body // SLOTS)
                                    + 16 * (phase.unit0 // SLOTS + u // SLOTS + 1))
                    act.wait_ge(sub_multiplied, i * (phase.body * phase.sps) + (phase.sub0 + sub + 1))
                    nc.scalar.activation(w_hi[sub % SUBS][:, 0:n, :], raw[slot][:, j * SUB:j * SUB + n, :], ACT.Copy)\
                        .then_inc(hi_ready, 1)

            def stream(phase, unit):
                turns = phase.units // phase.body
                with act.Fori(0, turns - 1) as i:
                    for u in range(phase.body):
                        split(phase, i, u + 1)
                        unit(i, u)
                for u in range(phase.body):
                    if u + 1 < phase.body:
                        split(phase, turns - 1, u + 1)
                    elif phase.after:
                        split(phase.after, 0, 0)
                    unit(turns - 1, u)

            def wait_unit(phase, i, u):
                act.wait_ge(sub_multiplied, i * (phase.body * phase.sps) + multiplied(phase, u + 1))

            def evacuate(phase, dst, n, func=ACT.Copy):
                def unit(i, u):
                    wait_unit(phase, i, u)
                    nc.scalar.activation(dst[:, i * phase.body + u, 0:n], PS[:, u % SLOTS, 0:n], func).then_inc(out_evacuated, 1)
                stream(phase, unit)

            def evacuate_y(k, phase, bias=None):
                banks = SLOTS if phase.upo == 1 else 2
                per = phase.body // phase.upo

                def unit(i, u):
                    if u % phase.upo < phase.upo - 1:
                        return
                    o = u // phase.upo
                    acc = PS[:, o % banks, 0:S1]
                    extra = {} if bias is None else {"bias": param(bias, 0, DC)[:, bass.ds(i * per + o, 1)]}
                    wait_unit(phase, i, u)
                    act.wait_ge(y_added, i * per + (FREE_SQUARES - per + DC * post_index(k) + o + 1))
                    nc.scalar.activation(sq[:, o, 0:S1], acc, ACT.Square, **extra).then_inc(y_squared, 1)
                    nc.scalar.activation(y[:, i * per + o, 0:S1], acc, ACT.Copy if bias is None else ACT.Identity, **extra)\
                        .then_inc(out_evacuated, 1)
                stream(phase, unit)

            def square_h(k, phase):
                per = phase.body // phase.upo

                def unit(i, u):
                    if u % phase.upo < phase.upo - 1:
                        return
                    o = u // phase.upo
                    act.wait_ge(out_evacuated, i * per + evacuated(phase, o + 1))
                    act.wait_ge(y_added, i * per + (FREE_SQUARES - per + DC * post_index(k) + o + 1))
                    nc.scalar.activation(sq[:, o, :], h[:, i * per + o, :], ACT.Square).then_inc(y_squared, 1)
                stream(phase, unit)

            def rms(n):
                step(nc.scalar.activation(lnv[:, 0:n], PS[:, 4, 0:n], ACT.Ln, bias=rms_eps))
                nc.scalar.activation(rstd[:, 0:n], lnv[:, 0:n], ACT.Exp, scale=-0.5).then_inc(rstd_ready, 1)

            def norm(k, src, n):
                first = DC * (k // 2)
                for c in range(DC):
                    if k:
                        act.wait_ge(x_ready, first - DC + c + 1)
                    act.wait_ge(square_summed, first + c + 1)
                    nc.scalar.activation(sq[:, c % 4, 0:n], src[:, c, 0:n], ACT.Square).then_inc(squares_ready, 1)
                act.wait_ge(square_summed, FREE_SQUARES + first + DC)
                rms(n)

            def post_norm(k, n):
                act.wait_ge(sum_ready, post_index(k) + 1)
                rms(n)

            def round_normed(number, n):
                for c in range(DC):
                    act.wait_ge(xt_ready, DC * number + c + 1)
                    nc.scalar.activation(xh[:, c, 0:n], xt[:, c % 4, 0:n], ACT.Copy).then_inc(xh_ready, 1)

            def silu_pairs(phase):
                def unit(i, u):
                    if u % 2 == 0:
                        wait_unit(phase, i, u)
                        nc.scalar.activation(silu[:, u // 2, 0:S1], PS[:, u, 0:S1], ACT.Silu).then_inc(gate_ready, 1)
                stream(phase, unit)

            def decay(j):
                for hd in range(RET_HEADS):
                    act.wait_ge(ret_sem["exponent_ready"], 4 * j + hd + 1)
                    nc.scalar.activation(ret_decay[:, hd, :], ret_exp[:, hd % 2, :], ACT.Exp).then_inc(ret_sem["decay_ready"], 1)

            def retention(j):
                R = ret_sem
                for hd in range(RET_HEADS):
                    n = 4 * j + hd
                    first = 6 if hd % 2 == 0 else 2
                    act.wait_ge(R["o_ready"], n + 1)
                    nc.scalar.activation(ret_sq[:, :, :], PS[:, first:first + 2, :].rearrange("p b (e t) -> p (b e) t", t=S1),
                                         ACT.Square).then_inc(R["squares_ready"], 1)
                    act.wait_ge(R["sum_ready"], n + 1)
                    step(nc.scalar.activation(lnv[:, 0:S1], PS[:, hd % 2, 0:S1], ACT.Ln, bias=rms_eps, scale=float(D) / RET_V))
                    if hd >= 1:
                        act.wait_ge(R["gated"], n)
                    nc.scalar.activation(rstd[:, 0:S1], lnv[:, 0:S1], ACT.Exp, scale=-0.5).then_inc(R["rstd_ready"], 1)

            def conv_in(phase):
                def unit(i, u):
                    if u % 2 == 0:
                        wait_unit(phase, i, u)
                        nc.scalar.activation(silu[:, u // 2, 0:S1], PS[:, u, 0:S1], ACT.Sigmoid,
                                             bias=param("conv_b_in", DC, DC)[:, bass.ds(i * 2 + u // 2, 1)]).then_inc(gate_ready, 1)
                stream(phase, unit)

            def conv():
                C = conv_sem
                act.wait_ge(C["centered"], 1)
                nc.scalar.activation(conv_sq[:, :, :], conv_acc[:, :, :], ACT.Square).then_inc(C["squares_ready"], 1)
                act.wait_ge(C["var_ready"], 1)
                step(nc.scalar.activation(lnv[:, 0:S1], PS[:, 5, 0:S1], ACT.Ln, bias=ln_eps))
                nc.scalar.activation(rstd[:, 0:S1], lnv[:, 0:S1], ACT.Exp, scale=-0.5).then_inc(C["rstd_ready"], 1)
                act.wait_ge(C["scaled"], 1)
                for c in range(DC):
                    nc.scalar.activation(conv_mix[:, c, :], conv_sq[:, c, :], ACT.Silu, bias=param("conv_ln_b", c),
                                         scale=param("conv_ln_g", c)).then_inc(C["mixed"], 1)

            def attention(half):
                A = att_sem
                base = half * (DC // 2)
                act.wait_ge(out_evacuated, evacuated(ph[f"att_in{half}"]))
                with act.Fori(0, DC // 2) as i:
                    for g in range(3):
                        nc.scalar.activation(att_vs[:, g, :], proj1[:, i + (g * 3 + 2) * 4, :], ACT.Copy).then_inc(A["v_staged"], 1)

                    def exp(u):
                        act.wait_ge(A["max_ready"], i * 4 + (4 * base + u + 1))
                        nc.scalar.activation(att_p[:, u % 2, :], att_s[:, u % 2, :], ACT.Exp, bias=att_max[:, u % 2, 4:5],
                                             scale=0.125, accum_out=att_den[:, u % 2:u % 2 + 1]).then_inc(A["p_ready"], 1)

                    exp(0)
                    for u in range(4):
                        e, it = u // 2, u % 2
                        if u < 3:
                            exp(u + 1)
                        act.wait_ge(A["p_turned"], i * 4 + (4 * base + u + 1))
                        nc.scalar.activation(att_pt[:, u % 2, 512:768], PS[:, 4, S1:512], ACT.Copy).then_inc(A["pt_ready"], 1)
                        act.wait_ge(A["o_ready"], i * 4 + (4 * base + u + 1))
                        act.wait_ge(A["den_ready"], i * 4 + (4 * base + u + 1))
                        nc.scalar.activation(att_o[:, it, e * 64:(e + 1) * 64], PS[:, 3, u * 64:(u + 1) * 64], ACT.Copy,
                                             scale=att_rden[:, u % 2:u % 2 + 1]).then_inc(A["o_scaled"], 1)

            def mlstm_rows():
                A = ab_sem
                act.wait_ge(A["log_in"], 1)
                step(nc.scalar.activation(r_l, r_e, ACT.Exp))
                nc.scalar.activation(r_l, r_l, ACT.Ln, bias=one[0:A_HEADS, :]).then_inc(A["log_ready"], 1)
                act.wait_ge(A["floor_in"], 1)
                nc.scalar.activation(r_en, r_sum, ACT.Exp, scale=-1.0).then_inc(A["floor_ready"], 1)

            def mlstm():
                A = ab_sem
                for hd in range(A_HEADS):
                    for st, (_, tl) in enumerate(TILES2):
                        act.wait_ge(A["shifted"], 3 * hd + st + 1)
                        nc.scalar.activation(ab_w[0:tl, st, :], ab_t[0:tl, st, :], ACT.Exp, bias=ab_col[0:tl, st, hd:hd + 1],
                                             scale=-1.0).then_inc(A["w_ready"], 1)
                    act.wait_ge(A["num_ready"], hd + 1)
                    nc.scalar.activation(ab_den[:, 0, :], PS[:, 4, 0:S2], ACT.Abs).then_inc(A["den_abs"], 1)
                    act.wait_ge(A["h_ready"], hd + 1)
                    for c in range(2):
                        last = nc.scalar.activation(ab_sq[:, c, :], ab_hh[:, c, :], ACT.Square)
                    last.then_inc(A["squares_ready"], 1)
                    act.wait_ge(A["sum_ready"], hd + 1)
                    step(nc.scalar.activation(lnv[:, :], PS[:, 0, 0:S2], ACT.Ln, bias=rms_eps, scale=float(D) / A_DIM))
                    nc.scalar.activation(ab_r[:, hd % 2, :], lnv[:, :], ACT.Exp, scale=-0.5).then_inc(A["rstd_ready"], 1)

            def lru():
                L = lru_sem
                for c in range(DC):
                    act.wait_ge(L["gates_summed"], c + 1)
                    for gate, dst, bias in ((0, lru_r, "lru_b_r"), (1, lru_i, "lru_b_i")):
                        nc.scalar.activation(dst[:, c, :], PS[:, 2 * (c % 2) + gate, 0:S2], ACT.Sigmoid, bias=param(bias, c))\
                            .then_inc(L["gates_ready"], 1)
                act.wait_ge(L["loga_ready"], 1)
                nc.scalar.activation(lru_a[:, :, :], lru_r[:, :, :], ACT.Exp)
                nc.scalar.activation(lru_r[:, :, :], lru_r[:, :, :], ACT.Tanh, scale=-1.0).then_inc(L["a_ready"], 1)
                act.wait_ge(L["root_in"], 1)
                nc.scalar.activation(lru_r[:, :, :], lru_r[:, :, :], ACT.Sqrt, scale=2.0).then_inc(L["root_ready"], 1)
                act.wait_ge(L["gelu_in"], 1)
                nc.scalar.activation(lru_r[:, :, :], lru_r[:, :, :], ACT.Tanh, scale=math.sqrt(2.0 / math.pi))\
                    .then_inc(L["gelu_ready"], 1)

            def relu(phase):
                def unit(i, u):
                    wait_unit(phase, i, u)
                    act.wait_ge(part_ready, i * phase.body + (hidden0[phase.name] - DEPTH * FFN + u + 1))
                    nc.scalar.activation(silu[:, u % 2, :], PS[:, u % SLOTS, 0:S2], ACT.Relu).then_inc(out_evacuated, 1)
                stream(phase, unit)

            def diff_attention():
                A = c_sem
                act.wait_ge(out_evacuated, evacuated(ph["c_in"]))
                with act.Fori(0, C_HEADS) as i:
                    nc.scalar.activation(c_vs, proj2[:, i + 16, :], ACT.Copy).then_inc(A["v_staged"], 1)
                    for u, (t0, tl) in enumerate(TILES2):
                        act.wait_ge(A["max_ready"], i * 3 + (u + 1))
                        for e in range(2):
                            last = nc.scalar.activation(c_p[0:tl, 2 * (u % 2) + e, 0:t0 + tl], c_s[0:tl, 2 * (u % 2) + e, 0:t0 + tl],
                                                        ACT.Exp, bias=c_max[0:tl, u % 2, 2 + e:3 + e], scale=0.125,
                                                        accum_out=c_den[0:tl, u % 2, e:e + 1])
                        last.then_inc(A["p_ready"], 1)
                    act.wait_ge(A["o_ready"], i + 1)
                    nc.scalar.activation(c_sq, PS[:, 2, 0:S2], ACT.Square).then_inc(A["squares_ready"], 1)
                    act.wait_ge(A["sum_ready"], i + 1)
                    nc.scalar.activation(c_ln, PS[:, 5, 0:S2], ACT.Ln, bias=rms_eps, scale=float(D) / P).then_inc(c_logged, 1)
                    act.wait_ge(c_logged, i + 1)
                    nc.scalar.activation(c_r, c_ln, ACT.Exp, scale=-0.5).then_inc(A["rstd_ready"], 1)

            def exp_tables():
                nc.scalar.preload_act_table_set("natural_log_exp_and_others")

            act.sem_inc(out_evacuated, FREE_BANKS)
            exp_tables()
            act.wait_ge(x_loaded, 16)
            act.wait_ge(consts_loaded, 48)
            for layer in range(DEPTH):
                norm(4 * layer, x, S1)
                if layer == 0:
                    step(nc.scalar.activation(lg, param("decay", 0, 16), ACT.Exp))
                    nc.scalar.activation(lg, lg, ACT.Ln, bias=one, scale=-1.0).then_inc(ret_sem["lg_ready"], 1)
                    act.wait_ge(lru_sem["lam_ready"], 1)
                    nc.scalar.activation(lam_t[:, 1, :], lam_t[:, 0, :], ACT.Exp).then_inc(lru_sem["softplus_ready"], 1)
                round_normed(2 * layer, S1)
                if layer == 0:
                    split(phases[0], 0, 0)
                    decay(0)
                if layer % 3 == 0:
                    j = layer // 3
                    nc.scalar.preload_act_table(ACT.Silu)
                    evacuate(ph[f"ret_qk{layer}"], proj1, S1)
                    evacuate(ph[f"ret_v{layer}"], proj1[:, 16:32, :], S1)
                    evacuate(ph[f"ret_g{layer}"], proj1[:, 32:48, :], S1, ACT.Silu)
                    exp_tables()
                    retention(j)
                    evacuate_y(4 * layer + 1, ph[f"ret_out{layer}"])
                elif layer % 3 == 1:
                    nc.scalar.preload_act_table(ACT.Sigmoid)
                    conv_in(ph["conv_in"])
                    exp_tables()
                    conv()
                    exp_tables()
                    evacuate_y(4 * layer + 1, ph["conv_out"], bias="conv_b_out")
                else:
                    for half in range(2):
                        evacuate(ph[f"att_in{half}"], proj1, S1)
                        attention(half)
                    evacuate_y(4 * layer + 1, ph["att_out"])
                post_norm(4 * layer + 1, S1)
                norm(4 * layer + 2, x, S1)
                nc.scalar.preload_act_table(ACT.Silu)
                round_normed(2 * layer + 1, S1)
                silu_pairs(ph[f"ffn_in{layer}"])
                exp_tables()
                if layer == 2:
                    decay(1)
                evacuate_y(4 * layer + 3, ph[f"ffn_out{layer}"])
                post_norm(4 * layer + 3, S1)
            act.wait_ge(meta_loaded, 32)
            norm(16, h, S2)
            for layer in range(2):
                round_normed(2 * DEPTH + 2 * layer, S2)
                if layer == 0:
                    evacuate(ph["ab_qkv"], proj2, S2)
                    mlstm_rows()
                    nc.scalar.preload_act_table(ACT.Sigmoid)
                    evacuate(ph["ab_o"], proj2[:, 24:32, :], S2, ACT.Sigmoid)
                    evacuate(ph["ab_x"], proj2[:, 32:48, :], S2)
                    exp_tables()
                    mlstm()
                    lru()
                    exp_tables()
                    square_h(17, ph["ab_out"])
                else:
                    act.wait_ge(c_sem["lam_in"], 1)
                    nc.scalar.activation(lam_s[:, 2:4], lam_s[:, 0:2], ACT.Exp).then_inc(c_sem["lam_exp"], 1)
                    evacuate(ph["c_in"], proj2, S2)
                    diff_attention()
                    square_h(19, ph["c_out"])
                post_norm(17 + 2 * layer, S2)
                round_normed(2 * DEPTH + 2 * layer + 1, S2)
                relu(ph[f"mlp_in{layer}"])
                square_h(18 + 2 * layer, ph[f"mlp_out{layer}"])
                post_norm(18 + 2 * layer, S2)

        @block.vector
        def _(dve):
            chain = [0]

            def step(ins):
                chain[0] += 1
                ins.then_inc(dve_chain, 1)
                dve.wait_ge(dve_chain, chain[0])

            stt = nc.vector.scalar_tensor_tensor

            def split(phase, i, u):
                slot = u % SLOTS
                for j in range(phase.sps):
                    n = min(SUB, phase.tiles - j * SUB)
                    sub = u * phase.sps + j
                    dve.wait_ge(hi_ready, i * (phase.body * phase.sps) + (phase.sub0 + sub + 1))
                    nc.vector.tensor_tensor(w_lo[sub % SUBS][:, 0:n, :], raw[slot][:, j * SUB:j * SUB + n, :],
                                            w_hi[sub % SUBS][:, 0:n, :].bitcast(F32), ALU.subtract).then_inc(split_ready, 1)

            def stream(phase, unit=None):
                turns = phase.units // phase.body
                with dve.Fori(0, turns - 1) as i:
                    for u in range(phase.body):
                        split(phase, i, u + 1)
                        if unit:
                            unit(i, u)
                for u in range(phase.body):
                    if u + 1 < phase.body:
                        split(phase, turns - 1, u + 1)
                    elif phase.after:
                        split(phase.after, 0, 0)
                    if unit:
                        unit(turns - 1, u)

            def wait_unit(phase, i, u):
                dve.wait_ge(sub_multiplied, i * (phase.body * phase.sps) + multiplied(phase, u + 1))

            def pre_norm(k, number, src, n, weight, col):
                dve.wait_ge(rstd_ready, k + 1)

                def rest(c):
                    dve.wait_ge(xh_ready, DC * number + c + 1)
                    nc.vector.tensor_tensor(xl[:, c, 0:n], xt[:, c % 4, 0:n], xh[:, c, 0:n].bitcast(F32), ALU.subtract)\
                        .then_inc(x_split, 1)

                for c in range(DC):
                    if c >= 4:
                        dve.wait_ge(x_split, DC * number + c - 3)
                    stt(xt[:, c % 4, 0:n], src[:, c, 0:n], param(weight, col + c), rstd[:, 0:n], ALU.mult, ALU.mult)\
                        .then_inc(xt_ready, 1)
                    if c >= 2:
                        rest(c - 2)
                rest(DC - 2)
                rest(DC - 1)

            def sum_squares(k, phase, n, unit=None):
                per = phase.body // phase.upo
                step(nc.vector.memset(ssum[:, 0:n], 0.0))

                def output(i, u):
                    if u % phase.upo < phase.upo - 1:
                        return
                    o = u // phase.upo
                    if unit:
                        unit(i, u)
                    dve.wait_ge(y_squared, i * per + (DC * post_index(k) + o + 1))
                    dve.wait_ge(y_added, i * per + (FREE_SQUARES + DC * post_index(k) + o))
                    nc.vector.tensor_tensor(ssum[:, 0:n], ssum[:, 0:n], sq[:, o, 0:n], ALU.add).then_inc(y_added, 1)
                stream(phase, output)

            def post_norm(k, col):
                first = DC * post_index(k)
                dve.wait_ge(rstd_ready, k + 1)

                def update(c):
                    dve.wait_ge(scaled, first + c + 1)
                    nc.vector.tensor_tensor(x[:, c, :], x[:, c, :], y[:, c, 0:S1], ALU.add).then_inc(x_ready, 1)

                for c in range(DC):
                    stt(y[:, c, 0:S1], y[:, c, 0:S1], param("norm_w", col + c), rstd[:, 0:S1], ALU.mult, ALU.mult)\
                        .then_inc(scaled, 1)
                    if c:
                        update(c - 1)
                update(DC - 1)

            def add_to_h(k, phase):
                banks = SLOTS if phase.upo == 1 else 2
                per = phase.body // phase.upo

                def unit(i, u):
                    o = u // phase.upo
                    wait_unit(phase, i, u)
                    nc.vector.tensor_tensor(h[:, i * per + o, :], h[:, i * per + o, :], PS[:, o % banks, 0:S2], ALU.add)\
                        .then_inc(out_evacuated, 1)
                sum_squares(k, phase, S2, unit)

            def split_hidden(hi, lo, t, i, number, first):
                nc.vector.tensor_copy(hi, t).then_inc(part_hi, 1)
                dve.wait_ge(part_hi, i + (first + number + 1))
                nc.vector.tensor_tensor(lo, t, hi.bitcast(F32), ALU.subtract).then_inc(part_lo, 1)

            def ffn_pairs(phase):
                first = hidden0[phase.name]

                def unit(i, u):
                    if u % 2 == 0:
                        return
                    q = u // 2
                    wait_unit(phase, i, u)
                    dve.wait_ge(gate_ready, i * 2 + (phase.pair0 + q + 1))
                    nc.vector.tensor_tensor(part[:, q, 0:S1], PS[:, u, 0:S1], silu[:, q, 0:S1], ALU.mult).then_inc(pair_done, 1)
                    dve.wait_ge(pair_done, i * 2 + (FREE_PAIRS + phase.pair0 + q + 1))
                    split_hidden(hid_hi[:, i * 2 + q, :], hid_lo[:, i * 2 + q, :], part[:, q, 0:S1], i * 2, q, first)
                stream(phase, unit)

            def square_relu(phase):
                first = hidden0[phase.name]

                def unit(i, u):
                    dve.wait_ge(out_evacuated, i * phase.body + evacuated(phase, u + 1))
                    nc.vector.tensor_tensor(part[:, u % 2, :], silu[:, u % 2, :], silu[:, u % 2, :], ALU.mult).then_inc(part_ready, 1)
                    dve.wait_ge(part_ready, i * phase.body + (first - DEPTH * FFN + u + 3))
                    m = i * phase.body + u
                    split_hidden(mlp_hi[:, m, :], mlp_lo[:, m, :], part[:, u % 2, :], i * phase.body, u, first)
                stream(phase, unit)

            def exponents(j):
                after, before = const("after"), const("before")
                if j == 0:
                    dve.wait_ge(ret_sem["lg_ready"], 1)
                for hd in range(RET_HEADS):
                    fwd = lg[:, 8 * j + hd:8 * j + hd + 1]
                    bwd = lg[:, 8 * j + 4 + hd:8 * j + 5 + hd]
                    if hd >= 2:
                        dve.wait_ge(ret_sem["decay_ready"], 4 * j + hd - 1)
                    step(nc.vector.tensor_scalar(ret_exp[:, hd % 2, :], after, fwd, None, ALU.mult))
                    stt(ret_exp[:, hd % 2, :], before, bwd, ret_exp[:, hd % 2, :], ALU.mult, ALU.add)\
                        .then_inc(ret_sem["exponent_ready"], 1)

            def rotate(j, phase):
                R = ret_sem
                cos, sin = const("ret_cos"), const("ret_sin")

                def unit(i, u):
                    if u % 2 == 0:
                        return
                    x1, x2 = proj1[:, i * phase.body + (u - 1), :], proj1[:, i * phase.body + u, :]
                    t = ret_half[:, 2 * (u // 2):2 * (u // 2) + 2, :].rearrange("p a (b t) -> p (a b) t", t=S1)
                    dve.wait_ge(out_evacuated, i * phase.body + evacuated(phase, u + 1))
                    nc.vector.tensor_tensor(t[:, 0, :], x1, cos, ALU.mult)
                    nc.vector.tensor_tensor(t[:, 1, :], x2, sin, ALU.mult)
                    nc.vector.tensor_tensor(t[:, 2, :], x2, cos, ALU.mult)
                    nc.vector.tensor_tensor(t[:, 3, :], x1, sin, ALU.mult).then_inc(R["half_rotated"], 1)
                    dve.wait_ge(R["half_rotated"], i * 2 + (8 * j + u // 2 + 1))
                    nc.vector.tensor_tensor(x1, t[:, 0, :], t[:, 1, :], ALU.subtract)
                    nc.vector.tensor_tensor(x2, t[:, 2, :], t[:, 3, :], ALU.add).then_inc(R["roped"], 1)
                stream(phase, unit)
                dve.wait_ge(R["roped"], 8 * j + 8)

            def values(j):
                R = ret_sem
                for b in range(8):
                    dve.wait_ge(R["v_turned"], 8 * j + b + 1)
                    hd, kt = b // 2, b % 2
                    nc.vector.tensor_copy(ret_v[:, kt, hd * RET_V:(hd + 1) * RET_V], PS[:, 4 + b % 2, :]).then_inc(R["v_ready"], 1)

            def retention(j, layer):
                R = ret_sem
                dve.wait_ge(R["decay_ready"], 4 * j + 4)

                def decayed(hd):
                    dve.wait_ge(R["scores_ready"], 4 * j + hd + 1)
                    if hd >= 2:
                        dve.wait_ge(R["o_ready"], 4 * j + hd - 1)
                    stt(ret_p[:, hd % 2, :], PS[:, 4 + hd % 2, :], RET_QK ** -0.5, ret_decay[:, hd, :], ALU.mult, ALU.mult)\
                        .then_inc(R["p_ready"], 1)

                dve.wait_ge(out_evacuated, evacuated(ph[f"ret_g{layer}"]))
                decayed(0)
                for hd in range(RET_HEADS):
                    if hd + 1 < RET_HEADS:
                        decayed(hd + 1)
                    first = 6 if hd % 2 == 0 else 2
                    dve.wait_ge(R["rstd_ready"], 4 * j + hd + 1)
                    g = proj1[:, 32 + 4 * hd:36 + 4 * hd, :]
                    step(nc.vector.tensor_tensor(g, g, spread(rstd[:, 0:S1], 4), ALU.mult))
                    nc.vector.tensor_tensor(ret_o, g, PS[:, first:first + 2, :].rearrange("p b (e t) -> p (b e) t", t=S1), ALU.mult)\
                        .then_inc(R["gated"], 1)
                    dve.wait_ge(R["gated"], 4 * j + hd + 1)
                    hi = proj1_r[:, 32 + 4 * hd:36 + 4 * hd, :]
                    step(nc.vector.tensor_copy(hi, ret_o))
                    for n in range(2):
                        last = nc.vector.tensor_tensor(proj1_r[:, 8 * n + 2 * hd:8 * n + 2 * hd + 2, :], ret_o[:, 2 * n:2 * n + 2, :],
                                                       hi[:, 2 * n:2 * n + 2, :].bitcast(F32), ALU.subtract)
                    last.then_inc(R["split"], 1)
                    dve.wait_ge(R["split"], 4 * j + hd + 1)

            def conv():
                C = conv_sem
                phase = ph["conv_in"]

                def unit(i, u):
                    if u % 2 == 0:
                        return
                    q = u // 2
                    wait_unit(phase, i, u)
                    dve.wait_ge(gate_ready, i * 2 + (phase.pair0 + q + 1))
                    stt(conv_u[:, i * 2 + q, :], PS[:, u, 0:S1], param("conv_b_in", 0, DC)[:, bass.ds(i * 2 + q, 1)],
                        silu[:, q, 0:S1], ALU.add, ALU.mult).then_inc(pair_done, 1)
                stream(phase, unit)
                dve.wait_ge(pair_done, pairs_done(phase))
                taps = [CONV_PAD] + [t for t in range(CONV_TAPS) if t != CONV_PAD]
                for t in taps:
                    for c in range(DC):
                        w = param("conv_w_dw", c * CONV_TAPS + t)
                        lo, hi = max(0, CONV_PAD - t), min(S1, S1 + CONV_PAD - t)
                        src = conv_u[:, c, lo + t - CONV_PAD:hi + t - CONV_PAD]
                        if t == CONV_PAD:
                            last = nc.vector.tensor_scalar(conv_acc[:, c, :], src, w, param("conv_b_dw", c), ALU.mult, ALU.add)
                        else:
                            last = stt(conv_acc[:, c, lo:hi], src, w, conv_acc[:, c, lo:hi], ALU.mult, ALU.add)
                    if t != taps[-1]:
                        step(last)
                last.then_inc(C["acc_ready"], 1)
                dve.wait_ge(C["mean_ready"], 1)
                nc.vector.tensor_tensor(conv_acc, conv_acc, spread(PS[:, 4, 0:S1], DC), ALU.subtract).then_inc(C["centered"], 1)
                dve.wait_ge(C["rstd_ready"], 1)
                nc.vector.tensor_tensor(conv_sq, conv_acc, spread(rstd[:, 0:S1], DC), ALU.mult).then_inc(C["scaled"], 1)
                for c in range(DC):
                    dve.wait_ge(C["mixed"], c + 1)
                    step(nc.vector.tensor_copy(conv_hi[:, c, :], conv_mix[:, c, :]))
                    nc.vector.tensor_tensor(conv_lo[:, c, :], conv_mix[:, c, :], conv_hi[:, c, :].bitcast(F32), ALU.subtract)\
                        .then_inc(C["split"], 1)

            def attention(half):
                A = att_sem
                base = half * (DC // 2)
                mask = const("att_mask").rearrange("p (n k) -> p n k", k=S1)
                mask_of = ((0, 1, 2), (3, 1, 2))
                dve.wait_ge(out_evacuated, evacuated(ph[f"att_in{half}"]))
                cos, sin = rope_cos[:, 0:S1], rope_sin[:, 0:S1]
                if half == 0:
                    dve.sem_inc(A["roped"], 3)
                with dve.Fori(0, DC // 2) as i:
                    for g in range(3):
                        dve.wait_ge(A["rotated"], i * 3 + (3 * base + g + 1))
                        nc.vector.tensor_tensor(att_t[:, 2 * g, :], PS[:, g, 0:S1], sin, ALU.mult)
                        nc.vector.tensor_tensor(att_t[:, 2 * g + 1, :], PS[:, g, S1:512], sin, ALU.mult)
                        nc.vector.tensor_tensor(att_q[:, g, :], proj1[:, i + g * 12, :], cos, ALU.mult)
                        nc.vector.tensor_tensor(att_k[:, g, :], proj1[:, i + (g * 12 + 4), :], cos, ALU.mult).then_inc(att_rot, 1)
                        dve.wait_ge(att_rot, i * 3 + (3 * base + g + 1))
                        nc.vector.tensor_tensor(att_q[:, g, :], att_q[:, g, :], att_t[:, 2 * g, :], ALU.add)
                        nc.vector.tensor_tensor(att_k[:, g, :], att_k[:, g, :], att_t[:, 2 * g + 1, :], ALU.add).then_inc(A["roped"], 1)
                    dve.wait_ge(A["v_turned"], i + (base + 1))
                    nc.vector.tensor_copy(att_vn[:, 0:4, :].rearrange("p a b -> p (a b)"), PS[:, 3, :])
                    nc.vector.tensor_copy(att_vn[:, 4:6, :].rearrange("p a b -> p (a b)"), PS[:, 4, 0:S1]).then_inc(A["v_ready"], 1)

                    def maxima(u):
                        it, m = u % 2, att_max[:, u % 2, :]
                        dve.wait_ge(A["scores_ready"], i * 4 + (4 * base + u + 1))
                        dve.sem_inc(wait_taken, 1)
                        for g in range(3):
                            b = (5 if u % 2 == 0 else 0) + g // 2
                            last = nc.vector.tensor_tensor_reduce(
                                att_s[:, u % 2, g * S1:(g + 1) * S1], PS[:, b, (g % 2) * S1:(g % 2 + 1) * S1],
                                mask[:, mask_of[it][g], :], 1.0, -3e38, ALU.add, ALU.max, m[:, g:g + 1])
                        last.then_inc(att_m1, 1)
                        dve.wait_ge(att_m1, i * 4 + (4 * base + u + 1))
                        nc.vector.tensor_reduce(m[:, 3:4], m[:, 0:3], AX, ALU.max).then_inc(att_m2, 1)
                        dve.wait_ge(att_m2, i * 4 + (4 * base + u + 1))
                        nc.vector.tensor_scalar(m[:, 4:5], m[:, 3:4], -0.125, None, ALU.mult).then_inc(A["max_ready"], 1)

                    maxima(0)
                    for u in range(4):
                        if u < 3:
                            maxima(u + 1)
                        dve.wait_ge(A["p_ready"], i * 4 + (4 * base + u + 1))
                        nc.vector.reciprocal(att_rden[:, u % 2:u % 2 + 1], att_den[:, u % 2:u % 2 + 1]).then_inc(A["den_ready"], 1)
                        dve.wait_ge(A["p_turned"], i * 4 + (4 * base + u + 1))
                        nc.vector.tensor_copy(att_pt[:, u % 2, 0:512], PS[:, 7, :]).then_inc(A["pt_ready"], 1)
                    dve.wait_ge(A["o_turned"], i + (base + 1))
                    dve.sem_inc(wait_taken, 1)
                    nc.vector.tensor_copy(att_hi[:, i + base, :], PS[:, 6, S1:512]).then_inc(att_rounded, 1)
                    dve.wait_ge(att_rounded, i + (base + 1))
                    nc.vector.tensor_tensor(att_lo[:, i + base, :], PS[:, 6, S1:512], att_hi[:, i + base, :].bitcast(F32),
                                            ALU.subtract).then_inc(A["mixed"], 1)

            def split_gates():
                dve.wait_ge(meta_loaded, 32)
                step(nc.vector.tensor_copy(gates_hi[:, :, :], w_gates[:, :, :]))
                nc.vector.tensor_tensor(gates_lo[:, :, :], w_gates[:, :, :], gates_hi[:, :, :].bitcast(F32), ALU.subtract)\
                    .then_inc(gates_split, 1)

            def mlstm_rows():
                A = ab_sem
                dve.wait_ge(A["gate_sums"], 1)
                bias_i, bias_f = (param("if_bias", n)[0:A_HEADS, :] for n in range(2))
                nc.vector.tensor_scalar(r_in, PS[0:A_HEADS, 5, 0:S2], bias_i, None, ALU.add)
                step(nc.vector.tensor_scalar(r_f, PS[0:A_HEADS, 6, 0:S2], bias_f, None, ALU.add))
                stt(r_e, r_f, -1.0, r_f, ALU.mult, ALU.min).then_inc(A["log_in"], 1)
                dve.wait_ge(A["log_ready"], 1)
                step(stt(r_lf, r_f, 0.0, r_l, ALU.min, ALU.subtract))
                step(nc.vector.memset(r_sum, 1.0))
                step(nc.vector.tensor_tensor_scan(r_F, r_sum, r_lf, 0.0, ALU.mult, ALU.add))
                step(nc.vector.tensor_tensor(r_a, r_in, r_F, ALU.subtract))
                step(nc.vector.tensor_tensor_scan(r_m, r_sum, r_a, 0.0, ALU.mult, ALU.max))
                nc.vector.tensor_tensor(r_sum, r_F, r_m, ALU.add).then_inc(A["floor_in"], 1)
                dve.wait_ge(A["floor_in"], 1)
                dve.sem_inc(A["rows_ready"], 1)

            def mlstm():
                A = ab_sem
                dve.wait_ge(A["turned"], 1)
                for st, (_, tl) in enumerate(TILES2):
                    last = nc.vector.tensor_copy(ab_col[0:tl, st, :], PS[0:tl, 7, st * 4:st * 4 + 4])
                last.then_inc(A["cols_ready"], 1)

            def mlstm_values():
                A = ab_sem
                for st, (_, tl) in enumerate(TILES2):
                    dve.wait_ge(A["v_turned"], st + 1)
                    nc.vector.tensor_copy(ab_v[0:tl, st, :], PS[0:tl, 2 * (st % 2):2 * (st % 2) + 2, :].rearrange("p b f -> p (b f)"))\
                        .then_inc(A["v_ready"], 1)

            def mlstm_heads():
                A = ab_sem
                dve.wait_ge(consts2_loaded, 48)
                causal = const("causal_T").rearrange("p (s t) -> p s t", s=3)
                for hd in range(A_HEADS):
                    dve.wait_ge(A["run_ready"], hd + 1)
                    if hd >= 1:
                        dve.wait_ge(A["w_ready"], 3 * hd)
                    for st, (_, tl) in enumerate(TILES2):
                        nc.vector.tensor_tensor(ab_t[0:tl, st, :], causal[0:tl, st, :], PS[0:tl, 0, 0:S2], ALU.add)\
                            .then_inc(A["shifted"], 1)
                    for st, (_, tl) in enumerate(TILES2):
                        dve.wait_ge(A["scores_ready"], 3 * hd + st + 1)
                        dve.wait_ge(A["w_ready"], 3 * hd + st + 1)
                        stt(ab_p[0:tl, 3 * (hd % 2) + st, :], PS[0:tl, 1 + st, 0:S2], A_DIM ** -0.5, ab_w[0:tl, st, :],
                            ALU.mult, ALU.mult).then_inc(A["p_ready"], 1)
                    den, rec = ab_den[:, 0, :], ab_den[:, 1, :]
                    dve.wait_ge(A["den_abs"], hd + 1)
                    step(nc.vector.tensor_tensor(den, den, PS[:, 7, 0:S2], ALU.max))
                    step(nc.vector.reciprocal(rec, den))
                    for c in range(2):
                        last = nc.vector.tensor_tensor(ab_hh[:, c, :], rec, PS[:, 5 + c, 0:S2], ALU.mult)
                    step(last)
                    nc.vector.tensor_tensor(ab_hh, ab_hh, proj2[:, 24 + 2 * hd:26 + 2 * hd, :], ALU.mult).then_inc(A["h_ready"], 1)
                    dve.wait_ge(A["rstd_ready"], hd + 1)
                    for c in range(2):
                        last = stt(ab_hh[:, c, :], ab_hh[:, c, :], param("mlstm_norm", 2 * hd + c), ab_r[:, hd % 2, :],
                                   ALU.mult, ALU.mult)
                    step(last)
                    hi, lo = proj2_r[:, 2 * hd:2 * hd + 2, :], proj2_r[:, 8 + 2 * hd:10 + 2 * hd, :]
                    step(nc.vector.tensor_copy(hi, ab_hh))
                    nc.vector.tensor_tensor(lo, ab_hh, hi.bitcast(F32), ALU.subtract).then_inc(A["mixed"], 1)
                    dve.wait_ge(A["mixed"], hd + 1)

            def softplus():
                L = lru_sem
                lam = param("lru_lambda", 0, DC)
                neg, e, z, z2 = (lam_t[:, n, :] for n in range(4))
                dve.wait_ge(L["softplus_ready"], 1)
                step(nc.vector.tensor_scalar(z, e, 2.0, None, ALU.add))
                step(nc.vector.reciprocal(z, z))
                step(nc.vector.tensor_tensor(z, z, e, ALU.mult))
                step(nc.vector.tensor_tensor(z2, z, z, ALU.mult))
                step(nc.vector.memset(e, 1.0 / 21))
                for n in range(19, 0, -2):
                    step(nc.vector.tensor_tensor(e, e, z2, ALU.mult))
                    step(nc.vector.tensor_scalar(e, e, 1.0 / n, None, ALU.add))
                step(nc.vector.tensor_tensor(e, e, z, ALU.mult))
                step(nc.vector.tensor_scalar(neg, lam, -1.0, 0.0, ALU.mult, ALU.max))
                step(stt(e, e, 2.0, neg, ALU.mult, ALU.add))
                step(nc.vector.tensor_scalar(lam8, e, -LRU_C, None, ALU.mult))

            def lru_conv():
                L = lru_sem
                for t in range(LRU_TAPS - 1, -1, -1):
                    back = LRU_TAPS - 1 - t
                    for c in range(DC):
                        w = param("lru_conv_w", c * LRU_TAPS + t)
                        if back == 0:
                            last = nc.vector.tensor_scalar(lru_xc[:, c, :], lru_xb[:, c, :], w, param("lru_conv_b", c), ALU.mult, ALU.add)
                        else:
                            last = stt(lru_xc[:, c, back:S2], lru_xb[:, c, 0:S2 - back], w, lru_xc[:, c, back:S2], ALU.mult, ALU.add)
                    if t:
                        step(last)
                last.then_inc(L["conv_ready"], 1)

            def lru():
                L = lru_sem
                dve.wait_ge(L["gates_ready"], 2 * DC)
                for c in range(DC):
                    last = nc.vector.tensor_scalar(lru_r[:, c, :], lru_r[:, c, :], lam8[:, c:c + 1], None, ALU.mult)
                last.then_inc(L["loga_ready"], 1)
                step(nc.vector.tensor_tensor(lru_i[:, :, :], lru_i[:, :, :], lru_xc[:, :, :], ALU.mult))
                dve.wait_ge(L["a_ready"], 1)
                step(nc.vector.tensor_scalar(y[:, :, :], lru_r[:, :, :], 1.0, None, ALU.add))
                step(nc.vector.reciprocal(y[:, :, :], y[:, :, :]))
                nc.vector.tensor_tensor(lru_r[:, :, :], lru_r[:, :, :], y[:, :, :], ALU.mult).then_inc(L["root_in"], 1)
                dve.wait_ge(L["root_ready"], 1)
                step(nc.vector.tensor_tensor(lru_i[:, :, :], lru_i[:, :, :], lru_r[:, :, :], ALU.mult))
                for c in range(DC):
                    last = nc.vector.tensor_tensor_scan(y[:, c, :], lru_a[:, c, :], lru_i[:, c, :], 0.0, ALU.mult, ALU.add)
                step(last)
                step(nc.vector.tensor_tensor(lru_r[:, :, :], lru_gate, lru_gate, ALU.mult))
                step(nc.vector.tensor_scalar(lru_r[:, :, :], lru_r[:, :, :], 0.044715, 1.0, ALU.mult, ALU.add))
                nc.vector.tensor_tensor(lru_r[:, :, :], lru_r[:, :, :], lru_gate, ALU.mult).then_inc(L["gelu_in"], 1)
                dve.wait_ge(L["gelu_ready"], 1)
                for c in range(DC):
                    last = stt(lru_r[:, c, :], lru_r[:, c, :], 1.0, lru_gate[:, c, :], ALU.add, ALU.mult)
                step(last)
                for c in range(DC):
                    last = stt(lru_o[:, c, :], y[:, c, :], 0.5, lru_r[:, c, :], ALU.mult, ALU.mult)
                step(last)
                hi, lo = proj2_r[:, 32:40, :], proj2_r[:, 40:48, :]
                step(nc.vector.tensor_copy(hi, lru_o))
                nc.vector.tensor_tensor(lo, lru_o, hi.bitcast(F32), ALU.subtract).then_inc(L["done"], 1)

            def lambdas():
                A = c_sem
                for n in range(2):
                    last = nc.vector.tensor_tensor_reduce(lam_s[:, 8 + C_QK * n:8 + C_QK * (n + 1)], param("c_lambda", 2 * n * C_QK, C_QK),
                                                          param("c_lambda", (2 * n + 1) * C_QK, C_QK), 1.0, 0.0, ALU.mult, ALU.add,
                                                          lam_s[:, n:n + 1])
                last.then_inc(A["lam_in"], 1)
                nc.vector.tensor_scalar(subln, param("subln"), 1.0 - LAMBDA_INIT, None, ALU.mult)
                dve.wait_ge(A["lam_exp"], 1)
                step(nc.vector.tensor_tensor(lam_s[:, 4:5], lam_s[:, 3:4], lam_s[:, 2:3], ALU.subtract))
                step(nc.vector.tensor_scalar(neg_lam, lam_s[:, 4:5], -LAMBDA_INIT, None, ALU.add))

            def diff_attention():
                A = c_sem
                causal = const("causal").rearrange("p (s t) -> p s t", s=3)
                dve.wait_ge(out_evacuated, evacuated(ph["c_in"]))
                dve.sem_inc(A["roped"], 1)
                dve.sem_inc(A["mixed"], 1)
                with dve.Fori(0, C_HEADS) as i:
                    dve.wait_ge(A["rotated"], i + 1)
                    nc.vector.tensor_tensor(c_t[:, 0, :], PS[:, 0, 0:S2], rope_sin, ALU.mult)
                    nc.vector.tensor_tensor(c_t[:, 1, :], PS[:, 1, 0:S2], rope_sin, ALU.mult)
                    nc.vector.tensor_tensor(c_q, proj2[:, i, :], rope_cos, ALU.mult)
                    nc.vector.tensor_tensor(c_k, proj2[:, i + 8, :], rope_cos, ALU.mult).then_inc(c_rot, 1)
                    dve.wait_ge(c_rot, i + 1)
                    nc.vector.tensor_tensor(c_q, c_q, c_t[:, 0, :], ALU.add)
                    nc.vector.tensor_tensor(c_k, c_k, c_t[:, 1, :], ALU.add).then_inc(A["roped"], 1)
                    dve.wait_ge(A["v_turned"], i + 1)
                    nc.vector.tensor_copy(c_vn[:, 0:2, :].rearrange("p a b -> p (a b)"), PS[:, 2, 0:2 * P])
                    nc.vector.tensor_copy(c_vn[0:META, 2, :], PS[0:META, 2, 2 * P:3 * P]).then_inc(A["v_ready"], 1)

                    def maxima(u):
                        t0, tl = TILES2[u]
                        m = c_max[0:tl, u % 2, :]
                        dve.wait_ge(A["scores_ready"], i * 3 + (u + 1))
                        dve.sem_inc(wait_taken, 1)
                        for e in range(2):
                            last = nc.vector.tensor_tensor_reduce(
                                c_s[0:tl, 2 * (u % 2) + e, 0:t0 + tl], PS[0:tl, 3 + 2 * (u % 2) + e, 0:t0 + tl],
                                causal[0:tl, u, 0:t0 + tl], 1.0, -3e38, ALU.add, ALU.max, m[:, e:e + 1])
                        last.then_inc(c_m1, 1)
                        dve.wait_ge(c_m1, i * 3 + (u + 1))
                        nc.vector.tensor_scalar(m[:, 2:4], m[:, 0:2], -0.125, None, ALU.mult).then_inc(A["max_ready"], 1)

                    maxima(0)
                    for u, (t0, tl) in enumerate(TILES2):
                        if u < 2:
                            maxima(u + 1)
                        n = t0 + tl
                        den = c_den[0:tl, u % 2, :]
                        p0, p1 = c_p[0:tl, 2 * (u % 2), 0:n], c_p[0:tl, 2 * (u % 2) + 1, 0:n]
                        dve.wait_ge(A["p_ready"], i * 3 + (u + 1))
                        nc.vector.reciprocal(den, den).then_inc(c_d1, 1)
                        dve.wait_ge(c_d1, i * 3 + (u + 1))
                        nc.vector.tensor_scalar(p1, p1, den[:, 1:2], neg_lam[0:tl, :], ALU.mult, ALU.mult).then_inc(c_d2, 1)
                        dve.wait_ge(c_d2, i * 3 + (u + 1))
                        stt(c_pd[0:tl, u % 2, 0:n], p0, den[:, 0:1], p1, ALU.mult, ALU.add).then_inc(A["pd_ready"], 1)
                    dve.wait_ge(A["p_turned"], i * 3 + 3)
                    for st, (s0, sl) in enumerate(TILES2):
                        last = nc.vector.tensor_copy(c_pt[0:sl, st, s0:S2], PS[0:sl, (7, 0, 1)[st], s0:S2])
                    last.then_inc(A["pt_ready"], 1)
                    dve.wait_ge(A["rstd_ready"], i + 1)
                    stt(c_o, PS[:, 2, 0:S2], subln, c_r, ALU.mult, ALU.mult).then_inc(c_scaled, 1)
                    dve.wait_ge(c_scaled, i + 1)
                    dve.sem_inc(wait_taken, 1)
                    nc.vector.tensor_copy(c_hi[:, i, :], c_o).then_inc(c_rounded, 1)
                    dve.wait_ge(c_rounded, i + 1)
                    nc.vector.tensor_tensor(c_lo[:, i, :], c_o, c_hi[:, i, :].bitcast(F32), ALU.subtract).then_inc(A["mixed"], 1)

            def final_norm():
                dve.wait_ge(rstd_ready, 21)
                for c in range(DC):
                    stt(y[:, c, :], h[:, c, :], param("norm_final", c), rstd[:, :], ALU.mult, ALU.mult).then_inc(final_ready, 1)

            dve.sem_inc(pair_done, FREE_PAIRS)
            dve.sem_inc(y_added, FREE_SQUARES)
            dve.sem_inc(part_ready, 2)
            dve.wait_ge(consts_loaded, 48)
            dve.wait_ge(x_loaded, 16)
            lam = param("lru_lambda", 0, DC)
            stt(lam_t[:, 0, :], lam, -1.0, lam, ALU.mult, ALU.min).then_inc(lru_sem["lam_ready"], 1)
            split_gates()
            for layer in range(DEPTH):
                j = layer // 3
                pre_norm(4 * layer, 2 * layer, x, S1, "norm_w", (4 * layer) * DC)
                if layer == 0:
                    split(phases[0], 0, 0)
                    exponents(0)
                    softplus()
                if layer % 3 == 0:
                    rotate(j, ph[f"ret_qk{layer}"])
                    stream(ph[f"ret_v{layer}"])
                    values(j)
                    stream(ph[f"ret_g{layer}"])
                    retention(j, layer)
                    sum_squares(4 * layer + 1, ph[f"ret_out{layer}"], S1)
                elif layer % 3 == 1:
                    conv()
                    sum_squares(4 * layer + 1, ph["conv_out"], S1)
                else:
                    for half in range(2):
                        stream(ph[f"att_in{half}"])
                        attention(half)
                    sum_squares(4 * layer + 1, ph["att_out"], S1)
                post_norm(4 * layer + 1, (4 * layer + 1) * DC)
                pre_norm(4 * layer + 2, 2 * layer + 1, x, S1, "norm_w", (4 * layer + 2) * DC)
                ffn_pairs(ph[f"ffn_in{layer}"])
                if layer == 2:
                    exponents(1)
                sum_squares(4 * layer + 3, ph[f"ffn_out{layer}"], S1)
                post_norm(4 * layer + 3, (4 * layer + 3) * DC)
            pre_norm(16, 2 * DEPTH, h, S2, "norm_mix", 0)
            stream(ph["ab_qkv"])
            mlstm_rows()
            stream(ph["ab_o"])
            stream(ph["ab_x"])
            mlstm_values()
            mlstm()
            lru_conv()
            mlstm_heads()
            lru()
            add_to_h(17, ph["ab_out"])
            pre_norm(17, 2 * DEPTH + 1, h, S2, "norm_mlp", 0)
            square_relu(ph["mlp_in0"])
            add_to_h(18, ph["mlp_out0"])
            pre_norm(18, 2 * DEPTH + 2, h, S2, "norm_mix", DC)
            lambdas()
            stream(ph["c_in"])
            diff_attention()
            add_to_h(19, ph["c_out"])
            pre_norm(19, 2 * DEPTH + 3, h, S2, "norm_mlp", DC)
            square_relu(ph["mlp_in1"])
            add_to_h(20, ph["mlp_out1"])
            final_norm()



def kernel(**inputs):
    import concourse.bacc as bacc
    from concourse.bass_utils import run_bass_kernel_spmd as run

    a = {k: np.asarray(v) for k, v in inputs.items()}

    def features(v):
        return v.reshape(-1, P).T

    def units(w, halves=1):
        k, m = w.shape
        t = k // P // halves
        return np.ascontiguousarray(w.reshape(halves, t, P, m // P, P).transpose(3, 0, 2, 1, 4).reshape(m // P * halves, P, t * P))

    def interleaved(w):
        u = units(w)
        n = u.shape[0] // 2
        return np.ascontiguousarray(np.stack([u[:n], u[n:]], 1).reshape(u.shape))

    (const_a, at_a), (const_b, at_b), (const_c, at_c) = constants()
    arrays = {"const_a": const_a, "const_b": const_b, "const_c": const_c}
    arrays["x"] = np.ascontiguousarray(a["x"][0].T.reshape(DC, P, S1).transpose(1, 0, 2))
    arrays["meta"] = np.ascontiguousarray(a["meta_tokens_2"].T.reshape(DC, P, META).transpose(1, 0, 2))
    for layer in range(DEPTH):
        j = layer // 3
        if layer % 3 == 0:
            u = units(a["ret_w_in"][j])
            arrays[f"ret_qk{layer}"] = np.ascontiguousarray(u[:16])
            arrays[f"ret_v{layer}"] = np.ascontiguousarray(u[16:32])
            arrays[f"ret_g{layer}"] = np.ascontiguousarray(u[32:])
            arrays[f"ret_out{layer}"] = units(a["ret_w_out"][j], 2)
        elif layer % 3 == 1:
            w = a["conv_w_in"][0]
            arrays["conv_in"] = interleaved(np.concatenate([w[:, D:], w[:, :D]], 1))
            arrays["conv_out"] = units(a["conv_w_out"][0])
        else:
            u = units(a["attn_w_in"][0]).reshape(9, 2, DC // 2, P, D)
            arrays["att_in0"], arrays["att_in1"] = (np.ascontiguousarray(u[:, n].reshape(-1, P, D)) for n in range(2))
            arrays["att_out"] = units(a["attn_w_out"][0])
        arrays[f"ffn_in{layer}"] = interleaved(a["ffn_w_in"][layer])
        arrays[f"ffn_out{layer}"] = units(a["ffn_w_out"][layer], 2)
    w = a["ab_w_in_2"][0]
    g0 = 4 * D
    u = units(np.concatenate([w[:, :g0], w[:, g0 + 2 * A_HEADS:]], 1))
    arrays["ab_qkv"], arrays["ab_o"], arrays["ab_x"] = (np.ascontiguousarray(v) for v in (u[:24], u[24:32], u[32:]))
    arrays["ab_gates"] = np.ascontiguousarray(w[:, g0:g0 + 2 * A_HEADS].reshape(DC, P, 2 * A_HEADS).transpose(1, 0, 2))
    arrays["ab_out"] = units(a["ab_w_out_2"][0], 2)
    arrays["c_in"] = units(a["c_w_in_2"][0])
    arrays["c_out"] = units(a["c_w_out_2"][0])
    for layer in range(2):
        arrays[f"mlp_in{layer}"] = units(a["mlp_w1_2"][layer])
        arrays[f"mlp_out{layer}"] = units(a["mlp_w2_2"][layer], 4)
    arrays["lru_w_r"] = np.ascontiguousarray(a["lru_w_r_2"][0].transpose(1, 0, 2))
    arrays["lru_w_i"] = np.ascontiguousarray(a["lru_w_i_2"][0].transpose(1, 0, 2))

    taps = lambda w, n: w.reshape(n, DC, P).transpose(2, 1, 0).reshape(P, DC * n)
    if_bias = np.zeros((P, 2), np.float32)
    if_bias[:A_HEADS] = a["ab_if_bias_2"][0].reshape(2, A_HEADS).T
    cols = {
        "norm_w": features(a["norm_w"].reshape(-1)), "conv_b_in": features(a["conv_b_in"][0]),
        "conv_w_dw": taps(a["conv_w_dw"][0], CONV_TAPS), "conv_b_dw": features(a["conv_b_dw"][0]),
        "conv_ln_g": features(a["conv_ln_g"][0]), "conv_ln_b": features(a["conv_ln_b"][0]),
        "conv_b_out": features(a["conv_b_out"][0]), "norm_mix": features(a["norm_mix_2"].reshape(-1)),
        "norm_mlp": features(a["norm_mlp_2"].reshape(-1)), "norm_final": features(a["norm_final_2"]),
        "mlstm_norm": features(a["mlstm_norm_2"][0]), "lru_conv_w": taps(a["lru_conv_w_2"][0], LRU_TAPS),
        "lru_conv_b": features(a["lru_conv_b_2"][0]), "lru_b_r": features(a["lru_b_r_2"][0]),
        "lru_b_i": features(a["lru_b_i_2"][0]), "lru_lambda": features(a["lru_lambda_2"][0]),
        "subln": features(a["c_subln_2"][0]),
        "decay": np.broadcast_to(a["ret_log1m_decay"].reshape(1, -1), (P, 16)), "if_bias": if_bias,
        "c_lambda": np.broadcast_to(a["c_lambda_2"][0].reshape(1, -1), (P, 4 * C_QK)),
    }
    assert all(cols[name].shape[1] == n for name, n in PARAMS)
    arrays["params"] = np.ascontiguousarray(np.concatenate([cols[name] for name, _ in PARAMS], 1))

    nc = bacc.Bacc("TRN2", target_bir_lowering=False, num_devices=1)
    dram = {k: nc.dram_tensor("in_" + k, v.shape, F32, kind="ExternalInput").ap() for k, v in arrays.items()}
    out = nc.dram_tensor("out", [P, DC, S1], F32, kind="ExternalOutput").ap()
    build(nc, dram, out, (at_a, at_b, at_c))
    got = run(nc, [{"in_" + k: v for k, v in arrays.items()}], core_ids=[0]).results[0]["out"]
    return np.ascontiguousarray(np.asarray(got).transpose(2, 1, 0).reshape(1, S1, D))
```

```python
from contextlib import ExitStack
import math

import concourse.bass as bass
from concourse import mybir
import numpy as np

F32 = mybir.dt.float32
F32R = mybir.dt.float32r
ALU = mybir.AluOpType
ACT = mybir.ActivationFunctionType
AX = mybir.AxisListType.X

P = 128
D = 1024
DC = D // P
S1 = 256
META = 16
S2 = S1 + META
DEPTH = 4
RMS_EPS, LN_EPS = 1e-6, 1e-5

RET_HEADS, RET_QK, RET_V = 4, 256, 512
FFN = 2816 // P
CONV_TAPS, CONV_PAD = 31, 15
PE_TAPS = 13
GROUPS = ((128, 1), (512, 4), (2048, 16))
ATT_IN = 3 * 3 * DC
A_HEADS, A_DIM = 4, 256
AB_IN = 6 * DC
LRU_TAPS, LRU_C = 4, 8.0
C_HEADS, C_QK = 8, 64
C_IN = 3 * DC
MLP = 32
LAMBDA_INIT = 0.8 - 0.6 * math.exp(-0.3)
ROPE_THETA, RET_BASE = 500000.0, 10000.0
BIG = 1e30
TILES2 = ((0, 128), (128, 128), (256, 16))
SLOTS = 4
SUB = 4
SUBS = 4
SLOT_TILES = 11


class Phase:

    def __init__(self, name, units, tiles=8, upo=1, pairs=False, body=0):
        self.name, self.units, self.tiles, self.upo, self.pairs = name, units, tiles, upo, pairs
        self.outs = units // upo
        self.body = body or max(SLOTS, 2 * upo)
        self.slots = next(n for n in (4, 3) if self.body % n == 0)
        self.sps = -(-tiles // SUB)
        self.subs = next(n for n in (4, 6) if self.body * self.sps % n == 0)


def plan():
    seq = []
    for layer in range(DEPTH):
        if layer % 3 == 0:
            seq += [Phase(f"ret_qk{layer}", 16), Phase(f"ret_v{layer}", 16), Phase(f"ret_g{layer}", 16), Phase(f"ret_out{layer}", 16, 8, 2)]
        elif layer % 3 == 1:
            seq += [Phase("conv_in", 16, pairs=True), Phase("conv_out", 8)]
        else:
            seq += [Phase("att_in", ATT_IN, body=9), Phase("att_out", 8)]
        seq += [Phase(f"ffn_in{layer}", 2 * FFN, pairs=True), Phase(f"ffn_out{layer}", 16, FFN // 2, 2)]
    seq += [Phase("ab_xb", DC), Phase("ab_gate", DC), Phase("ab_qkvo", 4 * DC, body=8), Phase("ab_out", 16, 8, 2)]
    seq += [Phase("mlp_in0", MLP), Phase("mlp_out0", MLP, 8, 4)]
    seq += [Phase("c_in", C_IN, body=3), Phase("c_out", 8)]
    seq += [Phase("mlp_in1", MLP), Phase("mlp_out1", MLP, 8, 4)]
    out = pair = sub = 0
    loads, split = [0] * SLOTS, [0] * SLOTS
    for ph, after in zip(seq, seq[1:] + [None]):
        ph.out0, ph.pair0, ph.sub0, ph.after = out, pair, sub, after
        ph.loads0, ph.split0 = list(loads), list(split)
        for s in range(ph.slots):
            loads[s] += ph.units // ph.slots
            split[s] = sub + (ph.units - ph.slots + s + 1) * ph.sps
        sub += ph.units * ph.sps
        if ph.pairs:
            pair += ph.units // 2
        else:
            out += ph.outs
    return seq



def constants():
    p = np.arange(P)
    first, second = {}, {}
    first["ident"] = np.eye(P)
    first["mean"] = np.full((P, P), 1.0 / D)
    first["ones"] = np.ones((P, P))
    swap = np.zeros((P, P))
    half = 8
    for base in (0, 64):
        for i in range(half):
            swap[base + half + i, base + i] = -1.0
            swap[base + i, base + half + i] = 1.0
    first["swap"] = swap
    inv = (np.float32(1.0) / np.float32(RET_BASE) ** np.linspace(0.0, 1.0, RET_QK // 2, dtype=np.float32)).astype(np.float32)
    ang = (np.arange(S1, dtype=np.float32)[None, :] * inv[:, None]).astype(np.float32).astype(np.float64)
    first["ret_cos"], first["ret_sin"] = np.cos(ang), np.sin(ang)
    inv = (np.float32(ROPE_THETA) ** (-np.arange(0, 16, 2, dtype=np.float32) / np.float32(16))).astype(np.float32)
    ang = (np.arange(S2, dtype=np.float32)[None, :] * inv[:, None]).astype(np.float32).astype(np.float64)
    cos, sin = np.ones((P, S2)), np.zeros((P, S2))
    for base in (0, 64):
        for i in range(16):
            cos[base + i], sin[base + i] = np.cos(ang[i % 8]), np.sin(ang[i % 8])
    first["rope_cos"], first["rope_sin"] = cos, sin
    first["rms_eps"], first["ln_eps"] = np.full((P, 1), RMS_EPS), np.full((P, 1), LN_EPS)
    first["one"] = np.ones((P, 1))
    n = np.arange(S1)
    m = np.arange(2)[:, None] * P + p[None, :]
    gap = n[None, None, :] - m[:, :, None]
    first_b = {}
    first_b["after"] = np.concatenate([np.maximum(gap[t], 0) for t in range(2)], 1)
    first_b["before"] = np.concatenate([np.maximum(-gap[t], 0) for t in range(2)], 1)
    masks = []
    for it in range(2):
        q = it * P + p[:, None]
        k = np.arange(S1)[None, :]
        for window, dil in GROUPS[:1] if it else GROUPS:
            radius = window // (2 * dil)
            live = ((q - k) % dil == 0) & (np.abs(q // dil - k // dil) <= radius)
            masks.append(np.where(live, 0.0, -BIG))
            assert dil == 1 or (live == ((q - k) % dil == 0)).all()
    first_b["att_mask"] = np.concatenate(masks, 1)
    pos = np.arange(S2)[None, :]
    row = [t0 + p[:, None] for t0, _ in TILES2]
    second["causal_T"] = np.concatenate([np.where(r > pos, BIG, 0.0) for r in row], 1)
    second["causal"] = np.concatenate([np.where(pos > r, -BIG, 0.0) for r in row], 1)
    sel = np.zeros((P, A_HEADS * P))
    for h in range(A_HEADS):
        sel[h, h * P:(h + 1) * P] = 1.0
    second["sel"] = sel

    def packed(parts):
        where, at = {}, 0
        for name, a in parts.items():
            where[name] = (at, a.shape[1])
            at += a.shape[1]
        return np.ascontiguousarray(np.concatenate(list(parts.values()), 1), dtype=np.float32), where

    return packed(first), packed(first_b), packed(second)


PARAMS = (
    ("norm_w", DEPTH * 4 * DC), ("conv_b_in", 2 * DC), ("conv_w_dw", DC * CONV_TAPS), ("conv_b_dw", DC),
    ("conv_ln_g", DC), ("conv_ln_b", DC), ("conv_b_out", DC), ("norm_mix", 2 * DC), ("norm_mlp", 2 * DC),
    ("norm_final", DC), ("mlstm_norm", DC), ("lru_conv_w", DC * LRU_TAPS), ("lru_conv_b", DC), ("lru_b_r", DC),
    ("lru_b_i", DC), ("lru_lambda", DC), ("subln", 1), ("decay", 2 * 2 * RET_HEADS), ("if_bias", 2),
    ("c_lambda", 4 * C_QK),
)
PARAM_AT = {}
_at = 0
for _name, _n in PARAMS:
    PARAM_AT[_name] = _at
    _at += _n
N_PARAMS = _at


def build(nc, dram, out, const_at):
    at_a, at_b, at_c = const_at
    phases = plan()
    ph = {x.name: x for x in phases}
    with ExitStack() as ctx:
        def sb(name, shape):
            return ctx.enter_context(nc.sbuf_tensor(name, shape, F32))

        def sbr(name, shape):
            return ctx.enter_context(nc.sbuf_tensor(name, shape, F32R))

        def sem(name):
            return ctx.enter_context(nc.semaphore(name))

        raw = [sb(f"weights{s}", [P, SLOT_TILES, P]) for s in range(SLOTS)]
        w_hi = [sbr(f"weights_hi{s}", [P, SUB, P]) for s in range(SUBS)]
        w_lo = [sbr(f"weights_lo{s}", [P, SUB, P]) for s in range(SUBS)]
        h = sb("h", [P, DC, S2])
        x = h[:, :, META:S2]
        xh = sbr("xn_hi", [P, DC, S2])
        xl = sbr("xn_lo", [P, DC, S2])
        xt = sb("xn", [P, 4, S2])
        y = sb("y", [P, DC, S2])
        sq = sb("sq", [P, 4, S2])
        ssum = sb("sum_of_squares", [P, S2])
        ca = sb("const_a", [P, sum(n for _, n in at_a.values())])
        n_b = max(sum(n for _, n in at_b.values()), sum(n for _, n in at_c.values()))
        cb = sb("const_b", [P, n_b])
        par = sb("params", [P, N_PARAMS])
        w_gates = sb("w_gates", [P, DC, 2 * A_HEADS])
        gates_hi = sbr("w_gates_hi", [P, DC, 2 * A_HEADS])
        gates_lo = sbr("w_gates_lo", [P, DC, 2 * A_HEADS])
        rstd = sb("rstd", [P, S2])
        lnv = sb("lnv", [P, S2])
        silu = sb("silu", [P, 2, S2])
        small = sb("small", [P, 64])
        lam_t = sb("lam_parts", [P, 4, DC])
        arena_at = -(-nc.sbuf_base // 64) * 64
        N_ARENA = 26400
        arena = nc.alloc_sbuf_tensor_at("arena", [P, N_ARENA], F32, offset=arena_at)
        arena_r = nc.alloc_sbuf_tensor_at("arena_r", [P, N_ARENA], F32R, offset=arena_at)
        PS = ctx.enter_context(nc.psum_tensor("acc", [P, 8, 512], F32))

        def chunks(buf, at, n, t):
            return buf[:, at:at + n * t].rearrange("p (c t) -> p c t", t=t)

        proj1 = chunks(arena, 0, 48, S1)
        proj1_r = chunks(arena_r, 0, 48, S1)
        proj2 = chunks(arena, 0, AB_IN, S2)
        proj2_r = chunks(arena_r, 0, AB_IN, S2)
        w_r = chunks(arena, 24288, DC, P)
        w_i = chunks(arena, 24288 + D, DC, P)
        hid_hi, hid_lo = chunks(arena_r, 0, FFN, S1), chunks(arena_r, FFN * S1, FFN, S1)
        mlp_hi, mlp_lo = chunks(arena_r, 0, MLP, S2), chunks(arena_r, MLP * S2, MLP, S2)
        w_hi += [chunks(arena_r, 22528 + n * SUB * P, SUB, P) for n in range(2)]
        w_lo += [chunks(arena_r, 22528 + (n + 2) * SUB * P, SUB, P) for n in range(2)]
        part = chunks(arena, 25344, 2, S2)

        def const(name):
            for buf, at in ((ca, at_a), (cb, at_b), (cb, at_c)):
                if name in at:
                    return buf[:, at[name][0]:at[name][0] + at[name][1]]
            raise KeyError(name)

        def param(name, c=0, n=1):
            return par[:, PARAM_AT[name] + c:PARAM_AT[name] + c + n]

        ident, mean, ones, swap = const("ident"), const("mean"), const("ones"), const("swap")
        rope_cos, rope_sin = const("rope_cos"), const("rope_sin")
        rms_eps, ln_eps, one = const("rms_eps"), const("ln_eps"), const("one")

        x_loaded = sem("x_loaded")
        consts_loaded = sem("consts_loaded")
        tables_loaded = sem("tables_loaded")
        consts2_loaded = sem("consts2_loaded")
        meta_loaded = sem("meta_loaded")
        weights_loaded = [sem(f"weights{s}_loaded") for s in range(SLOTS)]
        hi_ready = sem("hi_ready")
        split_ready = sem("split_ready")
        sub_multiplied = sem("sub_multiplied")
        square_summed = sem("square_summed")
        y_added = sem("y_added")
        y_squared = sem("y_squared")
        xt_ready, xh_ready, x_split = sem("xt_ready"), sem("xh_ready"), sem("x_split")
        part_ready, part_hi, part_lo = sem("part_ready"), sem("part_hi"), sem("part_lo")
        scaled = sem("post_scaled")
        out_evacuated = sem("out_evacuated")
        gate_ready = sem("gate_ready")
        pair_done = sem("pair_done")
        squares_ready = sem("squares_ready")
        sum_ready = sem("sum_ready")
        rstd_ready = sem("rstd_ready")
        x_ready = sem("x_ready")
        act_chain = sem("act_chain")
        dve_chain = sem("dve_chain")
        final_ready = sem("final_ready")
        out_stored = sem("out_stored")
        wait_taken = sem("wait_taken")
        c_logged, c_rot, c_m1, c_d1, c_d2 = (sem("c_" + n) for n in ("logged", "rotation_parts", "maxima", "den_inverse", "scaled"))
        att_rot, att_m1, att_m2 = (sem("att_" + n) for n in ("rotation_parts", "maxima", "maximum"))

        FREE_BANKS, FREE_PAIRS, FREE_SUBS = 4, 2, 4

        def multiplied(phase, units):
            return units * phase.sps + (FREE_SUBS + phase.sub0)

        def evacuated(phase, n=None):
            return FREE_BANKS + phase.out0 + (phase.outs if n is None else n)

        def pairs_done(phase):
            return FREE_PAIRS + phase.pair0 + phase.units // 2

        def region(buf, at, *shape):
            n = int(np.prod(shape))
            v = buf[:, at:at + n]
            if len(shape) == 2:
                v = v.rearrange("p (a b) -> p a b", a=shape[0])
            return v

        def spread(row, n):
            return row.unsqueeze(1).to_broadcast((row.shape[0], n, row.shape[1]))

        ret_v = region(arena, 48 * S1, 2, 2048)
        ret_half = region(arena, 48 * S1, 4, 1024)
        ret_decay = region(arena, 64 * S1, RET_HEADS, 512)
        ret_p = region(arena, 72 * S1, 2, 512)
        ret_exp = region(arena, 72 * S1, 4, 512)
        ret_sq = region(arena, 76 * S1, 4, S1)
        ret_o = region(arena, 80 * S1, 4, S1)
        ret_hi = [proj1_r[:, 32 + n, :] for n in range(16)]
        ret_lo = [proj1_r[:, (2 * (n // 4) + n % 2) + (8 if n % 4 >= 2 else 0), :] for n in range(16)]
        lg = small[:, 0:16]
        conv_acc, conv_sq, conv_mix = (proj1[:, n * DC:(n + 1) * DC, :] for n in range(1, 4))
        conv_u = chunks(arena, 48 * S1, DC, S1 + 2 * CONV_PAD)
        conv_diag = region(arena, 57 * S1, 2 * PE_TAPS, P)
        conv_odd = region(arena, 70 * S1, 2, S1)
        conv_hi, conv_lo = proj1_r[:, 4 * DC:5 * DC, :], proj1_r[:, 5 * DC:6 * DC, :]
        att_raw = arena[:, 9 * S1:]
        att_q = region(att_raw, 0, 3, S1)
        att_k = region(att_raw, 768, 3, S1)
        att_vn = region(att_raw, 2304, 6, P)
        att_s = region(att_raw, 3072, 2, 768)
        att_p = region(att_raw, 4608, 2, 768)
        att_pt = region(att_raw, 6144, 2, 768)
        att_o = region(att_raw, 7680, 2, P)
        att_t = region(att_raw, 7936, 6, S1)
        att_hi, att_lo = chunks(arena_r, 9 * S1 + 9728, DC, S1), chunks(arena_r, 9 * S1 + 9728 + DC * S1, DC, S1)
        att_max = small[:, 16:26].rearrange("p (u k) -> p u k", u=2)
        att_den = small[:, 26:28]
        att_rden = small[:, 28:30]
        ab_v = region(arena, AB_IN * S2, 3, A_DIM)
        ab_row = region(arena, AB_IN * S2 + 3 * A_DIM, 10, S2)
        r_in, r_f, r_e, r_l, r_lf, r_F, r_a, r_m, r_en, r_sum = (ab_row[0:A_HEADS, i, :] for i in range(10))
        ab_raw = arena[:, AB_IN * S2 + 3 * A_DIM + (10 + 2 * DC) * S2:]
        ab_t = region(ab_raw, 0, 3, S2)
        ab_w = region(ab_raw, 3 * S2, 3, S2)
        ab_p = region(ab_raw, 6 * S2, 3, S2)
        ab_den = region(ab_raw, 9 * S2, 2, S2)
        ab_hh = region(ab_raw, 11 * S2, 2, S2)
        ab_sq = region(ab_raw, 13 * S2, 2, S2)
        ab_r = region(ab_raw, 15 * S2, 1, S2)[:, 0, :]
        ab_col = small[:, 32:44].rearrange("p (t n) -> p t n", t=3)
        lru_xb, lru_gate = proj2[:, 32:40, :], proj2[:, 40:48, :]
        lru_xc, lru_i = y, proj2[:, 32:40, :]
        lru_a, lru_r = (chunks(arena, AB_IN * S2 + 3 * A_DIM + (10 + n * DC) * S2, DC, S2) for n in range(2))
        ab_hi = [proj2_r[:, n, :] for n in range(8)] + [proj2_r[:, 32 + n, :] for n in range(8)]
        ab_lo = [proj2_r[:, 8 + n, :] for n in range(8)] + [proj2_r[:, 40 + n, :] for n in range(8)]
        lam8 = small[:, 44:52]
        c_raw = arena[:, C_IN * S2:]
        c_q, c_k, c_vs = c_raw[:, 0:S2], c_raw[:, S2:2 * S2], c_raw[:, 2 * S2:3 * S2]
        c_t = region(c_raw, 3 * S2, 2, S2)
        c_vn = region(c_raw, 5 * S2, 3, P)
        c_s = region(arena, 66 * S2, 6, S2)
        c_p = region(arena, 72 * S2, 6, S2)
        c_pd = region(arena, 78 * S2, 3, S2)
        c_pt = region(c_raw, 17 * S2, 3, S2)
        c_sq, c_ln, c_r, c_o = (c_raw[:, n * S2:(n + 1) * S2] for n in range(20, 24))
        c_hi, c_lo = chunks(arena_r, 48 * S2, DC, S2), chunks(arena_r, 56 * S2, DC, S2)
        c_max = small[:, 0:12].rearrange("p (u k) -> p u k", u=3)
        c_den = small[:, 16:22].rearrange("p (u k) -> p u k", u=3)
        c_at = [sum(S2 - t for t, _ in TILES2[:n]) - t0 for n, (t0, _) in enumerate(TILES2)]
        lam_s = chunks(arena, 64 * S2, 1, 2 * C_QK + 8)[:, 0, :]
        neg_lam = small[:, 30:31]
        subln = small[:, 31:32]

        def sems(prefix, names):
            return {n: sem(prefix + n) for n in names.split()}

        ret_sem = sems("ret_", "v_turned v_ready lg_ready exponent_ready decay_ready half_rotated roped scores_ready p_ready "
                               "o_ready squares_ready sum_ready rstd_ready gated split")
        conv_sem = sems("conv_", "diag_ready taps_summed tapped folded acc_ready mean_ready centered squares_ready var_ready rstd_ready scaled mixed split")
        att_sem = sems("att_", "rotated roped v_staged v_turned v_ready scores_ready max_ready p_ready den_ready "
                               "p_turned pt_ready o_ready o_scaled o_turned mixed")
        ab_sem = sems("ab_", "gate_sums log_in log_ready rows_ready floor_in floor_ready turned cols_ready v_turned "
                             "v_ready run_ready shifted w_ready scores_ready p_ready num_ready den_abs h_ready "
                             "squares_ready sum_ready rstd_ready mixed")
        lru_sem = sems("lru_", "lam_ready softplus_ready tapped steps conv_ready gates_summed gates_ready loga_ready a_ready root_in "
                               "root_ready gelu_in gelu_ready gelu_done done")
        gates_split = sem("gate_weights_split")
        att_rounded, c_scaled, c_rounded = sem("att_rounded"), sem("c_output_scaled"), sem("c_output_rounded")
        c_sem = sems("c_", "lam_in lam_exp rotated roped v_staged v_turned v_ready scores_ready max_ready p_ready "
                           "pd_ready p_turned pt_ready o_ready squares_ready sum_ready rstd_ready mixed")

        FREE_SQUARES = 4
        hidden0 = {f"ffn_in{n}": FFN * n for n in range(DEPTH)}
        hidden0.update({f"mlp_in{n}": DEPTH * FFN + MLP * n for n in range(2)})

        def post_index(k):
            return k // 2 if k < 16 else k - 9

        block = ctx.enter_context(nc.Block())

        @block.sync
        def _(sp):
            sp.dma_start(x[:, :, :], dram["x"]).then_inc(x_loaded, 16)
            sp.dma_start(par[:, :], dram["params"]).then_inc(consts_loaded, 16)
            sp.dma_start(ca[:, :], dram["const_a"]).then_inc(consts_loaded, 16)
            sp.dma_start(cb[:, 0:sum(n for _, n in at_b.values())], dram["const_b"]).then_inc(tables_loaded, 16)

            def load(phase, slot, unit):
                n = phase.tiles * P
                sp.dma_start(raw[slot][:, 0:phase.tiles, :].rearrange("p k f -> p (k f)"),
                             dram[phase.name][unit, :, 0:n]).then_inc(weights_loaded[slot], 16)

            for phase in phases:
                for s in range(phase.slots):
                    if phase.split0[s]:
                        sp.wait_ge(split_ready, phase.split0[s])
                    load(phase, s, s)
                with sp.Fori(1, phase.units // phase.slots) as i:
                    for s in range(phase.slots):
                        sp.wait_ge(split_ready, i * (phase.slots * phase.sps) + (phase.sub0 + (s - phase.slots + 1) * phase.sps))
                        load(phase, s, i * phase.slots + s)
            for c in range(0, DC, 2):
                sp.wait_ge(final_ready, c + 2)
                sp.dma_start(out[:, c:c + 2, :], y[:, c:c + 2, META:S2]).then_inc(out_stored, 16)
            sp.wait_ge(out_stored, 16 * DC // 2)

        @block.gpsimd
        def _(pool):
            pool.dma_start(h[:, :, 0:META], dram["meta"]).then_inc(meta_loaded, 16)
            pool.dma_start(w_gates[:, :, :], dram["ab_gates"]).then_inc(meta_loaded, 16)
            pool.wait_ge(x_ready, 2 * DEPTH * DC)
            pool.dma_start(cb[:, 0:sum(n for _, n in at_c.values())], dram["const_c"]).then_inc(consts2_loaded, 16)
            pool.dma_start(w_r, dram["lru_w_r"]).then_inc(consts2_loaded, 16)
            pool.dma_start(w_i, dram["lru_w_i"]).then_inc(consts2_loaded, 16)

        @block.tensor
        def _(pe):
            def product(acc, hi, lo, src, first, last):
                src_hi, src_lo = src
                nc.tensor.matmul(acc, hi, src_hi, start=first, stop=False)
                nc.tensor.matmul(acc, hi, src_lo, start=False, stop=False)
                return nc.tensor.matmul(acc, lo, src_hi, start=False, stop=last)

            def multiply(phase, i, u, acc, src, ready=None):
                for k in range(phase.tiles):
                    kk = (u % phase.upo) * phase.tiles + k
                    sub = u * phase.sps + k // SUB
                    if k % SUB == 0:
                        pe.wait_ge(split_ready, i * (phase.body * phase.sps) + (phase.sub0 + sub + 1))
                    if ready:
                        pe.wait_ge(*ready(kk))
                    last = product(acc, w_hi[sub % phase.subs][:, k % SUB, :], w_lo[sub % phase.subs][:, k % SUB, :], src(kk),
                                   kk == 0, kk == phase.upo * phase.tiles - 1)
                    if k % SUB == SUB - 1 or k == phase.tiles - 1:
                        last.then_inc(sub_multiplied, 1)

            def dense(phase, src, n, free, first_free, ready):
                body = phase.body
                banks = SLOTS if phase.upo == 1 else 2
                with pe.Fori(0, phase.units // body) as i:
                    for u in range(body):
                        o = u // phase.upo
                        if phase.pairs:
                            if u % 2 == 0:
                                pe.wait_ge(free, i * (body // 2) + (first_free + u // 2))
                        elif u % phase.upo == 0:
                            pe.wait_ge(free, i * (body // phase.upo) + (first_free + o))
                        multiply(phase, i, u, PS[:, o % banks, 0:n], src, ready if u < phase.upo else None)

            def dense_outputs(phase, src, n, ready):
                banks = SLOTS if phase.upo == 1 else 2
                dense(phase, src, n, out_evacuated, FREE_BANKS + phase.out0 - banks + 1, ready)

            def dense_pairs(phase, src, n, ready):
                dense(phase, src, n, pair_done, FREE_PAIRS + phase.pair0 - 1, ready)

            def norm_sum(k, n):
                first = DC * (k // 2)
                for c in range(DC):
                    pe.wait_ge(squares_ready, first + c + 1)
                    nc.tensor.matmul(PS[:, 4, 0:n], mean, sq[:, c % 4, 0:n], start=(c == 0), stop=(c == DC - 1))\
                        .then_inc(square_summed, 1)

            def post_sum(k, n):
                pe.wait_ge(y_added, FREE_SQUARES + DC * (post_index(k) + 1))
                nc.tensor.matmul(PS[:, 4, 0:n], mean, ssum[:, 0:n], start=True, stop=True).then_inc(sum_ready, 1)

            def retention(j, layer):
                g_end = evacuated(ph[f"ret_g{layer}"])
                R = ret_sem
                pe.wait_ge(R["roped"], 8 * j + 8)
                pe.wait_ge(R["v_ready"], 8 * j + 8)
                pe.wait_ge(out_evacuated, g_end)

                def scores(hd):
                    acc = PS[:, 4 + hd % 2, :]
                    for kt in range(2):
                        for c in range(2):
                            last = nc.tensor.matmul(acc[:, kt * S1:(kt + 1) * S1],
                                                    proj1[:, 8 + 2 * hd + c, kt * P:(kt + 1) * P], proj1[:, 2 * hd + c, :],
                                                    start=(c == 0), stop=(c == 1))
                    last.then_inc(R["scores_ready"], 1)

                scores(0)
                for hd in range(RET_HEADS):
                    n = 4 * j + hd
                    pe.wait_ge(R["p_ready"], n + 1)
                    if hd >= 2:
                        pe.wait_ge(R["gated"], n - 1)
                    first = 6 if hd % 2 == 0 else 2
                    for e in range(4):
                        acc = PS[:, first + e // 2, (e % 2) * S1:(e % 2 + 1) * S1]
                        for kt in range(2):
                            last = nc.tensor.matmul(acc, ret_v[:, kt, hd * RET_V + e * P:hd * RET_V + (e + 1) * P],
                                                    ret_p[:, hd % 2, kt * S1:(kt + 1) * S1], start=(kt == 0), stop=(kt == 1))
                    last.then_inc(R["o_ready"], 1)
                    if hd + 1 < RET_HEADS:
                        scores(hd + 1)
                    pe.wait_ge(R["squares_ready"], n + 1)
                    for e in range(4):
                        last = nc.tensor.matmul(PS[:, hd % 2, 0:S1], mean, ret_sq[:, e, :], start=(e == 0), stop=(e == 3))
                    last.then_inc(R["sum_ready"], 1)
                pe.wait_ge(R["gated"], 4 * j + 3)

            def turn_values(j, layer):
                for b in range(8):
                    hd, kt = b // 2, b % 2
                    pe.wait_ge(out_evacuated, evacuated(ph[f"ret_v{layer}"], 4 * hd + 4))
                    if b >= 2:
                        pe.wait_ge(ret_sem["v_ready"], 8 * j + b - 1)
                    for e in range(4):
                        last = nc.tensor.transpose(PS[:, 4 + b % 2, e * P:(e + 1) * P],
                                                   proj1[:, 16 + 4 * hd + e, kt * P:(kt + 1) * P], ident)
                    last.then_inc(ret_sem["v_turned"], 1)

            def conv(src, ready):
                C = conv_sem
                phase = ph["conv_in"]

                def taps(m, parity, wait_bank):
                    if wait_bank:
                        pe.wait_ge(C["acc_ready"], m)
                    pe.wait_ge(pair_done, m + (FREE_PAIRS + phase.pair0 + 1))
                    pe.wait_ge(C["diag_ready"], m * 2 + 2)
                    for t in range(PE_TAPS):
                        last = nc.tensor.matmul(PS[:, 4 + parity, 0:S1], conv_diag[:, parity * PE_TAPS + t, :],
                                                conv_u[:, m, t:t + S1], start=(t == 0), stop=(t == PE_TAPS - 1))
                    last.then_inc(C["taps_summed"], 1)

                def turn(i, first, ready=None):
                    for u in range(phase.body):
                        if u % 2 == 0:
                            pe.wait_ge(pair_done, i * (phase.body // 2) + (FREE_PAIRS + phase.pair0 - 1 + u // 2))
                        multiply(phase, i, u, PS[:, u, 0:S1], src, ready if u == 0 else None)
                        if u == 1 and not first:
                            taps(i * 2 - 1, 1, True)
                        if u == 3:
                            taps(i * 2, 0, not first)

                turn(0, True, ready)
                with pe.Fori(1, phase.units // phase.body) as i:
                    turn(i, False)
                taps(DC - 1, 1, True)
                for c in range(DC):
                    pe.wait_ge(C["acc_ready"], c + 2)
                    last = nc.tensor.matmul(PS[:, 6, 0:S1], mean, conv_acc[:, c, :], start=(c == 0), stop=(c == DC - 1))
                last.then_inc(C["mean_ready"], 1)
                pe.wait_ge(C["squares_ready"], 1)
                for c in range(DC):
                    last = nc.tensor.matmul(PS[:, 7, 0:S1], mean, conv_sq[:, c, :], start=(c == 0), stop=(c == DC - 1))
                last.then_inc(C["var_ready"], 1)

            def attention(src, ready):
                A = att_sem
                phase = ph["att_in"]
                NU = phase.body

                def rotate(i, g):
                    pe.wait_ge(out_evacuated, i * NU + evacuated(phase, 2 * g + 2))
                    for w in range(2):
                        last = nc.tensor.matmul(PS[:, 2 + g, w * S1:(w + 1) * S1], swap, proj1[:, 2 * g + w, :], start=True, stop=True)
                    last.then_inc(A["rotated"], 1)

                def turn_v(i):
                    pe.wait_ge(out_evacuated, i * NU + evacuated(phase, 0))
                    pe.wait_ge(A["mixed"], i)
                    for g in range(3):
                        for kt in range(2):
                            last = nc.tensor.transpose(PS[:, 6 + g // 2, (g % 2) * S1 + kt * P:(g % 2) * S1 + (kt + 1) * P],
                                                       proj1[:, 6 + g, kt * P:(kt + 1) * P], ident)
                    last.then_inc(A["v_turned"], 1)

                def scores(i, u):
                    e, it = u // 2, u % 2
                    rows = slice(64 * e, 64 * e + 64)
                    if u == 0:
                        pe.wait_ge(A["roped"], i * 3)
                    for g in range(3):
                        last = nc.tensor.matmul(PS[:, 2 + 2 * (u % 2) + g // 2, (g % 2) * S1:(g % 2 + 1) * S1],
                                                att_q[rows, g, it * P:(it + 1) * P], att_k[rows, g, :], start=True, stop=True)
                    last.then_inc(A["scores_ready"], 1)

                def turn_p(i, u):
                    if u == 0:
                        pe.wait_ge(A["v_ready"], i)
                    else:
                        pe.wait_ge(A["pt_ready"], i * 8 + (2 * u - 8))
                    pe.wait_ge(A["p_ready"], i * 4 + (u - 3))
                    for t in range(6):
                        last = nc.tensor.transpose(PS[:, 6 + t // 4, (t % 4) * P:(t % 4 + 1) * P],
                                                   att_p[:, u % 2, t * P:(t + 1) * P], ident)
                    last.then_inc(A["p_turned"], 1)

                def mix(i, u):
                    if u == 3:
                        pe.wait_ge(A["pt_ready"], i * 8)
                    for t in range(6):
                        last = nc.tensor.matmul(PS[:, 7, S1 + u * 64:S1 + (u + 1) * 64], att_pt[:, u % 2, t * P:(t + 1) * P],
                                                att_vn[:, t, (u // 2) * 64:(u // 2 + 1) * 64], start=(t == 0), stop=(t == 5))
                    last.then_inc(A["o_ready"], 1)

                def turn_o(i):
                    pe.wait_ge(A["o_scaled"], i * 4)
                    for it in range(2):
                        last = nc.tensor.transpose(PS[:, 7, S1 + it * P:S1 + (it + 1) * P], att_o[:, it, :], ident)
                    last.then_inc(A["o_turned"], 1)

                def turn(i, project, attend, ready=None):
                    for n in range(NU):
                        if project:
                            pe.wait_ge(out_evacuated, i * NU + (FREE_BANKS + phase.out0 + (n - 1 if n else 0)))
                            multiply(phase, i, n, PS[:, n % 2, 0:S1], src, ready if n == 0 else None)
                        if attend:
                            if n == 0:
                                turn_v(i)
                                scores(i, 0)
                            if n == 1:
                                scores(i, 1)
                            if 2 <= n <= 5:
                                turn_p(i, n - 2)
                            if 3 <= n <= 6:
                                mix(i, n - 3)
                            if 2 <= n <= 3:
                                scores(i, n)
                            if n == 7:
                                turn_o(i)
                        if project and 4 <= n <= 6:
                            if attend:
                                pe.wait_ge(A["p_ready"], i * 4 + (-1 if n < 6 else 0))
                            rotate(i, n - 4)

                turn(0, True, False, ready)
                with pe.Fori(1, DC) as i:
                    turn(i, True, True)
                turn(DC, False, True)

            def gates():
                pe.wait_ge(gates_split, 1)
                for k in range(DC):
                    pe.wait_ge(x_split, DC * (2 * DEPTH) + k + 1)
                    for gate in range(2):
                        cols = slice(gate * A_HEADS, (gate + 1) * A_HEADS)
                        last = product(PS[0:A_HEADS, 5 + gate, 0:S2], gates_hi[:, k, cols], gates_lo[:, k, cols],
                                       (xh[:, k, :], xl[:, k, :]), k == 0, k == DC - 1)
                last.then_inc(ab_sem["gate_sums"], 1)

            def mlstm(src, ready):
                A = ab_sem
                phase = ph["ab_qkvo"]
                sel = const("sel")

                def scores(hd):
                    pe.wait_ge(out_evacuated, evacuated(phase, hd * phase.body + 4))
                    if hd:
                        pe.wait_ge(A["h_ready"], hd)
                    else:
                        pe.wait_ge(A["floor_ready"], 1)
                    nc.tensor.matmul(PS[:, 2, 0:S2], sel[0:A_HEADS, hd * P:(hd + 1) * P], r_m, start=True, stop=True)\
                        .then_inc(A["run_ready"], 1)
                    for st, (t0, tl) in enumerate(TILES2):
                        for c in range(2):
                            last = nc.tensor.matmul(PS[0:tl, 3 + st, 0:S2], proj2[:, 8 + 2 * hd + c, t0:t0 + tl],
                                                    proj2[:, 2 * hd + c, :], start=(c == 0), stop=(c == 1))
                        last.then_inc(A["scores_ready"], 1)

                def turn_v(hd):
                    pe.wait_ge(out_evacuated, evacuated(phase, hd * phase.body + 6))
                    pe.wait_ge(A["rstd_ready"], hd) if hd else pe.wait_ge(A["cols_ready"], 1)
                    for st, (t0, tl) in enumerate(TILES2):
                        for c in range(2):
                            last = nc.tensor.transpose(PS[0:tl, 6 + st // 2, (2 * (st % 2) + c) * P:(2 * (st % 2) + c + 1) * P],
                                                       proj2[:, 16 + 2 * hd + c, t0:t0 + tl], ident)
                    last.then_inc(A["v_turned"], 1)

                def mix(hd):
                    pe.wait_ge(A["p_ready"], 3 * hd + 3)
                    pe.wait_ge(A["v_ready"], hd + 1)
                    nc.tensor.matmul(PS[:, 2, 0:S2], sel[0:A_HEADS, hd * P:(hd + 1) * P], r_en, start=True, stop=True)
                    pt = [ab_p[0:tl, st, :] for st, (_, tl) in enumerate(TILES2)]
                    for st, (_, tl) in enumerate(TILES2):
                        nc.tensor.matmul(PS[:, 5, 0:S2], ones[0:tl, :], pt[st], start=(st == 0), stop=(st == 2))
                    for c in range(2):
                        for st, (_, tl) in enumerate(TILES2):
                            last = nc.tensor.matmul(PS[:, 3 + c, 0:S2], ab_v[0:tl, st, c * P:(c + 1) * P], pt[st],
                                                    start=(st == 0), stop=(st == 2))
                    last.then_inc(A["num_ready"], 1)

                def head_sum(hd):
                    pe.wait_ge(A["squares_ready"], hd + 1)
                    for c in range(2):
                        last = nc.tensor.matmul(PS[:, 6, 0:S2], mean, ab_sq[:, c, :], start=(c == 0), stop=(c == 1))
                    last.then_inc(A["sum_ready"], 1)

                for i in range(A_HEADS + 1):
                    for n in range(phase.body):
                        if i < A_HEADS:
                            pe.wait_ge(out_evacuated, FREE_BANKS + phase.out0 + i * phase.body + n - 1)
                            multiply(phase, i, n, PS[:, n % 2, 0:S2], src, ready if i == n == 0 else None)
                        if i:
                            if n == 0:
                                scores(i - 1)
                            if n == 1:
                                turn_v(i - 1)
                            if n == 3:
                                mix(i - 1)
                            if n == 6:
                                head_sum(i - 1)
                        elif n == 5:
                            pe.wait_ge(A["rows_ready"], 1)
                            for st, (t0, tl) in enumerate(TILES2):
                                last = nc.tensor.transpose(PS[0:tl, 7, st * 4:st * 4 + 4], r_a[:, t0:t0 + tl],
                                                           ident[0:A_HEADS, 0:A_HEADS])
                            last.then_inc(A["turned"], 1)

            def lru_gates():
                L = lru_sem
                pe.wait_ge(out_evacuated, evacuated(ph["ab_gate"]))
                pe.wait_ge(consts2_loaded, 48)
                for c in range(DC):
                    pe.wait_ge(L["conv_ready"], c + 1)
                    if c >= 2:
                        pe.wait_ge(L["gates_ready"], 2 * (c - 1))
                    for gate, w in ((0, w_r), (1, w_i)):
                        last = nc.tensor.matmul(PS[:, 2 * (c % 2) + gate, 0:S2], w[:, c, :], lru_xc[:, c, :], start=True, stop=True)
                    last.then_inc(L["gates_summed"], 1)
                pe.wait_ge(L["gates_ready"], 2 * DC)

            def diff_attention(src, ready):
                A = c_sem
                phase = ph["c_in"]
                NU = phase.body

                def rotate(i):
                    pe.wait_ge(out_evacuated, i * NU + evacuated(phase, 0))
                    for w in range(2):
                        last = nc.tensor.matmul(PS[:, 2 + w, 0:S2], swap, proj2[:, i + (w * 8 - 1), :], start=True, stop=True)
                    last.then_inc(A["rotated"], 1)

                def scores(i, u, normed_before):
                    t0, tl = TILES2[u]
                    if u == 0:
                        pe.wait_ge(A["roped"], i)
                    if u == 2:
                        if normed_before:
                            pe.wait_ge(c_logged, i - 2)
                        pe.wait_ge(A["roped"], i)
                        pe.sem_inc(wait_taken, 1)
                    for e in range(2):
                        rows = slice(64 * e, 64 * e + 64)
                        acc = (PS[:, 2 + e, 0:P], PS[:, 2 + e, P:P + S1], PS[0:META, 4 + e, 0:S2])[u]
                        last = nc.tensor.matmul(acc, c_q[rows, t0:t0 + tl], c_k[rows, 0:t0 + tl], start=True, stop=True)
                    last.then_inc(A["scores_ready"], 1)

                def turn_p(i, u):
                    t0, tl = TILES2[u]
                    pe.wait_ge(A["pd_ready"], i * 3 + (u - 5))
                    if u == 2:
                        pe.sem_inc(wait_taken, 1)
                    for st in range(u + 1):
                        s0, sl = TILES2[st]
                        at = c_at[st] + t0
                        last = nc.tensor.transpose(PS[0:sl, 6, at:at + tl], c_pd[0:tl, u, s0:s0 + sl], ident[0:tl, 0:tl])
                    last.then_inc(A["p_turned"], 1)

                def turn_v(i):
                    pe.wait_ge(A["v_staged"], i - 1)
                    for st, (t0, tl) in enumerate(TILES2):
                        last = nc.tensor.transpose(PS[0:tl, 4, st * P:(st + 1) * P], c_vs[:, t0:t0 + tl], ident)
                    last.then_inc(A["v_turned"], 1)

                def mix(i, normed_before):
                    if normed_before:
                        pe.wait_ge(A["mixed"], i - 2)
                    pe.wait_ge(A["v_ready"], i - 1)
                    pe.wait_ge(A["pt_ready"], i - 1)
                    for st, (s0, sl) in enumerate(TILES2):
                        last = nc.tensor.matmul(PS[:, 7, s0:S2], c_vn[0:sl, st, :], c_pt[0:sl, st, s0:S2],
                                                start=(st == 0), stop=(st == 2))
                    last.then_inc(A["o_ready"], 1)

                def turn(i, project, score, weigh, norm, ready=None):
                    for n in range(NU):
                        if project:
                            pe.wait_ge(out_evacuated, i * NU + (FREE_BANKS + phase.out0 + (n - 1 if n else 0)))
                            multiply(phase, i, n, PS[:, n % 2, 0:S2], src, ready if n == 0 else None)
                        if n == 0:
                            if weigh:
                                if norm:
                                    pe.wait_ge(A["pt_ready"], i - 2)
                                pe.wait_ge(A["max_ready"], i * 3 - 3)
                                turn_p(i, 0)
                                turn_p(i, 1)
                            if score:
                                rotate(i)
                            if norm:
                                pe.wait_ge(A["squares_ready"], i - 2)
                                nc.tensor.matmul(PS[:, 5, 0:S2], mean, c_sq, start=True, stop=True).then_inc(A["sum_ready"], 1)
                        if n == 1:
                            if weigh:
                                turn_v(i)
                            if score:
                                scores(i, 0, norm)
                                scores(i, 1, norm)
                            if weigh:
                                turn_p(i, 2)
                        if n == 2:
                            if weigh:
                                mix(i, norm)
                            if score:
                                scores(i, 2, norm)

                LAST = C_HEADS
                turn(0, True, False, False, False, ready)
                turn(1, True, True, False, False)
                turn(2, True, True, True, False)
                with pe.Fori(3, LAST) as i:
                    turn(i, True, True, True, True)
                turn(LAST, False, True, True, True)
                turn(LAST + 1, False, False, True, True)
                turn(LAST + 2, False, False, False, True)
                pe.wait_ge(A["mixed"], C_HEADS - 2)

            pe.sem_inc(sub_multiplied, FREE_SUBS)
            pe.sem_inc(square_summed, FREE_SQUARES)
            pe.wait_ge(consts_loaded, 32)

            def normed(number, n):
                return (lambda k: (xh[:, k, 0:n], xl[:, k, 0:n])), (lambda k: (x_split, DC * number + k + 1))

            def hidden(hi, lo, name):
                return (lambda k: (hi[:, k, :], lo[:, k, :])), (lambda k: (part_lo, hidden0[name] + k + 1))

            for layer in range(DEPTH):
                norm_sum(4 * layer, S1)
                src, ready = normed(2 * layer, S1)
                if layer % 3 == 0:
                    j = layer // 3
                    dense_outputs(ph[f"ret_qk{layer}"], src, S1, ready)
                    dense_outputs(ph[f"ret_v{layer}"], src, S1, ready)
                    turn_values(j, layer)
                    dense_outputs(ph[f"ret_g{layer}"], src, S1, ready)
                    retention(j, layer)
                    dense_outputs(ph[f"ret_out{layer}"], lambda k: (ret_hi[k], ret_lo[k]), S1,
                                  lambda k: (ret_sem["split"], 4 * j + k // 4 + 1))
                elif layer % 3 == 1:
                    conv(src, ready)
                    dense_outputs(ph["conv_out"], lambda k: (conv_hi[:, k, :], conv_lo[:, k, :]), S1,
                                  lambda k: (conv_sem["split"], k + 1))
                else:
                    attention(src, ready)
                    dense_outputs(ph["att_out"], lambda k: (att_hi[:, k, :], att_lo[:, k, :]), S1,
                                  lambda k: (att_sem["mixed"], k + 2))
                post_sum(4 * layer + 1, S1)
                norm_sum(4 * layer + 2, S1)
                src, ready = normed(2 * layer + 1, S1)
                dense_pairs(ph[f"ffn_in{layer}"], src, S1, ready)
                src, ready = hidden(hid_hi, hid_lo, f"ffn_in{layer}")
                dense_outputs(ph[f"ffn_out{layer}"], src, S1, ready)
                post_sum(4 * layer + 3, S1)
            norm_sum(16, S2)
            for layer in range(2):
                src, ready = normed(2 * DEPTH + 2 * layer, S2)
                if layer == 0:
                    gates()
                    dense_outputs(ph["ab_xb"], src, S2, ready)
                    dense_outputs(ph["ab_gate"], src, S2, ready)
                    lru_gates()
                    mlstm(src, ready)
                    dense_outputs(ph["ab_out"], lambda k: (ab_hi[k], ab_lo[k]), S2,
                                  lambda k: (ab_sem["mixed"], k // 2 + 1) if k < DC else (lru_sem["done"], 1))
                else:
                    diff_attention(src, ready)
                    dense_outputs(ph["c_out"], lambda k: (c_hi[:, k, :], c_lo[:, k, :]), S2,
                                  lambda k: (c_sem["mixed"], k + 1))
                post_sum(17 + 2 * layer, S2)
                src, ready = normed(2 * DEPTH + 2 * layer + 1, S2)
                dense_outputs(ph[f"mlp_in{layer}"], src, S2, ready)
                src, ready = hidden(mlp_hi, mlp_lo, f"mlp_in{layer}")
                dense_outputs(ph[f"mlp_out{layer}"], src, S2, ready)
                post_sum(18 + 2 * layer, S2)

        @block.scalar
        def _(act):
            chain = [0]

            def step(ins):
                chain[0] += 1
                ins.then_inc(act_chain, 1)
                act.wait_ge(act_chain, chain[0])

            def split_part(phase, i, u, j):
                slot = u % phase.slots
                n = min(SUB, phase.tiles - j * SUB)
                sub = u * phase.sps + j
                if j == 0:
                    act.wait_ge(weights_loaded[slot], i * (16 * phase.body // phase.slots)
                                + 16 * (phase.loads0[slot] + u // phase.slots + 1))
                act.wait_ge(sub_multiplied, i * (phase.body * phase.sps) + (phase.sub0 + sub + 1))
                nc.scalar.activation(w_hi[sub % phase.subs][:, 0:n, :], raw[slot][:, j * SUB:j * SUB + n, :], ACT.Copy)\
                    .then_inc(hi_ready, 1)

            def split(phase, i, u):
                for j in range(phase.sps):
                    split_part(phase, i, u, j)

            def stream(phase, unit):
                turns = phase.units // phase.body
                with act.Fori(0, turns - 1) as i:
                    for u in range(phase.body):
                        split(phase, i, u + 1)
                        unit(i, u)
                for u in range(phase.body):
                    if u + 1 < phase.body:
                        split(phase, turns - 1, u + 1)
                    elif phase.after:
                        split(phase.after, 0, 0)
                    unit(turns - 1, u)

            def wait_unit(phase, i, u):
                act.wait_ge(sub_multiplied, i * (phase.body * phase.sps) + multiplied(phase, u + 1))

            def evacuate(phase, dst, n, func=ACT.Copy):
                def unit(i, u):
                    wait_unit(phase, i, u)
                    nc.scalar.activation(dst[:, i * phase.body + u, 0:n], PS[:, u % SLOTS, 0:n], func).then_inc(out_evacuated, 1)
                stream(phase, unit)

            def evacuate_y(k, phase, bias=None):
                banks = SLOTS if phase.upo == 1 else 2
                per = phase.body // phase.upo

                def unit(i, u):
                    if u % phase.upo < phase.upo - 1:
                        return
                    o = u // phase.upo
                    acc = PS[:, o % banks, 0:S1]
                    extra = {} if bias is None else {"bias": param(bias, 0, DC)[:, bass.ds(i * per + o, 1)]}
                    wait_unit(phase, i, u)
                    act.wait_ge(y_added, i * per + (FREE_SQUARES - per + DC * post_index(k) + o + 1))
                    nc.scalar.activation(sq[:, o, 0:S1], acc, ACT.Square, **extra).then_inc(y_squared, 1)
                    nc.scalar.activation(y[:, i * per + o, 0:S1], acc, ACT.Copy if bias is None else ACT.Identity, **extra)\
                        .then_inc(out_evacuated, 1)
                stream(phase, unit)

            def square_h(k, phase):
                per = phase.body // phase.upo

                def unit(i, u):
                    if u % phase.upo < phase.upo - 1:
                        return
                    o = u // phase.upo
                    act.wait_ge(out_evacuated, i * per + evacuated(phase, o + 1))
                    act.wait_ge(y_added, i * per + (FREE_SQUARES - per + DC * post_index(k) + o + 1))
                    nc.scalar.activation(sq[:, o, :], h[:, i * per + o, :], ACT.Square).then_inc(y_squared, 1)
                stream(phase, unit)

            def rms(n):
                step(nc.scalar.activation(lnv[:, 0:n], PS[:, 4, 0:n], ACT.Ln, bias=rms_eps))
                nc.scalar.activation(rstd[:, 0:n], lnv[:, 0:n], ACT.Exp, scale=-0.5).then_inc(rstd_ready, 1)

            def norm(k, src, n, meanwhile=None):
                first = DC * (k // 2)
                for c in range(DC):
                    if k:
                        act.wait_ge(x_ready, first - DC + c + 1)
                    act.wait_ge(square_summed, first + c + 1)
                    nc.scalar.activation(sq[:, c % 4, 0:n], src[:, c, 0:n], ACT.Square).then_inc(squares_ready, 1)
                if meanwhile:
                    meanwhile()
                act.wait_ge(square_summed, FREE_SQUARES + first + DC)
                rms(n)

            def post_norm(k, n):
                act.wait_ge(sum_ready, post_index(k) + 1)
                rms(n)

            def round_normed(number, n):
                for c in range(DC):
                    act.wait_ge(xt_ready, DC * number + c + 1)
                    nc.scalar.activation(xh[:, c, 0:n], xt[:, c % 4, 0:n], ACT.Copy).then_inc(xh_ready, 1)

            def silu_pairs(phase):
                def unit(i, u):
                    if u % 2 == 0:
                        wait_unit(phase, i, u)
                        nc.scalar.activation(silu[:, u // 2, 0:S1], PS[:, u, 0:S1], ACT.Silu).then_inc(gate_ready, 1)
                stream(phase, unit)

            def decay(j):
                for hd in range(RET_HEADS):
                    act.wait_ge(ret_sem["exponent_ready"], 4 * j + hd + 1)
                    nc.scalar.activation(ret_decay[:, hd, :], ret_exp[:, hd, :], ACT.Exp).then_inc(ret_sem["decay_ready"], 1)

            def retention(j):
                R = ret_sem
                for hd in range(RET_HEADS):
                    n = 4 * j + hd
                    first = 6 if hd % 2 == 0 else 2
                    act.wait_ge(R["o_ready"], n + 1)
                    nc.scalar.activation(ret_sq[:, :, :], PS[:, first:first + 2, :].rearrange("p b (e t) -> p (b e) t", t=S1),
                                         ACT.Square).then_inc(R["squares_ready"], 1)
                    act.wait_ge(R["sum_ready"], n + 1)
                    step(nc.scalar.activation(lnv[:, 0:S1], PS[:, hd % 2, 0:S1], ACT.Ln, bias=rms_eps, scale=float(D) / RET_V))
                    if hd >= 1:
                        act.wait_ge(R["gated"], n)
                    nc.scalar.activation(rstd[:, 0:S1], lnv[:, 0:S1], ACT.Exp, scale=-0.5).then_inc(R["rstd_ready"], 1)

            def conv_in(phase):
                C = conv_sem

                def unit(i, u):
                    q = u // 2
                    if u % 2 == 0:
                        wait_unit(phase, i, u)
                        nc.scalar.activation(silu[:, q, 0:S1], PS[:, u, 0:S1], ACT.Sigmoid,
                                             bias=param("conv_b_in", DC, DC)[:, bass.ds(i * 2 + q, 1)]).then_inc(gate_ready, 1)
                        act.wait_ge(C["taps_summed"], i * 2 + (q + 1))
                    for t in range(PE_TAPS):
                        if t % 2 == u % 2:
                            w = param("conv_w_dw", 0, DC * CONV_TAPS)[:, bass.ds((i * 2 + q) * CONV_TAPS + t, 1)]
                            last = nc.scalar.activation(conv_diag[:, q * PE_TAPS + t, :], ident, ACT.Copy, scale=w)
                    last.then_inc(C["diag_ready"], 1)
                stream(phase, unit)

            def conv():
                C = conv_sem
                act.wait_ge(C["centered"], 1)
                nc.scalar.activation(conv_sq[:, :, :], conv_acc[:, :, :], ACT.Square).then_inc(C["squares_ready"], 1)
                act.wait_ge(C["var_ready"], 1)
                step(nc.scalar.activation(lnv[:, 0:S1], PS[:, 7, 0:S1], ACT.Ln, bias=ln_eps))
                nc.scalar.activation(rstd[:, 0:S1], lnv[:, 0:S1], ACT.Exp, scale=-0.5).then_inc(C["rstd_ready"], 1)
                act.wait_ge(C["scaled"], 1)
                for c in range(DC):
                    nc.scalar.activation(conv_mix[:, c, :], conv_sq[:, c, :], ACT.Silu, bias=param("conv_ln_b", c),
                                         scale=param("conv_ln_g", c)).then_inc(C["mixed"], 1)

            def attention():
                A = att_sem
                phase = ph["att_in"]
                NU = phase.body

                def exp(i, u):
                    act.wait_ge(A["max_ready"], i * 4 + (u - 3))
                    nc.scalar.activation(att_p[:, u % 2, :], att_s[:, u % 2, :], ACT.Exp, bias=att_max[:, u % 2, 4:5],
                                         scale=0.125, accum_out=att_den[:, u % 2:u % 2 + 1]).then_inc(A["p_ready"], 1)

                def copy_p(i, u):
                    act.wait_ge(A["p_turned"], i * 4 + (u - 3))
                    nc.scalar.activation(att_pt[:, u % 2, 512:768], PS[:, 7, 0:S1], ACT.Copy).then_inc(A["pt_ready"], 1)

                def scale_o(i, u):
                    e, it = u // 2, u % 2
                    act.wait_ge(A["o_ready"], i * 4 + (u - 3))
                    act.wait_ge(A["den_ready"], i * 4 + (u - 3))
                    nc.scalar.activation(att_o[:, it, e * 64:(e + 1) * 64], PS[:, 7, S1 + u * 64:S1 + (u + 1) * 64], ACT.Copy,
                                         scale=att_rden[:, u % 2:u % 2 + 1]).then_inc(A["o_scaled"], 1)

                def turn(i, project, attend, after=None):
                    for n in range(NU):
                        if project:
                            following = (phase, i, n + 1) if n + 1 < NU or after is None else (after, 0, 0)
                            split(*following)
                        if attend:
                            if 4 <= n <= 7:
                                scale_o(i, n - 4)
                            if 3 <= n <= 6:
                                copy_p(i, n - 3)
                            if 1 <= n <= 4:
                                exp(i, n - 1)
                        if project:
                            act.wait_ge(sub_multiplied, i * (NU * phase.sps) + multiplied(phase, n + 1))
                            if attend:
                                if n < 6:
                                    act.wait_ge(A["roped"], i * 3 + (n // 2 - 2))
                                else:
                                    act.wait_ge(A["v_turned"], i)
                            nc.scalar.activation(proj1[:, n, :], PS[:, n % 2, 0:S1], ACT.Copy).then_inc(out_evacuated, 1)

                turn(0, True, False)
                with act.Fori(1, DC - 1) as i:
                    turn(i, True, True)
                turn(DC - 1, True, True, phase.after)
                turn(DC, False, True)

            def mlstm_rows():
                A = ab_sem
                act.wait_ge(A["log_in"], 1)
                step(nc.scalar.activation(r_l, r_e, ACT.Exp))
                nc.scalar.activation(r_l, r_l, ACT.Ln, bias=one[0:A_HEADS, :]).then_inc(A["log_ready"], 1)
                act.wait_ge(A["floor_in"], 1)
                nc.scalar.activation(r_en, r_sum, ACT.Exp, scale=-1.0).then_inc(A["floor_ready"], 1)

            def mlstm():
                A = ab_sem
                phase = ph["ab_qkvo"]

                def weights(hd):
                    for st, (_, tl) in enumerate(TILES2):
                        act.wait_ge(A["shifted"], 3 * hd + st + 1)
                        nc.scalar.activation(ab_w[0:tl, st, :], ab_t[0:tl, st, :], ACT.Exp, bias=ab_col[0:tl, st, hd:hd + 1],
                                             scale=-1.0).then_inc(A["w_ready"], 1)

                def values(hd):
                    act.wait_ge(A["v_turned"], hd + 1)
                    for st, (_, tl) in enumerate(TILES2):
                        last = nc.scalar.activation(ab_v[0:tl, st, :], PS[0:tl, 6 + st // 2, (st % 2) * A_DIM:(st % 2 + 1) * A_DIM], ACT.Copy)
                    last.then_inc(A["v_ready"], 1)

                def denominator(hd):
                    act.wait_ge(A["num_ready"], hd + 1)
                    nc.scalar.activation(ab_den[:, 0, :], PS[:, 5, 0:S2], ACT.Abs).then_inc(A["den_abs"], 1)

                def squares(hd):
                    act.wait_ge(A["h_ready"], hd + 1)
                    for c in range(2):
                        last = nc.scalar.activation(ab_sq[:, c, :], ab_hh[:, c, :], ACT.Square)
                    last.then_inc(A["squares_ready"], 1)

                def factor(hd):
                    act.wait_ge(A["sum_ready"], hd + 1)
                    exp_tables()
                    step(nc.scalar.activation(lnv[:, :], PS[:, 6, 0:S2], ACT.Ln, bias=rms_eps, scale=float(D) / A_DIM))
                    nc.scalar.activation(ab_r, lnv[:, :], ACT.Exp, scale=-0.5).then_inc(A["rstd_ready"], 1)

                for i in range(A_HEADS + 1):
                    for n in range(phase.body):
                        if i < A_HEADS:
                            if n + 1 < phase.body or i + 1 < A_HEADS:
                                split(phase, i, n + 1)
                            else:
                                split(phase.after, 0, 0)
                        elif n == 0:
                            lru_root()
                        if i:
                            if n == 1:
                                weights(i - 1)
                            if n == 2:
                                values(i - 1)
                            if n == 4:
                                denominator(i - 1)
                            if n == 6:
                                squares(i - 1)
                            if n == 7:
                                factor(i - 1)
                        if i < A_HEADS:
                            if n == 0:
                                nc.scalar.preload_act_table_set("exp_and_others")
                            lru_unit(2 * i + n // 4, n % 4)
                            wait_unit(phase, i, n)
                            nc.scalar.activation(proj2[:, 8 * (n // 2) + 2 * i + n % 2, :], PS[:, n % 2, 0:S2],
                                                 ACT.Copy if n < 6 else ACT.Sigmoid).then_inc(out_evacuated, 1)
            def lru():
                L = lru_sem
                for c in range(DC):
                    act.wait_ge(L["gates_summed"], c + 1)
                    for gate, dst, bias in ((0, lru_r, "lru_b_r"), (1, lru_i, "lru_b_i")):
                        nc.scalar.activation(dst[:, c, :], PS[:, 2 * (c % 2) + gate, 0:S2], ACT.Sigmoid, bias=param(bias, c))\
                            .then_inc(L["gates_ready"], 1)

            def lru_unit(i, u):
                L = lru_sem
                if u == 1:
                    act.wait_ge(L["loga_ready"], i + 1)
                    nc.scalar.activation(lru_a[:, i, :], lru_r[:, i, :], ACT.Exp)
                    nc.scalar.activation(lru_r[:, i, :], lru_r[:, i, :], ACT.Tanh, scale=-1.0).then_inc(L["a_ready"], 1)
                if u == 2:
                    act.wait_ge(L["gelu_in"], i + 1)
                    nc.scalar.activation(sq[:, 1, :], sq[:, 0, :], ACT.Tanh, scale=math.sqrt(2.0 / math.pi)).then_inc(L["gelu_ready"], 1)

            def lru_root():
                L = lru_sem
                act.wait_ge(L["root_in"], DC)
                nc.scalar.activation(lru_r[:, :, :], lru_r[:, :, :], ACT.Sqrt, scale=2.0).then_inc(L["root_ready"], 1)

            def relu(phase):
                def unit(i, u):
                    wait_unit(phase, i, u)
                    act.wait_ge(part_ready, i * phase.body + (hidden0[phase.name] - DEPTH * FFN + u + 1))
                    nc.scalar.activation(silu[:, u % 2, :], PS[:, u % SLOTS, 0:S2], ACT.Relu).then_inc(out_evacuated, 1)
                stream(phase, unit)

            def diff_attention():
                A = c_sem
                phase = ph["c_in"]
                NU = phase.body

                def exp(i, u):
                    t0, tl = TILES2[u]
                    act.wait_ge(A["max_ready"], i * 3 + (u - 2))
                    for e in range(2):
                        last = nc.scalar.activation(c_p[0:tl, 2 * u + e, 0:t0 + tl], c_s[0:tl, 2 * u + e, 0:t0 + tl],
                                                    ACT.Exp, bias=c_max[0:tl, u, 2 + e:3 + e], scale=0.125,
                                                    accum_out=c_den[0:tl, u, e:e + 1])
                    last.then_inc(A["p_ready"], 1)

                def copy_p(i):
                    act.wait_ge(A["p_turned"], i * 3 - 3)
                    for st, (s0, sl) in enumerate(TILES2):
                        at = c_at[st]
                        last = nc.scalar.activation(c_pt[0:sl, st, s0:S2], PS[0:sl, 6, at + s0:at + S2], ACT.Copy)
                    last.then_inc(A["pt_ready"], 1)

                def turn(i, project, score, weigh, norm, after=None):
                    for n in range(NU):
                        if project:
                            following = (phase, i, n + 1) if n + 1 < NU or after is None else (after, 0, 0)
                            split(*following)
                        if n == 0:
                            if norm:
                                act.wait_ge(A["o_ready"], i - 2)
                                nc.scalar.activation(c_sq, PS[:, 7, 0:S2], ACT.Square).then_inc(A["squares_ready"], 1)
                            if weigh:
                                exp(i - 1, 2)
                                if norm:
                                    act.wait_ge(A["v_turned"], i - 2)
                                act.wait_ge(out_evacuated, (i - 1) * NU + evacuated(phase, 0))
                                nc.scalar.activation(c_vs, proj2[:, i + 14, :], ACT.Copy).then_inc(A["v_staged"], 1)
                        if n == 1 and norm:
                            act.wait_ge(A["sum_ready"], i - 2)
                            nc.scalar.activation(c_ln, PS[:, 5, 0:S2], ACT.Ln, bias=rms_eps, scale=float(D) / P).then_inc(c_logged, 1)
                            act.wait_ge(c_logged, i - 2)
                            nc.scalar.activation(c_r, c_ln, ACT.Exp, scale=-0.5).then_inc(A["rstd_ready"], 1)
                        if n == 2:
                            if weigh:
                                copy_p(i)
                            if score:
                                exp(i, 0)
                                exp(i, 1)
                        if project:
                            act.wait_ge(sub_multiplied, i * (NU * phase.sps) + multiplied(phase, n + 1))
                            nc.scalar.activation(proj2[:, i + 8 * n, :], PS[:, n % 2, 0:S2], ACT.Copy).then_inc(out_evacuated, 1)

                LAST = C_HEADS
                turn(0, True, False, False, False)
                turn(1, True, True, False, False)
                turn(2, True, True, True, False)
                with act.Fori(3, LAST - 1) as i:
                    turn(i, True, True, True, True)
                turn(LAST - 1, True, True, True, True, phase.after)
                turn(LAST, False, True, True, True)
                turn(LAST + 1, False, False, True, True)
                turn(LAST + 2, False, False, False, True)

            def exp_tables():
                nc.scalar.preload_act_table_set("natural_log_exp_and_others")

            act.sem_inc(out_evacuated, FREE_BANKS)
            exp_tables()
            act.wait_ge(x_loaded, 16)
            act.wait_ge(consts_loaded, 32)
            act.wait_ge(lru_sem["lam_ready"], 1)
            nc.scalar.activation(lam_t[:, 1, :], lam_t[:, 0, :], ACT.Exp).then_inc(lru_sem["softplus_ready"], 1)
            for layer in range(DEPTH):
                if layer == 0:
                    step(nc.scalar.activation(lg, param("decay", 0, 16), ACT.Exp))
                    nc.scalar.activation(lg, lg, ACT.Ln, bias=one, scale=-1.0).then_inc(ret_sem["lg_ready"], 1)
                    norm(0, x, S1, lambda: split(phases[0], 0, 0))
                else:
                    norm(4 * layer, x, S1)
                round_normed(2 * layer, S1)
                if layer % 3 == 0:
                    j = layer // 3
                    evacuate(ph[f"ret_qk{layer}"], proj1, S1)
                    evacuate(ph[f"ret_v{layer}"], proj1[:, 16:32, :], S1)
                    if layer == 0:
                        decay(0)
                    nc.scalar.preload_act_table(ACT.Silu)
                    evacuate(ph[f"ret_g{layer}"], proj1[:, 32:48, :], S1, ACT.Silu)
                    exp_tables()
                    retention(j)
                    evacuate_y(4 * layer + 1, ph[f"ret_out{layer}"])
                elif layer % 3 == 1:
                    nc.scalar.preload_act_table(ACT.Sigmoid)
                    conv_in(ph["conv_in"])
                    exp_tables()
                    conv()
                    exp_tables()
                    evacuate_y(4 * layer + 1, ph["conv_out"], bias="conv_b_out")
                else:
                    attention()
                    decay(1)
                    evacuate_y(4 * layer + 1, ph["att_out"])
                post_norm(4 * layer + 1, S1)
                norm(4 * layer + 2, x, S1)
                nc.scalar.preload_act_table(ACT.Silu)
                round_normed(2 * layer + 1, S1)
                silu_pairs(ph[f"ffn_in{layer}"])
                exp_tables()
                evacuate_y(4 * layer + 3, ph[f"ffn_out{layer}"])
                post_norm(4 * layer + 3, S1)
            act.wait_ge(meta_loaded, 32)
            norm(16, h, S2)
            for layer in range(2):
                round_normed(2 * DEPTH + 2 * layer, S2)
                if layer == 0:
                    evacuate(ph["ab_xb"], proj2[:, 32:40, :], S2)
                    evacuate(ph["ab_gate"], proj2[:, 40:48, :], S2)
                    mlstm_rows()
                    nc.scalar.preload_act_table(ACT.Sigmoid)
                    lru()
                    mlstm()
                    exp_tables()
                    square_h(17, ph["ab_out"])
                else:
                    act.wait_ge(c_sem["lam_in"], 1)
                    nc.scalar.activation(lam_s[:, 2:4], lam_s[:, 0:2], ACT.Exp).then_inc(c_sem["lam_exp"], 1)
                    diff_attention()
                    square_h(19, ph["c_out"])
                post_norm(17 + 2 * layer, S2)
                round_normed(2 * DEPTH + 2 * layer + 1, S2)
                relu(ph[f"mlp_in{layer}"])
                square_h(18 + 2 * layer, ph[f"mlp_out{layer}"])
                post_norm(18 + 2 * layer, S2)

        @block.vector
        def _(dve):
            chain = [0]

            def step(ins):
                chain[0] += 1
                ins.then_inc(dve_chain, 1)
                dve.wait_ge(dve_chain, chain[0])

            stt = nc.vector.scalar_tensor_tensor

            def split_part(phase, i, u, j):
                slot = u % phase.slots
                n = min(SUB, phase.tiles - j * SUB)
                sub = u * phase.sps + j
                dve.wait_ge(hi_ready, i * (phase.body * phase.sps) + (phase.sub0 + sub + 1))
                nc.vector.tensor_tensor(w_lo[sub % phase.subs][:, 0:n, :], raw[slot][:, j * SUB:j * SUB + n, :],
                                        w_hi[sub % phase.subs][:, 0:n, :].bitcast(F32), ALU.subtract).then_inc(split_ready, 1)

            def split(phase, i, u):
                for j in range(phase.sps):
                    split_part(phase, i, u, j)

            def stream(phase, unit=None):
                turns = phase.units // phase.body
                with dve.Fori(0, turns - 1) as i:
                    for u in range(phase.body):
                        split(phase, i, u + 1)
                        if unit:
                            unit(i, u)
                for u in range(phase.body):
                    if u + 1 < phase.body:
                        split(phase, turns - 1, u + 1)
                    elif phase.after:
                        split(phase.after, 0, 0)
                    if unit:
                        unit(turns - 1, u)

            def wait_unit(phase, i, u):
                dve.wait_ge(sub_multiplied, i * (phase.body * phase.sps) + multiplied(phase, u + 1))

            def pre_norm(k, number, src, n, weight, col):
                dve.wait_ge(rstd_ready, k + 1)

                def rest(c):
                    dve.wait_ge(xh_ready, DC * number + c + 1)
                    nc.vector.tensor_tensor(xl[:, c, 0:n], xt[:, c % 4, 0:n], xh[:, c, 0:n].bitcast(F32), ALU.subtract)\
                        .then_inc(x_split, 1)

                for c in range(DC):
                    if c >= 4:
                        dve.wait_ge(x_split, DC * number + c - 3)
                    stt(xt[:, c % 4, 0:n], src[:, c, 0:n], param(weight, col + c), rstd[:, 0:n], ALU.mult, ALU.mult)\
                        .then_inc(xt_ready, 1)
                    if c >= 2:
                        rest(c - 2)
                rest(DC - 2)
                rest(DC - 1)

            def sum_squares(k, phase, n, unit=None):
                per = phase.body // phase.upo
                step(nc.vector.memset(ssum[:, 0:n], 0.0))

                def output(i, u):
                    if u % phase.upo < phase.upo - 1:
                        return
                    o = u // phase.upo
                    if unit:
                        unit(i, u)
                    dve.wait_ge(y_squared, i * per + (DC * post_index(k) + o + 1))
                    dve.wait_ge(y_added, i * per + (FREE_SQUARES + DC * post_index(k) + o))
                    nc.vector.tensor_tensor(ssum[:, 0:n], ssum[:, 0:n], sq[:, o, 0:n], ALU.add).then_inc(y_added, 1)
                stream(phase, output)

            def post_norm(k, col):
                first = DC * post_index(k)
                dve.wait_ge(rstd_ready, k + 1)

                def update(c):
                    dve.wait_ge(scaled, first + c + 1)
                    nc.vector.tensor_tensor(x[:, c, :], x[:, c, :], y[:, c, 0:S1], ALU.add).then_inc(x_ready, 1)

                for c in range(DC):
                    stt(y[:, c, 0:S1], y[:, c, 0:S1], param("norm_w", col + c), rstd[:, 0:S1], ALU.mult, ALU.mult)\
                        .then_inc(scaled, 1)
                    if c:
                        update(c - 1)
                update(DC - 1)

            def add_to_h(k, phase):
                banks = SLOTS if phase.upo == 1 else 2
                per = phase.body // phase.upo

                def unit(i, u):
                    o = u // phase.upo
                    wait_unit(phase, i, u)
                    nc.vector.tensor_tensor(h[:, i * per + o, :], h[:, i * per + o, :], PS[:, o % banks, 0:S2], ALU.add)\
                        .then_inc(out_evacuated, 1)
                sum_squares(k, phase, S2, unit)

            def split_hidden(hi, lo, t, i, number, first):
                nc.vector.tensor_copy(hi, t).then_inc(part_hi, 1)
                dve.wait_ge(part_hi, i + (first + number + 1))
                nc.vector.tensor_tensor(lo, t, hi.bitcast(F32), ALU.subtract).then_inc(part_lo, 1)

            def ffn_pairs(phase):
                first = hidden0[phase.name]

                def unit(i, u):
                    if u % 2 == 0:
                        return
                    q = u // 2
                    wait_unit(phase, i, u)
                    dve.wait_ge(gate_ready, i * 2 + (phase.pair0 + q + 1))
                    nc.vector.tensor_tensor(part[:, q, 0:S1], PS[:, u, 0:S1], silu[:, q, 0:S1], ALU.mult).then_inc(pair_done, 1)
                    dve.wait_ge(pair_done, i * 2 + (FREE_PAIRS + phase.pair0 + q + 1))
                    split_hidden(hid_hi[:, i * 2 + q, :], hid_lo[:, i * 2 + q, :], part[:, q, 0:S1], i * 2, q, first)
                stream(phase, unit)

            def square_relu(phase):
                first = hidden0[phase.name]

                def unit(i, u):
                    dve.wait_ge(out_evacuated, i * phase.body + evacuated(phase, u + 1))
                    nc.vector.tensor_tensor(part[:, u % 2, :], silu[:, u % 2, :], silu[:, u % 2, :], ALU.mult).then_inc(part_ready, 1)
                    dve.wait_ge(part_ready, i * phase.body + (first - DEPTH * FFN + u + 3))
                    m = i * phase.body + u
                    split_hidden(mlp_hi[:, m, :], mlp_lo[:, m, :], part[:, u % 2, :], i * phase.body, u, first)
                stream(phase, unit)

            def exponents(j):
                after, before = const("after"), const("before")
                if j == 0:
                    dve.wait_ge(ret_sem["lg_ready"], 1)
                    dve.wait_ge(tables_loaded, 16)
                for hd in range(RET_HEADS):
                    fwd = lg[:, 8 * j + hd:8 * j + hd + 1]
                    bwd = lg[:, 8 * j + 4 + hd:8 * j + 5 + hd]
                    step(nc.vector.tensor_scalar(ret_exp[:, hd, :], after, fwd, None, ALU.mult))
                    stt(ret_exp[:, hd, :], before, bwd, ret_exp[:, hd, :], ALU.mult, ALU.add)\
                        .then_inc(ret_sem["exponent_ready"], 1)

            def rotate(j, phase):
                R = ret_sem
                cos, sin = const("ret_cos"), const("ret_sin")

                def parts(m, parity):
                    x1, x2 = proj1[:, m * 2, :], proj1[:, m * 2 + 1, :]
                    t = ret_half[:, 2 * parity:2 * parity + 2, :].rearrange("p a (b t) -> p (a b) t", t=S1)
                    return x1, x2, t

                def begin(m, parity):
                    x1, x2, t = parts(m, parity)
                    dve.wait_ge(out_evacuated, m * 2 + evacuated(phase, 2))
                    nc.vector.tensor_tensor(t[:, 0, :], x1, cos, ALU.mult)
                    nc.vector.tensor_tensor(t[:, 1, :], x2, sin, ALU.mult)
                    nc.vector.tensor_tensor(t[:, 3, :], x1, sin, ALU.mult).then_inc(R["half_rotated"], 1)

                def end(m, parity):
                    x1, x2, t = parts(m, parity)
                    nc.vector.tensor_tensor(t[:, 2, :], x2, cos, ALU.mult).then_inc(R["half_rotated"], 1)
                    dve.wait_ge(R["half_rotated"], m * 2 + (16 * j + 2))
                    nc.vector.tensor_tensor(x1, t[:, 0, :], t[:, 1, :], ALU.subtract)
                    nc.vector.tensor_tensor(x2, t[:, 2, :], t[:, 3, :], ALU.add).then_inc(R["roped"], 1)

                def turn(i, first, after=None):
                    for u in range(phase.body):
                        following = (phase, i, u + 1) if u + 1 < phase.body or after is None else (after, 0, 0)
                        split(*following)
                        q = u // 2
                        if u % 2:
                            begin(i * 2 + q, q)
                        elif q or not first:
                            end(i * 2 + (q - 1), 1 - q)

                turns = phase.units // phase.body
                turn(0, True)
                with dve.Fori(1, turns - 1) as i:
                    turn(i, False)
                turn(turns - 1, False, phase.after)
                end(2 * RET_HEADS - 1, 1)
                dve.wait_ge(R["roped"], 8 * j + 8)

            def values(j):
                R = ret_sem
                for b in range(8):
                    dve.wait_ge(R["v_turned"], 8 * j + b + 1)
                    hd, kt = b // 2, b % 2
                    nc.vector.tensor_copy(ret_v[:, kt, hd * RET_V:(hd + 1) * RET_V], PS[:, 4 + b % 2, :]).then_inc(R["v_ready"], 1)

            def retention(j, layer):
                R = ret_sem
                dve.wait_ge(R["decay_ready"], 4 * j + 4)

                def decayed(hd):
                    dve.wait_ge(R["scores_ready"], 4 * j + hd + 1)
                    if hd >= 2:
                        dve.wait_ge(R["o_ready"], 4 * j + hd - 1)
                    stt(ret_p[:, hd % 2, :], PS[:, 4 + hd % 2, :], RET_QK ** -0.5, ret_decay[:, hd, :], ALU.mult, ALU.mult)\
                        .then_inc(R["p_ready"], 1)

                dve.wait_ge(out_evacuated, evacuated(ph[f"ret_g{layer}"]))
                decayed(0)
                for hd in range(RET_HEADS):
                    if hd + 1 < RET_HEADS:
                        decayed(hd + 1)
                    first = 6 if hd % 2 == 0 else 2
                    dve.wait_ge(R["rstd_ready"], 4 * j + hd + 1)
                    g = proj1[:, 32 + 4 * hd:36 + 4 * hd, :]
                    step(nc.vector.tensor_tensor(g, g, spread(rstd[:, 0:S1], 4), ALU.mult))
                    nc.vector.tensor_tensor(ret_o, g, PS[:, first:first + 2, :].rearrange("p b (e t) -> p (b e) t", t=S1), ALU.mult)\
                        .then_inc(R["gated"], 1)
                    dve.wait_ge(R["gated"], 4 * j + hd + 1)
                    hi = proj1_r[:, 32 + 4 * hd:36 + 4 * hd, :]
                    step(nc.vector.tensor_copy(hi, ret_o))
                    for n in range(2):
                        last = nc.vector.tensor_tensor(proj1_r[:, 8 * n + 2 * hd:8 * n + 2 * hd + 2, :], ret_o[:, 2 * n:2 * n + 2, :],
                                                       hi[:, 2 * n:2 * n + 2, :].bitcast(F32), ALU.subtract)
                    last.then_inc(R["split"], 1)
                    dve.wait_ge(R["split"], 4 * j + hd + 1)

            def conv():
                C = conv_sem
                phase = ph["conv_in"]
                mine = range(PE_TAPS, CONV_TAPS)
                half = len(mine) // 2

                def product(i, q):
                    u = 2 * q + 1
                    wait_unit(phase, i, u)
                    dve.wait_ge(gate_ready, i * 2 + (phase.pair0 + q + 1))
                    stt(conv_u[:, i * 2 + q, CONV_PAD:CONV_PAD + S1], PS[:, u, 0:S1],
                        param("conv_b_in", 0, DC)[:, bass.ds(i * 2 + q, 1)], silu[:, q, 0:S1], ALU.add, ALU.mult).then_inc(pair_done, 1)

                def taps(m, parity, numbers):
                    dve.wait_ge(pair_done, m + (FREE_PAIRS + phase.pair0 + 1))
                    for n in numbers:
                        w = param("conv_w_dw", 0, DC * CONV_TAPS)[:, bass.ds(m * CONV_TAPS + mine[n], 1)]
                        u = conv_u[:, m, mine[n]:mine[n] + S1]
                        acc = conv_odd[:, parity, :] if n % 2 else conv_acc[:, m, :]
                        if n < 2:
                            last = nc.vector.tensor_scalar(acc, u, w, None, ALU.mult)
                        else:
                            dve.wait_ge(C["tapped"], m * len(mine) + (n - 1))
                            last = stt(acc, u, w, acc, ALU.mult, ALU.add)
                        last.then_inc(C["tapped"], 1)

                def fold(m, parity):
                    dve.wait_ge(C["tapped"], m * len(mine) + len(mine))
                    nc.vector.tensor_tensor(conv_acc[:, m, :], conv_acc[:, m, :], conv_odd[:, parity, :], ALU.add).then_inc(C["folded"], 1)

                def combine(m, parity):
                    dve.wait_ge(C["folded"], m + 1)
                    dve.wait_ge(C["taps_summed"], m + 3)
                    stt(conv_acc[:, m, :], PS[:, 4 + parity, 0:S1], param("conv_b_dw", 0, DC)[:, bass.ds(m, 1)], conv_acc[:, m, :],
                        ALU.add, ALU.add).then_inc(C["acc_ready"], 1)

                def turn(i, first, after=None):
                    for u in range(phase.body):
                        following = (phase, i, u + 1) if u + 1 < phase.body or after is None else (after, 0, 0)
                        split(*following)
                        q = u // 2
                        if u % 2:
                            product(i, q)
                            taps(i * 2 + q, q, range(half))
                        else:
                            if not first or q == 1:
                                taps(i * 2 + (q - 1), 1 - q, range(half, len(mine)))
                                fold(i * 2 + (q - 1), 1 - q)
                            if not first:
                                combine(i * 2 + (q - 2), q)

                turns = phase.units // phase.body
                dve.sem_inc(C["acc_ready"], 1)
                dve.sem_inc(C["taps_summed"], 2)
                step(nc.vector.memset(conv_u, 0.0))
                turn(0, True)
                with dve.Fori(1, turns - 1) as i:
                    turn(i, False)
                turn(turns - 1, False, phase.after)
                taps(DC - 1, 1, range(half, len(mine)))
                fold(DC - 1, 1)
                combine(DC - 2, 0)
                combine(DC - 1, 1)
                dve.wait_ge(C["mean_ready"], 1)
                nc.vector.tensor_tensor(conv_acc, conv_acc, spread(PS[:, 6, 0:S1], DC), ALU.subtract).then_inc(C["centered"], 1)
                softplus()
                dve.wait_ge(C["rstd_ready"], 1)
                nc.vector.tensor_tensor(conv_sq, conv_acc, spread(rstd[:, 0:S1], DC), ALU.mult).then_inc(C["scaled"], 1)
                for c in range(DC):
                    dve.wait_ge(C["mixed"], c + 1)
                    step(nc.vector.tensor_copy(conv_hi[:, c, :], conv_mix[:, c, :]))
                    nc.vector.tensor_tensor(conv_lo[:, c, :], conv_mix[:, c, :], conv_hi[:, c, :].bitcast(F32), ALU.subtract)\
                        .then_inc(C["split"], 1)

            def attention():
                A = att_sem
                phase = ph["att_in"]
                NU = phase.body
                mask = const("att_mask").rearrange("p (n k) -> p n k", k=S1)
                mask_of = ((0, 1, 2), (3, 1, 2))
                cos, sin = rope_cos[:, 0:S1], rope_sin[:, 0:S1]

                def rope(i, g):
                    dve.wait_ge(A["rotated"], i * 3 + (g + 1))
                    nc.vector.tensor_tensor(att_t[:, 2 * g, :], PS[:, 2 + g, 0:S1], sin, ALU.mult)
                    nc.vector.tensor_tensor(att_t[:, 2 * g + 1, :], PS[:, 2 + g, S1:512], sin, ALU.mult)
                    nc.vector.tensor_tensor(att_q[:, g, :], proj1[:, 2 * g, :], cos, ALU.mult)
                    nc.vector.tensor_tensor(att_k[:, g, :], proj1[:, 2 * g + 1, :], cos, ALU.mult).then_inc(att_rot, 1)
                    dve.wait_ge(att_rot, i * 3 + (g + 1))
                    nc.vector.tensor_tensor(att_q[:, g, :], att_q[:, g, :], att_t[:, 2 * g, :], ALU.add)
                    nc.vector.tensor_tensor(att_k[:, g, :], att_k[:, g, :], att_t[:, 2 * g + 1, :], ALU.add).then_inc(A["roped"], 1)

                def copy_v(i):
                    dve.wait_ge(A["v_turned"], i)
                    nc.vector.tensor_copy(att_vn[:, 0:4, :].rearrange("p a b -> p (a b)"), PS[:, 6, :])
                    nc.vector.tensor_copy(att_vn[:, 4:6, :].rearrange("p a b -> p (a b)"), PS[:, 7, 0:S1]).then_inc(A["v_ready"], 1)

                def maxima(i, u):
                    it, m = u % 2, att_max[:, u % 2, :]
                    dve.wait_ge(A["scores_ready"], i * 4 + (u - 3))
                    dve.sem_inc(wait_taken, 1)
                    for g in range(3):
                        last = nc.vector.tensor_tensor_reduce(
                            att_s[:, u % 2, g * S1:(g + 1) * S1], PS[:, 2 + 2 * (u % 2) + g // 2, (g % 2) * S1:(g % 2 + 1) * S1],
                            mask[:, mask_of[it][g], :], 1.0, -3e38, ALU.add, ALU.max, m[:, g:g + 1])
                    last.then_inc(att_m1, 1)
                    dve.wait_ge(att_m1, i * 4 + (u - 3))
                    nc.vector.tensor_reduce(m[:, 3:4], m[:, 0:3], AX, ALU.max).then_inc(att_m2, 1)
                    dve.wait_ge(att_m2, i * 4 + (u - 3))
                    nc.vector.tensor_scalar(m[:, 4:5], m[:, 3:4], -0.125, None, ALU.mult).then_inc(A["max_ready"], 1)

                def copy_p(i, u):
                    if u >= 2:
                        dve.wait_ge(A["o_scaled"], i * 4 + (u - 5))
                    dve.wait_ge(A["p_ready"], i * 4 + (u - 3))
                    nc.vector.reciprocal(att_rden[:, u % 2:u % 2 + 1], att_den[:, u % 2:u % 2 + 1]).then_inc(A["den_ready"], 1)
                    dve.wait_ge(A["p_turned"], i * 4 + (u - 3))
                    nc.vector.tensor_copy(att_pt[:, u % 2, 0:512], PS[:, 6, :]).then_inc(A["pt_ready"], 1)

                def take_o(i):
                    dve.wait_ge(A["o_turned"], i)
                    dve.sem_inc(wait_taken, 1)
                    nc.vector.tensor_copy(att_hi[:, i - 1, :], PS[:, 7, S1:512]).then_inc(att_rounded, 1)
                    dve.wait_ge(att_rounded, i)
                    nc.vector.tensor_tensor(att_lo[:, i - 1, :], PS[:, 7, S1:512], att_hi[:, i - 1, :].bitcast(F32),
                                            ALU.subtract).then_inc(A["mixed"], 1)

                def turn(i, project, attend, after=None):
                    for n in range(NU):
                        if project:
                            following = (phase, i, n + 1) if n + 1 < NU or after is None else (after, 0, 0)
                            split(*following)
                        if attend:
                            if 3 <= n <= 6:
                                copy_p(i, n - 3)
                            if 1 <= n <= 4:
                                maxima(i, n - 1)
                            if n == 1:
                                copy_v(i)
                            if n == 7 and not project:
                                exponents(1)
                            if n == 8:
                                take_o(i)
                        if project and 5 <= n <= 7:
                            rope(i, n - 5)

                dve.sem_inc(A["mixed"], 1)
                turn(0, True, False)
                with dve.Fori(1, DC - 1) as i:
                    turn(i, True, True)
                turn(DC - 1, True, True, phase.after)
                turn(DC, False, True)

            def split_gates():
                dve.wait_ge(meta_loaded, 32)
                step(nc.vector.tensor_copy(gates_hi[:, :, :], w_gates[:, :, :]))
                nc.vector.tensor_tensor(gates_lo[:, :, :], w_gates[:, :, :], gates_hi[:, :, :].bitcast(F32), ALU.subtract)\
                    .then_inc(gates_split, 1)

            def mlstm_rows():
                A = ab_sem
                dve.wait_ge(A["gate_sums"], 1)
                bias_i, bias_f = (param("if_bias", n)[0:A_HEADS, :] for n in range(2))
                nc.vector.tensor_scalar(r_in, PS[0:A_HEADS, 5, 0:S2], bias_i, None, ALU.add)
                step(nc.vector.tensor_scalar(r_f, PS[0:A_HEADS, 6, 0:S2], bias_f, None, ALU.add))
                stt(r_e, r_f, -1.0, r_f, ALU.mult, ALU.min).then_inc(A["log_in"], 1)
                dve.wait_ge(A["log_ready"], 1)
                step(stt(r_lf, r_f, 0.0, r_l, ALU.min, ALU.subtract))
                step(nc.vector.memset(r_sum, 1.0))
                step(nc.vector.tensor_tensor_scan(r_F, r_sum, r_lf, 0.0, ALU.mult, ALU.add))
                step(nc.vector.tensor_tensor(r_a, r_in, r_F, ALU.subtract))
                step(nc.vector.tensor_tensor_scan(r_m, r_sum, r_a, 0.0, ALU.mult, ALU.max))
                nc.vector.tensor_tensor(r_sum, r_F, r_m, ALU.add).then_inc(A["floor_in"], 1)
                dve.wait_ge(A["floor_in"], 1)
                dve.sem_inc(A["rows_ready"], 1)

            def mlstm():
                A = ab_sem
                phase = ph["ab_qkvo"]
                causal = const("causal_T").rearrange("p (s t) -> p s t", s=3)

                def columns():
                    dve.wait_ge(A["turned"], 1)
                    for st, (_, tl) in enumerate(TILES2):
                        last = nc.vector.tensor_copy(ab_col[0:tl, st, :], PS[0:tl, 7, st * 4:st * 4 + 4])
                    last.then_inc(A["cols_ready"], 1)

                def shifts(hd):
                    dve.wait_ge(A["run_ready"], hd + 1)
                    if hd:
                        dve.wait_ge(A["w_ready"], 3 * hd)
                    for st, (_, tl) in enumerate(TILES2):
                        nc.vector.tensor_tensor(ab_t[0:tl, st, :], causal[0:tl, st, :], PS[0:tl, 2, 0:S2], ALU.add)\
                            .then_inc(A["shifted"], 1)

                def weights(hd):
                    for st, (_, tl) in enumerate(TILES2):
                        dve.wait_ge(A["scores_ready"], 3 * hd + st + 1)
                        dve.wait_ge(A["w_ready"], 3 * hd + st + 1)
                        stt(ab_p[0:tl, st, :], PS[0:tl, 3 + st, 0:S2], A_DIM ** -0.5, ab_w[0:tl, st, :], ALU.mult, ALU.mult)\
                            .then_inc(A["p_ready"], 1)

                def denominator(hd):
                    den, rec = ab_den[:, 0, :], ab_den[:, 1, :]
                    dve.wait_ge(A["den_abs"], hd + 1)
                    step(nc.vector.tensor_tensor(den, den, PS[:, 2, 0:S2], ALU.max))
                    step(nc.vector.reciprocal(rec, den))

                def gated(hd):
                    for c in range(2):
                        last = nc.vector.tensor_tensor(ab_hh[:, c, :], ab_den[:, 1, :], PS[:, 3 + c, 0:S2], ALU.mult)
                    step(last)
                    nc.vector.tensor_tensor(ab_hh, ab_hh, proj2[:, 24 + 2 * hd:26 + 2 * hd, :], ALU.mult).then_inc(A["h_ready"], 1)

                def take(hd):
                    dve.wait_ge(A["rstd_ready"], hd + 1)
                    for c in range(2):
                        last = stt(ab_hh[:, c, :], ab_hh[:, c, :], param("mlstm_norm", 2 * hd + c), ab_r, ALU.mult, ALU.mult)
                    step(last)
                    hi, lo = proj2_r[:, 2 * hd:2 * hd + 2, :], proj2_r[:, 8 + 2 * hd:10 + 2 * hd, :]
                    step(nc.vector.tensor_copy(hi, ab_hh))
                    nc.vector.tensor_tensor(lo, ab_hh, hi.bitcast(F32), ALU.subtract).then_inc(A["mixed"], 1)
                    dve.wait_ge(A["mixed"], hd + 1)

                for i in range(A_HEADS + 1):
                    for n in range(phase.body):
                        if i < A_HEADS:
                            if n + 1 < phase.body or i + 1 < A_HEADS:
                                split(phase, i, n + 1)
                            else:
                                split(phase.after, 0, 0)
                        if i >= 2 and n == 0:
                            take(i - 2)
                        if i == 0 and n == 6:
                            columns()
                        if i:
                            if n == 1:
                                shifts(i - 1)
                            if n == 2:
                                weights(i - 1)
                            if n == 4:
                                denominator(i - 1)
                            if n == 5:
                                gated(i - 1)
                        if i < A_HEADS:
                            lru_unit(2 * i + n // 4, n % 4)
                        elif n in (1, 2, 5):
                            (lru_scan if n == 1 else lru_out if n == 2 else lru_split)()
                take(A_HEADS - 1)

            def softplus():
                L = lru_sem
                lam = param("lru_lambda", 0, DC)
                neg, e, z, z2 = (lam_t[:, n, :] for n in range(4))
                dve.wait_ge(L["softplus_ready"], 1)
                step(nc.vector.tensor_scalar(z, e, 2.0, None, ALU.add))
                step(nc.vector.reciprocal(z, z))
                step(nc.vector.tensor_tensor(z, z, e, ALU.mult))
                step(nc.vector.tensor_tensor(z2, z, z, ALU.mult))
                step(nc.vector.memset(e, 1.0 / 21))
                for n in range(19, 0, -2):
                    step(nc.vector.tensor_tensor(e, e, z2, ALU.mult))
                    step(nc.vector.tensor_scalar(e, e, 1.0 / n, None, ALU.add))
                step(nc.vector.tensor_tensor(e, e, z, ALU.mult))
                step(nc.vector.tensor_scalar(neg, lam, -1.0, 0.0, ALU.mult, ALU.max))
                step(stt(e, e, 2.0, neg, ALU.mult, ALU.add))
                step(nc.vector.tensor_scalar(lam8, e, -LRU_C, None, ALU.mult))

            def lru_conv(phase):
                L = lru_sem

                def unit(i, u):
                    c = i * phase.body + u
                    xc, xb = lru_xc[:, c, :], lru_xb[:, c, :]
                    for n, t in enumerate(range(LRU_TAPS - 1, -1, -1)):
                        w = param("lru_conv_w", 0, DC * LRU_TAPS)[:, bass.ds(c * LRU_TAPS + t, 1)]
                        if n == 0:
                            dve.wait_ge(out_evacuated, evacuated(ph["ab_xb"]))
                            nc.vector.tensor_scalar(xc, xb, w, param("lru_conv_b", 0, DC)[:, bass.ds(c, 1)], ALU.mult, ALU.add)\
                                .then_inc(L["tapped"], 1)
                        else:
                            dve.wait_ge(L["tapped"], i * (phase.body * (LRU_TAPS - 1)) + (u * (LRU_TAPS - 1) + n))
                            stt(lru_xc[:, c, n:S2], lru_xb[:, c, 0:S2 - n], w, lru_xc[:, c, n:S2], ALU.mult, ALU.add)\
                                .then_inc(L["tapped"] if n < LRU_TAPS - 1 else L["conv_ready"], 1)
                stream(phase, unit)

            def lru_unit(i, u):
                L = lru_sem
                g, r = lru_gate[:, i, :], lru_r[:, i, :]
                if u == 0:
                    dve.wait_ge(L["gates_ready"], 2 * DC)
                    nc.vector.tensor_scalar(r, r, lam8[:, bass.ds(i, 1)], None, ALU.mult).then_inc(L["loga_ready"], 1)
                    nc.vector.tensor_tensor(lru_i[:, i, :], lru_i[:, i, :], lru_xc[:, i, :], ALU.mult).then_inc(L["steps"], 1)
                if u == 1:
                    nc.vector.tensor_tensor(sq[:, 0, :], g, g, ALU.mult).then_inc(L["steps"], 1)
                    dve.wait_ge(L["steps"], i * 5 + 2)
                    nc.vector.tensor_scalar(sq[:, 0, :], sq[:, 0, :], 0.044715, 1.0, ALU.mult, ALU.add).then_inc(L["steps"], 1)
                    dve.wait_ge(L["steps"], i * 5 + 3)
                    nc.vector.tensor_tensor(sq[:, 0, :], sq[:, 0, :], g, ALU.mult).then_inc(L["gelu_in"], 1)
                if u == 2:
                    dve.wait_ge(L["a_ready"], i + 1)
                    nc.vector.tensor_scalar(y[:, i, :], r, 1.0, None, ALU.add).then_inc(L["steps"], 1)
                    dve.wait_ge(L["steps"], i * 5 + 4)
                    dve.sem_inc(wait_taken, 1)
                    nc.vector.reciprocal(y[:, i, :], y[:, i, :]).then_inc(L["steps"], 1)
                if u == 3:
                    dve.wait_ge(L["steps"], i * 5 + 5)
                    nc.vector.tensor_tensor(r, r, y[:, i, :], ALU.mult).then_inc(L["root_in"], 1)
                    dve.wait_ge(L["gelu_ready"], i + 1)
                    stt(g, sq[:, 1, :], 1.0, g, ALU.add, ALU.mult).then_inc(L["gelu_done"], 1)

            def lru_scan():
                L = lru_sem
                dve.wait_ge(L["root_ready"], 1)
                step(nc.vector.tensor_tensor(lru_i[:, :, :], lru_i[:, :, :], lru_r[:, :, :], ALU.mult))
                for c in range(DC):
                    last = nc.vector.tensor_tensor_scan(y[:, c, :], lru_a[:, c, :], lru_i[:, c, :], 0.0, ALU.mult, ALU.add)
                step(last)

            def lru_out():
                dve.wait_ge(lru_sem["gelu_done"], DC)
                for c in range(DC):
                    last = stt(lru_a[:, c, :], y[:, c, :], 0.5, lru_gate[:, c, :], ALU.mult, ALU.mult)
                step(last)

            def lru_split():
                hi, lo = proj2_r[:, 32:40, :], proj2_r[:, 40:48, :]
                step(nc.vector.tensor_copy(hi, lru_a))
                nc.vector.tensor_tensor(lo, lru_a, hi.bitcast(F32), ALU.subtract).then_inc(lru_sem["done"], 1)

            def lambdas():
                A = c_sem
                for n in range(2):
                    last = nc.vector.tensor_tensor_reduce(lam_s[:, 8 + C_QK * n:8 + C_QK * (n + 1)], param("c_lambda", 2 * n * C_QK, C_QK),
                                                          param("c_lambda", (2 * n + 1) * C_QK, C_QK), 1.0, 0.0, ALU.mult, ALU.add,
                                                          lam_s[:, n:n + 1])
                last.then_inc(A["lam_in"], 1)
                nc.vector.tensor_scalar(subln, param("subln"), 1.0 - LAMBDA_INIT, None, ALU.mult)
                dve.wait_ge(A["lam_exp"], 1)
                step(nc.vector.tensor_tensor(lam_s[:, 4:5], lam_s[:, 3:4], lam_s[:, 2:3], ALU.subtract))
                step(nc.vector.tensor_scalar(neg_lam, lam_s[:, 4:5], -LAMBDA_INIT, None, ALU.add))

            def diff_attention():
                A = c_sem
                phase = ph["c_in"]
                NU = phase.body
                causal = const("causal").rearrange("p (s t) -> p s t", s=3)

                def rope(i):
                    dve.wait_ge(A["rotated"], i)
                    nc.vector.tensor_tensor(c_t[:, 0, :], PS[:, 2, 0:S2], rope_sin, ALU.mult)
                    nc.vector.tensor_tensor(c_t[:, 1, :], PS[:, 3, 0:S2], rope_sin, ALU.mult)
                    nc.vector.tensor_tensor(c_q, proj2[:, i - 1, :], rope_cos, ALU.mult)
                    nc.vector.tensor_tensor(c_k, proj2[:, i + 7, :], rope_cos, ALU.mult).then_inc(c_rot, 1)
                    dve.wait_ge(c_rot, i)
                    nc.vector.tensor_tensor(c_q, c_q, c_t[:, 0, :], ALU.add)
                    nc.vector.tensor_tensor(c_k, c_k, c_t[:, 1, :], ALU.add).then_inc(A["roped"], 1)

                def maxima(i, u):
                    t0, tl = TILES2[u]
                    m = c_max[0:tl, u, :]
                    dve.wait_ge(A["scores_ready"], i * 3 + (max(u, 1) - 2))
                    dve.sem_inc(wait_taken, 1)
                    for e in range(2):
                        s = (PS[:, 2 + e, 0:P], PS[:, 2 + e, P:P + S1], PS[0:META, 4 + e, 0:S2])[u]
                        last = nc.vector.tensor_tensor_reduce(c_s[0:tl, 2 * u + e, 0:t0 + tl], s, causal[0:tl, u, 0:t0 + tl],
                                                              1.0, -3e38, ALU.add, ALU.max, m[:, e:e + 1])
                    last.then_inc(c_m1, 1)
                    dve.wait_ge(c_m1, i * 3 + (u - 2))
                    nc.vector.tensor_scalar(m[:, 2:4], m[:, 0:2], -0.125, None, ALU.mult).then_inc(A["max_ready"], 1)

                def weights(i, u):
                    t0, tl = TILES2[u]
                    n = t0 + tl
                    den = c_den[0:tl, u, :]
                    p0, p1 = c_p[0:tl, 2 * u, 0:n], c_p[0:tl, 2 * u + 1, 0:n]
                    dve.wait_ge(A["p_ready"], i * 3 + (u - 5))
                    nc.vector.reciprocal(den, den).then_inc(c_d1, 1)
                    dve.wait_ge(c_d1, i * 3 + (u - 5))
                    nc.vector.tensor_scalar(p1, p1, den[:, 1:2], neg_lam[0:tl, :], ALU.mult, ALU.mult).then_inc(c_d2, 1)
                    dve.wait_ge(c_d2, i * 3 + (u - 5))
                    stt(c_pd[0:tl, u, 0:n], p0, den[:, 0:1], p1, ALU.mult, ALU.add).then_inc(A["pd_ready"], 1)

                def take_o(i):
                    dve.wait_ge(A["rstd_ready"], i - 2)
                    stt(c_o, PS[:, 7, 0:S2], subln, c_r, ALU.mult, ALU.mult).then_inc(c_scaled, 1)
                    dve.wait_ge(c_scaled, i - 2)
                    dve.sem_inc(wait_taken, 1)
                    nc.vector.tensor_copy(c_hi[:, i - 3, :], c_o).then_inc(c_rounded, 1)
                    dve.wait_ge(c_rounded, i - 2)
                    nc.vector.tensor_tensor(c_lo[:, i - 3, :], c_o, c_hi[:, i - 3, :].bitcast(F32), ALU.subtract).then_inc(A["mixed"], 1)

                def turn(i, project, score, weigh, norm, after=None):
                    for n in range(NU):
                        if project:
                            following = (phase, i, n + 1) if n + 1 < NU or after is None else (after, 0, 0)
                            split(*following)
                        if n == 0 and weigh:
                            weights(i, 0)
                            maxima(i - 1, 2)
                            weights(i, 1)
                        if n == 1:
                            if score:
                                rope(i)
                            if weigh:
                                weights(i, 2)
                        if n == 2:
                            if weigh:
                                dve.wait_ge(A["v_turned"], i - 1)
                                nc.vector.tensor_copy(c_vn[:, 0:2, :].rearrange("p a b -> p (a b)"), PS[:, 4, 0:2 * P])
                                nc.vector.tensor_copy(c_vn[0:META, 2, :], PS[0:META, 4, 2 * P:3 * P]).then_inc(A["v_ready"], 1)
                            if norm:
                                take_o(i)
                            if score:
                                maxima(i, 0)
                                maxima(i, 1)

                LAST = C_HEADS
                turn(0, True, False, False, False)
                turn(1, True, True, False, False)
                turn(2, True, True, True, False)
                with dve.Fori(3, LAST - 1) as i:
                    turn(i, True, True, True, True)
                turn(LAST - 1, True, True, True, True, phase.after)
                turn(LAST, False, True, True, True)
                turn(LAST + 1, False, False, True, True)
                turn(LAST + 2, False, False, False, True)

            def final_norm():
                dve.wait_ge(rstd_ready, 21)
                for c in range(DC):
                    stt(y[:, c, :], h[:, c, :], param("norm_final", c), rstd[:, :], ALU.mult, ALU.mult).then_inc(final_ready, 1)

            dve.sem_inc(pair_done, FREE_PAIRS)
            dve.sem_inc(y_added, FREE_SQUARES)
            dve.sem_inc(part_ready, 2)
            dve.wait_ge(consts_loaded, 32)
            dve.wait_ge(x_loaded, 16)
            lam = param("lru_lambda", 0, DC)
            stt(lam_t[:, 0, :], lam, -1.0, lam, ALU.mult, ALU.min).then_inc(lru_sem["lam_ready"], 1)
            for layer in range(DEPTH):
                j = layer // 3
                if layer == 0:
                    exponents(0)
                    split(phases[0], 0, 0)
                pre_norm(4 * layer, 2 * layer, x, S1, "norm_w", (4 * layer) * DC)
                if layer % 3 == 0:
                    rotate(j, ph[f"ret_qk{layer}"])
                    stream(ph[f"ret_v{layer}"])
                    values(j)
                    stream(ph[f"ret_g{layer}"])
                    retention(j, layer)
                    sum_squares(4 * layer + 1, ph[f"ret_out{layer}"], S1)
                elif layer % 3 == 1:
                    conv()
                    sum_squares(4 * layer + 1, ph["conv_out"], S1)
                else:
                    attention()
                    sum_squares(4 * layer + 1, ph["att_out"], S1)
                post_norm(4 * layer + 1, (4 * layer + 1) * DC)
                pre_norm(4 * layer + 2, 2 * layer + 1, x, S1, "norm_w", (4 * layer + 2) * DC)
                ffn_pairs(ph[f"ffn_in{layer}"])
                sum_squares(4 * layer + 3, ph[f"ffn_out{layer}"], S1)
                post_norm(4 * layer + 3, (4 * layer + 3) * DC)
            split_gates()
            pre_norm(16, 2 * DEPTH, h, S2, "norm_mix", 0)
            stream(ph["ab_xb"])
            lru_conv(ph["ab_gate"])
            mlstm_rows()
            mlstm()
            add_to_h(17, ph["ab_out"])
            pre_norm(17, 2 * DEPTH + 1, h, S2, "norm_mlp", 0)
            square_relu(ph["mlp_in0"])
            add_to_h(18, ph["mlp_out0"])
            pre_norm(18, 2 * DEPTH + 2, h, S2, "norm_mix", DC)
            lambdas()
            diff_attention()
            add_to_h(19, ph["c_out"])
            pre_norm(19, 2 * DEPTH + 3, h, S2, "norm_mlp", DC)
            square_relu(ph["mlp_in1"])
            add_to_h(20, ph["mlp_out1"])
            final_norm()



def kernel(**inputs):
    import concourse.bacc as bacc
    from concourse.bass_utils import run_bass_kernel_spmd as run

    a = {k: np.asarray(v) for k, v in inputs.items()}

    def features(v):
        return v.reshape(-1, P).T

    def units(w, halves=1):
        k, m = w.shape
        t = k // P // halves
        return np.ascontiguousarray(w.reshape(halves, t, P, m // P, P).transpose(3, 0, 2, 1, 4).reshape(m // P * halves, P, t * P))

    def interleaved(w):
        u = units(w)
        n = u.shape[0] // 2
        return np.ascontiguousarray(np.stack([u[:n], u[n:]], 1).reshape(u.shape))

    (const_a, at_a), (const_b, at_b), (const_c, at_c) = constants()
    arrays = {"const_a": const_a, "const_b": const_b, "const_c": const_c}
    arrays["x"] = np.ascontiguousarray(a["x"][0].T.reshape(DC, P, S1).transpose(1, 0, 2))
    arrays["meta"] = np.ascontiguousarray(a["meta_tokens_2"].T.reshape(DC, P, META).transpose(1, 0, 2))
    for layer in range(DEPTH):
        j = layer // 3
        if layer % 3 == 0:
            u = units(a["ret_w_in"][j])
            arrays[f"ret_qk{layer}"] = np.ascontiguousarray(u[:16])
            arrays[f"ret_v{layer}"] = np.ascontiguousarray(u[16:32])
            arrays[f"ret_g{layer}"] = np.ascontiguousarray(u[32:])
            arrays[f"ret_out{layer}"] = units(a["ret_w_out"][j], 2)
        elif layer % 3 == 1:
            w = a["conv_w_in"][0]
            arrays["conv_in"] = interleaved(np.concatenate([w[:, D:], w[:, :D]], 1))
            arrays["conv_out"] = units(a["conv_w_out"][0])
        else:
            u = units(a["attn_w_in"][0]).reshape(3, 3, DC, P, D)
            order = [(g, w) for g in range(3) for w in range(2)] + [(g, 2) for g in range(3)]
            arrays["att_in"] = np.ascontiguousarray(np.stack([u[g, w] for g, w in order], 1).reshape(-1, P, D))
            arrays["att_out"] = units(a["attn_w_out"][0])
        arrays[f"ffn_in{layer}"] = interleaved(a["ffn_w_in"][layer])
        arrays[f"ffn_out{layer}"] = units(a["ffn_w_out"][layer], 2)
    w = a["ab_w_in_2"][0]
    g0 = 4 * D
    u = units(np.concatenate([w[:, :g0], w[:, g0 + 2 * A_HEADS:]], 1))
    arrays["ab_xb"], arrays["ab_gate"] = np.ascontiguousarray(u[32:40]), np.ascontiguousarray(u[40:])
    u = u[:32].reshape(4, A_HEADS, 2, P, D)
    arrays["ab_qkvo"] = np.ascontiguousarray(u.transpose(1, 0, 2, 3, 4).reshape(-1, P, D))
    arrays["ab_gates"] = np.ascontiguousarray(w[:, g0:g0 + 2 * A_HEADS].reshape(DC, P, 2 * A_HEADS).transpose(1, 0, 2))
    arrays["ab_out"] = units(a["ab_w_out_2"][0], 2)
    u = units(a["c_w_in_2"][0]).reshape(3, C_HEADS, P, D)
    arrays["c_in"] = np.ascontiguousarray(u.transpose(1, 0, 2, 3).reshape(-1, P, D))
    arrays["c_out"] = units(a["c_w_out_2"][0])
    for layer in range(2):
        arrays[f"mlp_in{layer}"] = units(a["mlp_w1_2"][layer])
        arrays[f"mlp_out{layer}"] = units(a["mlp_w2_2"][layer], 4)
    arrays["lru_w_r"] = np.ascontiguousarray(a["lru_w_r_2"][0].transpose(1, 0, 2))
    arrays["lru_w_i"] = np.ascontiguousarray(a["lru_w_i_2"][0].transpose(1, 0, 2))

    taps = lambda w, n: w.reshape(n, DC, P).transpose(2, 1, 0).reshape(P, DC * n)
    if_bias = np.zeros((P, 2), np.float32)
    if_bias[:A_HEADS] = a["ab_if_bias_2"][0].reshape(2, A_HEADS).T
    cols = {
        "norm_w": features(a["norm_w"].reshape(-1)), "conv_b_in": features(a["conv_b_in"][0]),
        "conv_w_dw": taps(a["conv_w_dw"][0], CONV_TAPS), "conv_b_dw": features(a["conv_b_dw"][0]),
        "conv_ln_g": features(a["conv_ln_g"][0]), "conv_ln_b": features(a["conv_ln_b"][0]),
        "conv_b_out": features(a["conv_b_out"][0]), "norm_mix": features(a["norm_mix_2"].reshape(-1)),
        "norm_mlp": features(a["norm_mlp_2"].reshape(-1)), "norm_final": features(a["norm_final_2"]),
        "mlstm_norm": features(a["mlstm_norm_2"][0]), "lru_conv_w": taps(a["lru_conv_w_2"][0], LRU_TAPS),
        "lru_conv_b": features(a["lru_conv_b_2"][0]), "lru_b_r": features(a["lru_b_r_2"][0]),
        "lru_b_i": features(a["lru_b_i_2"][0]), "lru_lambda": features(a["lru_lambda_2"][0]),
        "subln": features(a["c_subln_2"][0]),
        "decay": np.broadcast_to(a["ret_log1m_decay"].reshape(1, -1), (P, 16)), "if_bias": if_bias,
        "c_lambda": np.broadcast_to(a["c_lambda_2"][0].reshape(1, -1), (P, 4 * C_QK)),
    }
    assert all(cols[name].shape[1] == n for name, n in PARAMS)
    arrays["params"] = np.ascontiguousarray(np.concatenate([cols[name] for name, _ in PARAMS], 1))

    nc = bacc.Bacc("TRN2", target_bir_lowering=False, num_devices=1)
    dram = {k: nc.dram_tensor("in_" + k, v.shape, F32, kind="ExternalInput").ap() for k, v in arrays.items()}
    out = nc.dram_tensor("out", [P, DC, S1], F32, kind="ExternalOutput").ap()
    build(nc, dram, out, (at_a, at_b, at_c))
    got = run(nc, [{"in_" + k: v for k, v in arrays.items()}], core_ids=[0]).results[0]["out"]
    return np.ascontiguousarray(np.asarray(got).transpose(2, 1, 0).reshape(1, S1, D))
```
